# Optimizing a Trainium2 kernel written in Bass

```python
import math, functools
import jax, jax.numpy as jnp
from jax import lax
import numpy as np

D_MODEL = 1024
BATCH = 1
SEQ = 1024
DEPTH = 2

GRID_W = 64
CTX_LEN = 256
Q_BLOCK = 128
ROPE_THETA = 10000.0
EPS = 1e-6
N_EVEN = (DEPTH + 1) // 2
N_ODD = DEPTH // 2

A_HEADS = 8
A_Q_LORA = 256
A_KV_LORA = 128
A_NOPE = 64
A_ROPE = 32
A_QK = A_NOPE + A_ROPE
A_V = 64
A_WIDTH = A_HEADS * A_V

B_HEADS = 4
B_D = 64
B_V = 2 * B_D
B_WIDTH = B_HEADS * B_V

E_SIZES = (A_Q_LORA, A_KV_LORA, A_ROPE, A_WIDTH,
           2 * B_HEADS * B_D, 2 * B_HEADS * B_D, B_WIDTH, B_WIDTH)
E_IN = sum(E_SIZES)
E_MIX = A_WIDTH + B_WIDTH

C_HEADS = 8
C_KV_HEADS = 2
C_HD = 128
C_WIDTH = C_HEADS * C_HD
O_SIZES = (C_WIDTH, C_KV_HEADS * C_HD, C_KV_HEADS * C_HD, C_WIDTH)
O_IN = sum(O_SIZES)

kernel_name = 'hybrid_mla_diff_gqa_prefix_trunk'

def rmsnorm(x, g):
    xf = x.astype(jnp.float32)
    y = xf * lax.rsqrt(jnp.mean(xf * xf, axis=-1, keepdims=True) + EPS)
    return (y * g.astype(jnp.float32)).astype(x.dtype)

def split_cols(p, sizes):
    return jnp.split(p, np.cumsum(sizes)[:-1].tolist(), axis=-1)

def prefix_angles(rows, cols, dim):
    n_freq = dim // 4
    inv = ROPE_THETA ** (-jnp.arange(n_freq, dtype=jnp.float32) / n_freq)
    ang = jnp.concatenate([rows[:, None] * inv, cols[:, None] * inv], axis=-1)
    return jnp.concatenate([jnp.zeros((CTX_LEN, dim // 2), jnp.float32), ang], axis=0)

def apply_rope(x, ang):
    half = x.shape[-1] // 2
    cos = jnp.cos(ang)[None, :, None, :]
    sin = jnp.sin(ang)[None, :, None, :]
    xf = x.astype(jnp.float32)
    x1, x2 = xf[..., :half], xf[..., half:]
    return jnp.concatenate([x1 * cos - x2 * sin, x2 * cos + x1 * sin], axis=-1).astype(x.dtype)

def gqa_attend(q, k, v):
    B, T, H, d = q.shape
    Hk = k.shape[2]
    qg = q.reshape(B, T, Hk, H // Hk, d)
    s = jnp.einsum('btkgd,bskd->bkgts', qg, k, preferred_element_type=jnp.float32) * (d ** -0.5)
    p = jax.nn.softmax(s, axis=-1).astype(v.dtype)
    o = jnp.einsum('bkgts,bskd->btkgd', p, v)
    return o.reshape(B, T, H, v.shape[-1])

def diff_attend(q1, q2, k1, k2, v, lam):
    scale = q1.shape[-1] ** -0.5
    p1 = jax.nn.softmax(jnp.einsum('bthd,bshd->bhts', q1, k1, preferred_element_type=jnp.float32) * scale, axis=-1)
    p2 = jax.nn.softmax(jnp.einsum('bthd,bshd->bhts', q2, k2, preferred_element_type=jnp.float32) * scale, axis=-1)
    w = (p1 - lam * p2).astype(v.dtype)
    return jnp.einsum('bhts,bshd->bthd', w, v)

def sweep_queries(attend, q_list, kv_list):
    B, N = q_list[0].shape[:2]
    nb = N // Q_BLOCK
    qb = tuple(jnp.moveaxis(q.reshape(B, nb, Q_BLOCK, *q.shape[2:]), 1, 0) for q in q_list)
    out = lax.map(lambda qs: attend(*qs, *kv_list), qb)
    return jnp.moveaxis(out, 0, 1).reshape(B, N, *out.shape[3:])

def prefix_attend(attend, q_list, kv_list, update_ctx):
    lat = sweep_queries(attend, tuple(q[:, CTX_LEN:] for q in q_list), kv_list)
    if not update_ctx:
        return lat
    ctx_o = attend(*(q[:, :CTX_LEN] for q in q_list), *(kv[:, :CTX_LEN] for kv in kv_list))
    return jnp.concatenate([ctx_o, lat], axis=1)

def modulated_input(x_ctx, x_lat, c, c_ctx, norm_g, w_mod, b_mod):
    m_l = jax.nn.silu(c) @ w_mod + b_mod
    m_c = jax.nn.silu(c_ctx) @ w_mod + b_mod
    sh_l, sc_l, g_l = jnp.split(m_l[:, None, :], 3, axis=-1)
    sh_c, sc_c, g_c = jnp.split(m_c, 3, axis=-1)
    h = jnp.concatenate([rmsnorm(x_ctx, norm_g) * (1 + sc_c) + sh_c,
                         rmsnorm(x_lat, norm_g) * (1 + sc_l) + sh_l], axis=1)
    return h, g_c, g_l

def residual_update(x_ctx, x_lat, out, g_c, g_l, update_ctx):
    N = x_lat.shape[1]
    x_lat = x_lat + g_l * out[:, out.shape[1] - N:]
    if update_ctx:
        x_ctx = x_ctx + g_c * out[:, :CTX_LEN]
    return x_ctx, x_lat

def mla_diff_layer(x_ctx, x_lat, c, c_ctx, rows, cols, lam_init, update_ctx,
                   norm_g, w_mod, b_mod, w_in, a_g_cq, a_w_uq, a_g_ckv, a_w_ukv, a_g_qn, a_g_kn,
                   b_g_qn, b_g_kn, b_lam_q1, b_lam_k1, b_lam_q2, b_lam_k2, b_g_out, w_out):
    h, g_c, g_l = modulated_input(x_ctx, x_lat, c, c_ctx, norm_g, w_mod, b_mod)
    B, L, _ = h.shape
    a_cq, a_ckv, a_kr, a_gate, b_q, b_k, b_v, b_gate = split_cols(h @ w_in, E_SIZES)

    ang_a = prefix_angles(rows, cols, A_ROPE)
    q = (rmsnorm(a_cq, a_g_cq) @ a_w_uq).reshape(B, L, A_HEADS, A_QK)
    kv = (rmsnorm(a_ckv, a_g_ckv) @ a_w_ukv).reshape(B, L, A_HEADS, A_NOPE + A_V)
    k = jnp.concatenate([kv[..., :A_NOPE],
                         jnp.broadcast_to(a_kr[:, :, None, :], (B, L, A_HEADS, A_ROPE))], axis=-1)
    q, k = rmsnorm(q, a_g_qn), rmsnorm(k, a_g_kn)
    q = jnp.concatenate([q[..., :A_NOPE], apply_rope(q[..., A_NOPE:], ang_a)], axis=-1)
    k = jnp.concatenate([k[..., :A_NOPE], apply_rope(k[..., A_NOPE:], ang_a)], axis=-1)
    o_a = prefix_attend(gqa_attend, (q,), (k, kv[..., A_NOPE:]), update_ctx)
    T = o_a.shape[1]
    y_a = o_a.reshape(B, T, A_WIDTH) * jax.nn.silu(a_gate[:, L - T:])

    ang_b = prefix_angles(rows, cols, B_D)
    bq = apply_rope(rmsnorm(b_q.reshape(B, L, 2 * B_HEADS, B_D), b_g_qn), ang_b)
    bk = apply_rope(rmsnorm(b_k.reshape(B, L, 2 * B_HEADS, B_D), b_g_kn), ang_b)
    lq1, lk1 = b_lam_q1.astype(jnp.float32), b_lam_k1.astype(jnp.float32)
    lq2, lk2 = b_lam_q2.astype(jnp.float32), b_lam_k2.astype(jnp.float32)
    lam = jnp.exp(jnp.sum(lq1 * lk1)) - jnp.exp(jnp.sum(lq2 * lk2)) + lam_init
    o_b = prefix_attend(functools.partial(diff_attend, lam=lam),
                        (bq[:, :, 0::2], bq[:, :, 1::2]),
                        (bk[:, :, 0::2], bk[:, :, 1::2], b_v.reshape(B, L, B_HEADS, B_V)), update_ctx)
    o_b = rmsnorm(o_b, b_g_out) * (1.0 - lam_init)
    y_b = o_b.reshape(B, T, B_WIDTH) * jax.nn.silu(b_gate[:, L - T:])

    out = jnp.concatenate([y_a, y_b], axis=-1) @ w_out
    return residual_update(x_ctx, x_lat, out, g_c, g_l, update_ctx)

def gqa_layer(x_ctx, x_lat, c, c_ctx, rows, cols, update_ctx,
              norm_g, w_mod, b_mod, w_in, g_qn, g_kn, w_out):
    h, g_c, g_l = modulated_input(x_ctx, x_lat, c, c_ctx, norm_g, w_mod, b_mod)
    B, L, _ = h.shape
    q, k, v, gate = split_cols(h @ w_in, O_SIZES)
    ang = prefix_angles(rows, cols, C_HD)
    q = apply_rope(rmsnorm(q.reshape(B, L, C_HEADS, C_HD), g_qn), ang)
    k = apply_rope(rmsnorm(k.reshape(B, L, C_KV_HEADS, C_HD), g_kn), ang)
    v = v.reshape(B, L, C_KV_HEADS, C_HD)
    o = prefix_attend(gqa_attend, (q,), (k, v), update_ctx)
    T = o.shape[1]
    out = (o.reshape(B, T, C_WIDTH) * jax.nn.silu(gate[:, L - T:])) @ w_out
    return residual_update(x_ctx, x_lat, out, g_c, g_l, update_ctx)

def setup_inputs(seed: int = 0) -> dict:
    key = jax.random.key(seed)
    ks = iter(jax.random.split(key, 40))

    def nrm(shape, scale):
        return jax.random.normal(next(ks), shape, jnp.float32) * scale

    def gain(shape):
        return 1.0 + nrm(shape, 0.05)

    D = D_MODEL
    NE, NO = N_EVEN, N_ODD
    inputs = {}
    inputs['x'] = nrm((BATCH, SEQ, D), 1.0)
    inputs['c'] = nrm((BATCH, D), 1.0)
    inputs['ctx'] = nrm((BATCH, CTX_LEN, D), 1.0)
    inputs['c_ctx'] = nrm((D,), 1.0)
    inputs['e_norm_g'] = gain((NE, D))
    inputs['e_w_mod'] = nrm((NE, D, 3 * D), 0.5 * D ** -0.5)
    inputs['e_b_mod'] = nrm((NE, 3 * D), 0.02)
    inputs['e_w_in'] = nrm((NE, D, E_IN), D ** -0.5)
    inputs['a_g_cq'] = gain((NE, A_Q_LORA))
    inputs['a_w_uq'] = nrm((NE, A_Q_LORA, A_HEADS * A_QK), A_Q_LORA ** -0.5)
    inputs['a_g_ckv'] = gain((NE, A_KV_LORA))
    inputs['a_w_ukv'] = nrm((NE, A_KV_LORA, A_HEADS * (A_NOPE + A_V)), A_KV_LORA ** -0.5)
    inputs['a_g_qn'] = gain((NE, A_QK))
    inputs['a_g_kn'] = gain((NE, A_QK))
    inputs['b_g_qn'] = gain((NE, B_D))
    inputs['b_g_kn'] = gain((NE, B_D))
    inputs['b_lam_q1'] = nrm((NE, B_D), 0.1)
    inputs['b_lam_k1'] = nrm((NE, B_D), 0.1)
    inputs['b_lam_q2'] = nrm((NE, B_D), 0.1)
    inputs['b_lam_k2'] = nrm((NE, B_D), 0.1)
    inputs['b_g_out'] = gain((NE, B_V))
    inputs['e_w_out'] = nrm((NE, E_MIX, D), E_MIX ** -0.5)
    inputs['o_norm_g'] = gain((NO, D))
    inputs['o_w_mod'] = nrm((NO, D, 3 * D), 0.5 * D ** -0.5)
    inputs['o_b_mod'] = nrm((NO, 3 * D), 0.02)
    inputs['o_w_in'] = nrm((NO, D, O_IN), D ** -0.5)
    inputs['c_g_qn'] = gain((NO, C_HD))
    inputs['c_g_kn'] = gain((NO, C_HD))
    inputs['o_w_out'] = nrm((NO, C_WIDTH, D), C_WIDTH ** -0.5)
    return inputs

def reference(x, c, ctx, c_ctx, e_norm_g, e_w_mod, e_b_mod, e_w_in, a_g_cq, a_w_uq, a_g_ckv, a_w_ukv,
              a_g_qn, a_g_kn, b_g_qn, b_g_kn, b_lam_q1, b_lam_k1, b_lam_q2, b_lam_k2, b_g_out, e_w_out,
              o_norm_g, o_w_mod, o_b_mod, o_w_in, c_g_qn, c_g_kn, o_w_out):
    n_tok = x.shape[1]
    ROWS = n_tok // GRID_W
    rows, cols = jnp.meshgrid(jnp.arange(ROWS, dtype=jnp.float32),
                              jnp.arange(GRID_W, dtype=jnp.float32), indexing='ij')
    rows, cols = rows.reshape(-1), cols.reshape(-1)
    x_ctx, x_lat = ctx, x
    for layer in range(DEPTH):
        i = layer // 2
        update_ctx = layer < DEPTH - 1
        if layer % 2 == 0:
            lam_init = 0.8 - 0.6 * math.exp(-0.3 * layer)
            x_ctx, x_lat = mla_diff_layer(
                x_ctx, x_lat, c, c_ctx, rows, cols, lam_init, update_ctx,
                e_norm_g[i], e_w_mod[i], e_b_mod[i], e_w_in[i], a_g_cq[i], a_w_uq[i], a_g_ckv[i], a_w_ukv[i],
                a_g_qn[i], a_g_kn[i], b_g_qn[i], b_g_kn[i], b_lam_q1[i], b_lam_k1[i], b_lam_q2[i], b_lam_k2[i],
                b_g_out[i], e_w_out[i])
        else:
            x_ctx, x_lat = gqa_layer(
                x_ctx, x_lat, c, c_ctx, rows, cols, update_ctx,
                o_norm_g[i], o_w_mod[i], o_b_mod[i], o_w_in[i], c_g_qn[i], c_g_kn[i], o_w_out[i])
    return x_lat


_drawn_inputs = setup_inputs


def setup_inputs(seed=0):
    import zlib

    import numpy as np

    out = dict(_drawn_inputs(seed))
    spreads = {}
    factors = {'ctx': 4.675,
     'e_norm_g': 8.0,
     'e_b_mod': 4.424,
     'a_g_cq': 8.0,
     'a_w_uq': 5.027,
     'a_g_ckv': 8.0,
     'a_g_qn': 8.0,
     'a_g_kn': 8.0,
     'b_g_qn': 8.0,
     'b_g_kn': 8.0,
     'b_lam_q1': 8.0,
     'b_lam_q2': 8.0,
     'b_lam_k2': 8.0,
     'b_g_out': 8.0,
     'o_norm_g': 8.0,
     'o_b_mod': 8.0,
     'c_g_qn': 8.0,
     'c_g_kn': 8.0}
    for name, (base, spread) in spreads.items():
        noise = np.random.default_rng([zlib.crc32(name.encode()), seed]).standard_normal(out[name].shape)
        drawn = base * np.exp(spread * noise) if base else spread * noise
        out[name] = __import__('jax').numpy.asarray(drawn.astype(out[name].dtype))
    for name, factor in factors.items():
        out[name] = (out[name] * factor).astype(out[name].dtype)
    return out
```

```python
from contextlib import ExitStack

import numpy as np

import concourse.bass as bass
from concourse import mybir

F32 = mybir.dt.float32
F32R = mybir.dt.float32r
ALU = mybir.AluOpType
ACT = mybir.ActivationFunctionType
AX = mybir.AxisListType.X

P = 128
D = 1024
KD = D // P
CTX = 256
LAT = 1024
TOK = CTX + LAT
NT = TOK // P
NCT = CTX // P
GRID_W = 64
EPS = 1e-6

A_HEADS, A_NOPE, A_ROPE, A_V = 8, 64, 32, 64
A_QK = A_NOPE + A_ROPE
A_Q_LORA, A_KV_LORA = 256, 128
B_HEADS, B_D, B_V = 4, 64, 128
C_HEADS, C_KV, C_HD = 8, 2, 128
A_WIDTH, B_WIDTH = A_HEADS * A_V, B_HEADS * B_V
LAM_INIT = 0.2

W0 = A_Q_LORA + A_KV_LORA + A_ROPE
E_GATE_A = W0
E_BQ = E_GATE_A + A_WIDTH
E_BK = E_BQ + 2 * B_HEADS * B_D
E_BV = E_BK + 2 * B_HEADS * B_D
E_GATE_B = E_BV + B_WIDTH
O_K = C_HEADS * C_HD
O_GATE = O_K + 2 * C_KV * C_HD
WR = 16
RAW = 5


def three_passes(nc, out, lhs, rhs, start, stop):
    nc.tensor.matmul(out, lhs[1], rhs[0], start=start, stop=False)
    nc.tensor.matmul(out, lhs[0], rhs[1], start=False, stop=False)
    return nc.tensor.matmul(out, lhs[0], rhs[0], start=False, stop=stop)


class Chain:

    def __init__(self, nc, eng, sem):
        self.nc, self.eng, self.sem, self.n = nc, eng, sem, 0

    def link(self, ins):
        ins.then_inc(self.sem, 1)
        self.n += 1
        self.eng.wait_ge(self.sem, self.n)



def setup(nc, A, K, sem, PS):
    with ExitStack() as ctx:
        def sb(name, shape, dt=F32):
            return ctx.enter_context(nc.sbuf_tensor(name, shape, dt))

        cc = sb("su_cc", [16, P])
        ce = sb("su_ce", [16, P])
        lam = sb("su_lam", [P, 4, B_D])
        lp = sb("su_lp", [P, 2, B_D])
        ls = sb("su_ls", [P, 2])
        kinds = {"A": (A_ROPE, A_QK), "B": (B_D, B_D), "C": (C_HD, C_HD)}
        gain, cs, tab = {}, {}, {}
        for n, (rd, full) in kinds.items():
            gain[n] = sb(f"su_g{n}", [P, 2, full])
            cs[n] = sb(f"su_cs{n}", [P, NT, 2, rd // 2])
            tab[n] = sb(f"su_t{n}", [P, NT, 2, 2, rd])

        s_in, s_cc, s_id, s_e, s_c, s_v, s_le, s_tab, s_st, s_p = (
            sem(n) for n in ("su_in", "su_ccin", "su_id", "su_exp", "su_silu", "su_chain", "su_lexp",
                             "su_tab", "su_stored", "su_cT"))
        block = ctx.enter_context(nc.Block())

        @block.sync
        def _(sp):
            sp.dma_start(cc[0:8, :], A["c_ctx"].rearrange("(k p) -> k p", p=P)).then_inc(s_cc, 16)
            sp.dma_start(cc[8:16, :], A["c"][0, :].rearrange("(k p) -> k p", p=P)).then_inc(s_cc, 16)
            for j, n in enumerate(("b_lam_q1", "b_lam_k1", "b_lam_q2", "b_lam_k2")):
                sp.dma_start(lam[:, j, :], A[n][0, :].partition_broadcast(P)).then_inc(s_in, 16)
            for n, (q, k) in {"A": ("a_g_qn", "a_g_kn"), "B": ("b_g_qn", "b_g_kn"),
                              "C": ("c_g_qn", "c_g_kn")}.items():
                sp.dma_start(gain[n][:, 0, :], A[q][0, :].partition_broadcast(P)).then_inc(s_in, 16)
                sp.dma_start(gain[n][:, 1, :], A[k][0, :].partition_broadcast(P)).then_inc(s_in, 16)
                sp.dma_start(cs[n][:], A["rope" + n].rearrange("(t p) a f -> p t a f", p=P)).then_inc(s_in, 16)
            sp.dma_start(K["gcol"][:, 0:2], A["a_g_cq"][0, :].rearrange("(k p) -> p k", p=P),
                         allow_slow_non_contiguous=True).then_inc(s_in, 16)
            sp.dma_start(K["gcol"][:, 2:3], A["a_g_ckv"][0, :].rearrange("(k p) -> p k", p=P),
                         allow_slow_non_contiguous=True).then_inc(s_in, 16)
            for i, n in enumerate("ABC"):
                sp.wait_ge(s_tab, i + 1)
                sp.dma_start(A["tab" + n].rearrange("(t p) q a f -> p t q a f", p=P), tab[n][:]).then_inc(s_st, 16)
            sp.wait_ge(s_st, 48)

        @block.gpsimd
        def _(pool):
            nc.gpsimd.memset(K["idn"][:], 0.0).then_inc(s_id, 1)
            pool.wait_ge(s_id, 1)
            nc.gpsimd.affine_select(out=K["idn"][:], in_=K["idn"][:], compare_op=ALU.not_equal, fill=1.0,
                                    base=0, pattern=[[-1, P]], channel_multiplier=1).then_inc(s_id, 1)

        @block.scalar
        def _(act):
            act.wait_ge(s_cc, 32)
            nc.scalar.activation(ce[:], cc[:], ACT.Exp, scale=-1.0).then_inc(s_e, 1)
            act.wait_ge(s_v, 5)
            nc.scalar.activation(ls[:], ls[:], ACT.Exp).then_inc(s_le, 1)

        @block.tensor
        def _(pe):
            pe.wait_ge(s_id, 2)
            pe.wait_ge(s_c, 1)
            nc.tensor.transpose(PS[:, 0, 0:16], cc[:], K["idn"][0:16, 0:16]).then_inc(s_p, 1)

        @block.vector
        def _(dve):
            ch = Chain(nc, dve, s_v)
            dve.wait_ge(s_e, 1)
            ch.link(nc.vector.tensor_scalar_add(ce[:], ce[:], 1.0))
            ch.link(nc.vector.reciprocal(ce[:], ce[:]))
            nc.vector.tensor_tensor(cc[:], cc[:], ce[:], ALU.mult).then_inc(s_c, 1)
            dve.wait_ge(s_in, 16 * 15)
            for j in range(2):
                ch.link(nc.vector.tensor_tensor(lp[:, j, :], lam[:, 2 * j, :], lam[:, 2 * j + 1, :], ALU.mult))
            ch.link(nc.vector.tensor_reduce(ls[:], lp[:], AX, ALU.add))
            dve.wait_ge(s_le, 1)
            ch.link(nc.vector.tensor_tensor(K["neglam"][:], ls[:, 1:2], ls[:, 0:1], ALU.subtract))
            nc.vector.tensor_scalar_add(K["neglam"][:], K["neglam"][:], -LAM_INIT)
            for n, (rd, full) in kinds.items():
                ch.link(nc.vector.tensor_scalar_mul(gain[n][:, 0, :], gain[n][:, 0, :], float(full) ** -0.5))
                for q in range(2):
                    for a in range(2):
                        for half in range(2):
                            o = full - rd + half * rd // 2
                            g = gain[n][:, q, o:o + rd // 2].unsqueeze(1).to_broadcast([P, NT, rd // 2])
                            last = nc.vector.tensor_tensor(tab[n][:, :, q, a, half * rd // 2:(half + 1) * rd // 2],
                                                           cs[n][:, :, a, :], g, ALU.mult)
                last.then_inc(s_tab, 1)
            nc.vector.tensor_copy(K["gnope"][:], gain["A"][:, :, 0:A_NOPE])
            dve.wait_ge(s_p, 1)
            nc.vector.tensor_copy(K["cT"][:], PS[:, 0, 0:16])



def plan_project(layer):
    jobs = []

    def mod(l, js):
        for j in js:
            jobs.append(("mod", l, j))
            if j < 4:
                jobs.append(("modT", l, j))

    def norm(t):
        jobs.extend([("hT", t, 0), ("hT", t, 1)])

    if layer == 0:
        mod(0, range(4))
    norm(0)
    norm(1)
    first = "c0" if layer == 0 else "kv"
    for t in range(NT):
        jobs.append(("row", first, t))
        if t + 2 < NT:
            norm(t + 2)
        if t:
            jobs.append(("rowT", first, t - 1))
    jobs.append(("rowT", first, NT - 1))
    if layer == 0:
        mod(0, (4, 5))
        chunks = ("bq", "bk")
        tiles = range(NT)
    else:
        chunks = ("q0", "q1")
        tiles = range(NCT, NT)
    prev = None
    for c in chunks:
        for t in tiles:
            jobs.append(("row", c, t))
            if prev:
                jobs.append(("rowT",) + prev)
            prev = (c, t)
    jobs.append(("rowT",) + prev)
    if layer == 0:
        for t in range(NT):
            jobs.append(("v", "bv", t))
    groups = [(0, 512), (512, 512), (1024, 256)] if layer == 0 else [(256, 512), (768, 512)]
    gates = [[("gate", c, j, a, n) for j in range(4) for a, n in groups] for c in ("ga", "gb")]
    if layer == 1:
        return jobs + gates[0] + gates[1]
    jobs += gates[0]
    late = gates[1]
    prev = None
    for t in range(NT):
        jobs += [("row", "uq", t, 0), ("row", "uq", t, 1)]
        if prev is not None:
            jobs += [("rowT", "uk", prev, 0), ("rowT", "uk", prev, 1)]
        jobs += [("row", "uk", t, 0), ("row", "uk", t, 1)]
        if t >= 2:
            jobs += late[:2]
            late = late[2:]
        jobs += [("rowT", "uq", t, 0), ("rowT", "uq", t, 1)]
        if t >= 4:
            mod(1, (t - 4,))
        prev = t
    jobs += late + [("rowT", "uk", prev, 0), ("rowT", "uk", prev, 1)]
    return jobs


ITEMS = {"bq": (8, 64, 64, 0), "bk": (8, 64, 64, 1), "uq": (8, 96, 32, 0), "uk": (8, 96, 32, 1),
         "q0": (4, 128, 128, 0), "q1": (4, 128, 128, 0), "kv": (2, 128, 128, 1), "c0": (2, 0, 0, 0)}
TABLE = {"b": "tabB", "u": "tabA", "q": "tabC", "k": "tabC"}


def project(nc, A, K, sem, PS, layer):
    jobs = plan_project(layer)
    L = f"p{layer}_"
    ordinal, done_by = {}, {}
    for i, job in enumerate(jobs):
        ordinal[job] = i
    free_name = {"mod": "modrow", "modT": "modcol", "hT": "h_evac", "v": "e_done", "gate": "gate_out"}
    counts = {}

    def free_of(job):
        kind = job[0]
        if kind == "row":
            if job[1] == "c0":
                return "x_in"
            return "e_done" if job[1] in ("kv", "uk") else "x_in"
        if kind == "rowT":
            return "cq_out" if job[1] == "c0" else "e_done"
        return free_name[kind]

    for i, job in enumerate(jobs):
        n = free_of(job)
        counts[n] = counts.get(n, 0) + 1
        done_by[job] = (n, counts[n])
    order_e = [j for j in jobs if free_of(j) == "e_done"]
    items = []
    for j in jobs:
        if j[0] == "row" and (j[1], j[2]) not in items:
            items.append((j[1], j[2]))
    item_no = {it: i for i, it in enumerate(items)}
    e_no = {j: i for i, j in enumerate(order_e)}
    gs_jobs = [j for j in jobs if j[0] == "gate" or (j[0] == "rowT" and j[1] == "c0")]
    gs_no = {j: i for i, j in enumerate(gs_jobs)}

    w_in = A["e_w_in"] if layer == 0 else A["o_w_in"]
    if layer == 0:
        cols = {"c0": (0, W0), "bq": (E_BQ, 512), "bk": (E_BK, 512), "bv": (E_BV, 512),
                "ga": (E_GATE_A, 512), "gb": (E_GATE_B, 512)}
        chunk_order = ["c0", "bq", "bk", "bv", "ga", "u", "gb"]
    else:
        cols = {"kv": (O_K, 512), "q0": (0, 512), "q1": (512, 512), "ga": (O_GATE, 512), "gb": (O_GATE + 512, 512)}
        chunk_order = ["kv", "q0", "q1", "ga", "gb"]
    pieces, piece_of = [], {}
    for c in chunk_order:
        if c == "u":
            srcs = [(A["a_w_uq"][0, k * P:(k + 1) * P, h * 384:(h + 1) * 384], 384) for k in range(2) for h in range(2)]
            srcs += [(A["a_w_ukv"][0, :, h * 512:(h + 1) * 512], 512) for h in range(2)]
        else:
            o, n = cols[c]
            srcs = [(w_in[0, k * P:(k + 1) * P, o:o + n], n) for k in range(KD)]
        for k, s in enumerate(srcs):
            piece_of[c, k] = len(pieces)
            pieces.append(s)
    mods = [("mod", l, j) for (k, l, j) in [x for x in jobs if x[0] == "mod"]]

    raws = []

    def chunk_raws(c):
        return [("w", piece_of[c, k]) for k in range(6 if c == "u" else KD)]

    def mod_raws(js):
        return [("m", j, k) for j in js for k in range(KD)]

    if layer == 0:
        m = mod_raws(mods[:4])
        w = chunk_raws("c0")
        for i, x in enumerate(m):
            raws.append(x)
            if i % 4 == 1:
                raws.append(w[i // 4])
        raws += chunk_raws("bq") + mod_raws(mods[4:6])
        for c in chunk_order[2:]:
            raws += chunk_raws(c)
        raws += mod_raws(mods[6:])
    else:
        for c in chunk_order:
            raws += chunk_raws(c)
    raw_no = {r: i for i, r in enumerate(raws)}
    m_no = {r: i for i, r in enumerate([r for r in raws if r[0] == "m" and r[2] < KD - 1])}
    w_order = [r[1] for r in raws if r[0] == "w"]
    assert w_order == sorted(w_order)

    def raw_landed(r):
        i = raw_no[r]
        return f"raw{i % RAW}", 16 * (i // RAW + 1)

    split_at = {}
    pos = {}
    for i, j in enumerate(jobs):
        if j[0] in ("row", "v", "gate"):
            pos.setdefault(j[1], []).append(j)
    seq = ["c0", "bq", "bk", "bv", "ga"] if layer == 0 else ["kv", "q0", "q1", "ga"]
    nxt = {"c0": ["bq"], "bq": ["bk"], "bk": ["bv"], "bv": ["ga"], "ga": ["u", "gb"]} if layer == 0 else \
        {"kv": ["q0"], "q0": ["q1"], "q1": ["ga"], "ga": ["gb"]}
    for c in seq:
        want = [p for n in nxt[c] for p in range(piece_of[n, 0], piece_of[n, 0] + (6 if n == "u" else KD))]
        at = pos[c]
        for k, p in enumerate(want):
            if layer == 0 and c == "ga" and k >= 8:
                split_at.setdefault(at[-1], []).append(p)
            else:
                split_at.setdefault(at[min(k, len(at) - 1)], []).append(p)

    chunk_of = {p: c for (c, _), p in piece_of.items()}

    with ExitStack() as ctx:
        def sb(name, shape, dt=F32):
            return ctx.enter_context(nc.sbuf_tensor(L + name, shape, dt))

        hh = sb("hT_hi", [P, KD, TOK], F32R)
        hl = sb("hT_lo", [P, KD, TOK], F32R)
        wh = sb("w_hi", [P, WR, 512], F32R)
        wl = sb("w_lo", [P, WR, 512], F32R)
        raw = sb("raw", [P, RAW, 512])
        X = sb("x_rows", [P, 2, 768])
        SQ = sb("squares", [P, 768])
        junk = sb("junk", [P, D], mybir.dt.bfloat16)
        Y = sb("y_rows", [P, 2, 768])
        U = sb("rope_u", [P, 512])
        V = sb("rope_v", [P, 512])
        eh = sb("e_hi", [P, 2, 512], F32R)
        el = sb("e_lo", [P, 2, 512], F32R)
        gs = sb("gate_rows", [P, 2, 512])
        tb = sb("table", [P, 2, 256])
        st = sb("stats", [P, 2, 4, 8])
        ssx = sb("x_stats", [P, 2, 4])
        if layer == 0:
            mrow = sb("mod_row", [2, 512])
            mb = sb("mod_bg", [2, 2, 512])
            with nc.sbuf_tensor(L + "x_tiles", [P, 2, D], F32) as xt:
                pass
            cl = sb("c_in", [P, 2, 384])
            chh = sb("c_hi", [P, 384], F32R)
            cll = sb("c_lo", [P, 384], F32R)
            kr = sb("kr_in", [P, 2, A_ROPE])
            sb("rest_of_x_tiles", [P, 2 * D - 4 * 384 - 2 * A_ROPE])
            tmpv = Y[:].rearrange("p a b -> p (a b)")[:, 0:D]
        else:
            xt = sb("x_tiles", [P, 2, D])
            tmpv = sb("modulated", [P, D])[:]

        S = {}

        def s(name):
            if name not in S:
                S[name] = sem(L + name)
            return S[name]

        block = ctx.enter_context(nc.Block())

        def free_wait(eng, i):
            if i >= 8:
                n, v = done_by[jobs[i - 8]]
                if n == "x_in":
                    v = x_in_value[jobs[i - 8]]
                eng.wait_ge(s(n), v)

        x_in_value, k = {}, 0
        for j in jobs:
            if j[0] == "row":
                k += 1
                x_in_value[j] = k
        last_piece = {}
        for j in jobs:
            if j[0] == "row":
                last_piece[j[1], j[2]] = x_in_value[j]

        c_split_at, c_load_at = {}, {}
        if layer == 0:
            last_ga = [j for j in jobs if j[0] == "gate" and j[1] == "ga"]
            c_load_at[last_ga[0]] = 0
            c_load_at[last_ga[1]] = 1
            c_split_at[last_ga[-1]] = 0
            for t in range(NT - 1):
                c_split_at["row", "uk", t, 1] = t + 1
                if t + 2 < NT:
                    c_load_at["row", "uk", t, 1] = t + 2

        tab_no, y_user, per_slot = {}, {}, [0, 0]
        rope_items = [it for it in items if it[0] != "c0"]
        for it in rope_items:
            b = item_no[it] % 2
            per_slot[b] += 1
            tab_no[it] = per_slot[b]
        last_T = {}
        for j in jobs:
            if j[0] == "rowT" and j[1] != "c0":
                last_T[j[1], j[2]] = ordinal[j]
        for it in rope_items:
            r = item_no[it]
            if r >= 2 and items[r - 2] in last_T:
                y_user[r] = last_T[items[r - 2]]

        def store_of(j, t_ap, half):
            kind, c, t = j[:3]
            tok = slice(t * P, (t + 1) * P)
            if kind == "v":
                return [(A["vB" + half][tok, :], t_ap)]
            if kind == "row" and c == "uk":
                return [(A["vA" + half][tok, j[3] * 256:(j[3] + 1) * 256], t_ap[:, 0:256])]
            if kind == "row" and c == "kv":
                return [(A["vC" + half][tok, :], t_ap[:, 0:256])]
            v = t_ap.rearrange("p (h n) -> p h n", h=4)
            if c in ("uq", "uk"):
                u = (0 if c == "uq" else 8) + 4 * j[3]
                return [(A["qkA" + half][u:u + 4, :, tok].rearrange("h p n -> p h n"), v[0:A_QK])]
            if c in ("bq", "bk"):
                return [(A["qkB" + half][0 if c == "bq" else 1, :, :, tok].rearrange("h p n -> p h n"), v)]
            if c in ("q0", "q1"):
                u = 0 if c == "q0" else 4
                tk = slice((t - NCT) * P, (t - NCT + 1) * P)
                return [(A["qC" + half][u:u + 4, :, tk].rearrange("h p n -> p h n"), v)]
            return [(A["kC" + half][:, :, tok].rearrange("h p n -> p h n"), v[:, 0:2, :])]

        def e_free(eng, e):
            if e >= 2:
                eng.wait_ge(s(f"e_st{e % 2}"), 32 * (e // 2))

        def g_free(eng, g):
            if g >= 2:
                eng.wait_ge(s(f"g_st{g % 2}"), 16 * (g // 2))

        def row_slot_free(eng, r):
            if r >= 2:
                c, t = items[r - 2]
                eng.wait_ge(s("y_ready"), r - 1)
                if c == "c0":
                    eng.wait_ge(s("job"), ordinal["rowT", "c0", t] + 1)
                    eng.wait_ge(s(f"kr_st{t % 2}"), 16 * (t // 2 + 1))

        def load_mod(act, j):
            _, l, jj = j
            m = mods.index(j)
            if m:
                act.wait_ge(s("modrow"), m)
            bias, g = (A["e_b_mod"], A["e_norm_g"]) if l == 0 else (A["o_b_mod"], A["o_norm_g"])
            act.dma_start(mb[:, 0, :], bias[0, jj * 512:(jj + 1) * 512].partition_broadcast(2)).then_inc(s("mbg"), 16)
            if jj in (2, 3):
                act.dma_start(mb[:, 1, :], g[0, (jj - 2) * 512:(jj - 1) * 512].partition_broadcast(2))\
                    .then_inc(s("mbg"), 16)

        def load_table(act, c, t, r):
            n, qk, rd = TABLE[c[0]], ITEMS[c][3], ITEMS[c][2]
            act.dma_start(tb[:, r % 2, 0:2 * rd], A[n][t * P:(t + 1) * P, qk, :, :].rearrange("p a f -> p (a f)"))\
                .then_inc(s(f"tab{r % 2}"), 16)

        def load_c(act, t):
            if t == 0:
                for b in range(2):
                    act.wait_ge(s(f"g_st{b}"), 16 * (NT // 2))
                for b in range(2):
                    act.wait_ge(s(f"kr_st{b}"), 16 * NT // 2)
            if t >= 2:
                act.wait_ge(s("c_split"), t - 1)
                act.wait_ge(s("x_in"), x_in_value["row", "uk", t - 2, 1])
            act.dma_start(cl[:, t % 2, :].rearrange("p (k n) -> p k n", k=3),
                          A["cT"][:, :, t * P:(t + 1) * P].rearrange("k p n -> p k n")).then_inc(s(f"c_in{t % 2}"), 16)
            act.dma_start(kr[:, t % 2, :], A["krow"][t * P:(t + 1) * P, :]).then_inc(s(f"c_in{t % 2}"), 16)

        def x_stats(dve, ch, t):
            b = t % 2
            dve.wait_ge(s("xss"), t + 1)
            nc.vector.tensor_scalar(ssx[:, b, 1:2], ssx[:, b, 0:1], 1.0 / D, EPS, ALU.mult, ALU.add)\
                .then_inc(s("xvar"), 1)
            dve.wait_ge(s("xsd"), t + 1)
            nc.vector.reciprocal(ssx[:, b, 3:4], ssx[:, b, 2:3]).then_inc(s("xrs"), 1)

        def row_norm(dve, ch, c, t, r):
            nh, hd, rd, qk = ITEMS[c]
            b = r % 2
            x, q, y = X[:, b, :], SQ[:], Y[:, b, :]
            dve.wait_ge(s("x_in"), last_piece[c, t])
            if c == "c0":
                nc.vector.tensor_reduce(st[:, b, 0, 0:1], q[:, 0:256], AX, ALU.add)
                ch.link(nc.vector.tensor_reduce(st[:, b, 0, 1:2], q[:, 256:384], AX, ALU.add))
                nc.vector.tensor_scalar(st[:, b, 1, 0:1], st[:, b, 0, 0:1], 1.0 / A_Q_LORA, EPS, ALU.mult, ALU.add)
                nc.vector.tensor_scalar(st[:, b, 1, 1:2], st[:, b, 0, 1:2], 1.0 / A_KV_LORA, EPS, ALU.mult, ALU.add)\
                    .then_inc(s("var"), 1)
                dve.wait_ge(s("sd"), r + 1)
                ch.link(nc.vector.reciprocal(st[:, b, 3, 0:2], st[:, b, 2, 0:2]))
                nc.vector.tensor_scalar(x[:, 0:256], x[:, 0:256], st[:, b, 3, 0:1], None, ALU.mult)
                nc.vector.tensor_scalar(x[:, 256:384], x[:, 256:384], st[:, b, 3, 1:2], None, ALU.mult)\
                    .then_inc(s("y_ready"), 1)
                return
            w = nh * hd
            x3 = x[:, 0:w].rearrange("p (h n) -> p h n", h=nh)
            y3 = y[:, 0:w].rearrange("p (h n) -> p h n", h=nh)
            q3 = q[:, 0:w].rearrange("p (h n) -> p h n", h=nh)
            ch.link(nc.vector.tensor_reduce(st[:, b, 0, 0:nh], q3, AX, ALU.add))
            nc.vector.tensor_scalar(st[:, b, 1, 0:nh], st[:, b, 0, 0:nh], 1.0 / hd, EPS, ALU.mult, ALU.add)\
                .then_inc(s("var"), 1)
            dve.wait_ge(s("sd"), r + 1)
            ch.link(nc.vector.reciprocal(st[:, b, 3, 0:nh], st[:, b, 2, 0:nh]))
            ch.link(nc.vector.tensor_tensor(x3, x3, st[:, b, 3, 0:nh].unsqueeze(2).to_broadcast([P, nh, hd]), ALU.mult))
            dve.wait_ge(s(f"tab{b}"), 16 * tab_no[c, t])
            prev = y_user.get(r)
            if prev is not None:
                dve.wait_ge(s("job"), prev + 1)
            o, h2 = hd - rd, rd // 2
            tv = tb[:, b, 0:2 * rd].rearrange("p (a f) -> p a f", a=2)
            u3 = U[:, 0:nh * rd].rearrange("p (h n) -> p h n", h=nh)
            v3 = V[:, 0:nh * rd].rearrange("p (h n) -> p h n", h=nh)
            if o:
                nc.vector.tensor_tensor(y3[:, :, 0:o], x3[:, :, 0:o],
                                        K["gnope"][:, qk, :].unsqueeze(1).to_broadcast([P, nh, o]), ALU.mult)
            nc.vector.tensor_tensor(u3, x3[:, :, o:], tv[:, 0, :].unsqueeze(1).to_broadcast([P, nh, rd]), ALU.mult)
            ch.link(nc.vector.tensor_tensor(v3, x3[:, :, o:], tv[:, 1, :].unsqueeze(1).to_broadcast([P, nh, rd]), ALU.mult))
            nc.vector.tensor_tensor(y3[:, :, o:o + h2], u3[:, :, 0:h2], v3[:, :, h2:rd], ALU.subtract)
            nc.vector.tensor_tensor(y3[:, :, o + h2:], u3[:, :, h2:rd], v3[:, :, 0:h2], ALU.add)\
                .then_inc(s("y_ready"), 1)

        @block.sync
        def _(sp):
            for i, r in enumerate(raws):
                if i >= RAW:
                    o = raws[i - RAW]
                    if o[0] == "w":
                        sp.wait_ge(s("w_split"), o[1] + 1)
                    elif o[2] < KD - 1:
                        sp.wait_ge(s("m_used"), m_no[o] + 1)
                    else:
                        sp.wait_ge(s("job"), ordinal[o[1]] + 1)
                if r[0] == "w":
                    src, n = pieces[r[1]]
                else:
                    _, (_, l, j), k = r
                    wm = A["e_w_mod"] if l == 0 else A["o_w_mod"]
                    src, n = wm[0, k * P:(k + 1) * P, j * 512:(j + 1) * 512], 512
                sp.dma_start(raw[:, i % RAW, 0:n], src).then_inc(s(raw_landed(r)[0]), 16)

        @block.gpsimd
        def _(pool):
            def split(p):
                name, v = raw_landed(("w", p))
                pool.wait_ge(s(name), v)
                if p >= WR:
                    pool.wait_ge(s("job"), ordinal[pos[chunk_of[p - WR]][-1]] + 1)
                n = pieces[p][1]
                src = raw[:, raw_no["w", p] % RAW, 0:n]
                nc.gpsimd.tensor_copy(wh[:, p % WR, 0:n], src).then_inc(s("w_high"), 1)
                pool.wait_ge(s("w_high"), p + 1)
                nc.gpsimd.tensor_tensor(wl[:, p % WR, 0:n], src, wh[:, p % WR, 0:n].bitcast(F32),
                                        ALU.subtract).then_inc(s("w_split"), 1)

            for p in chunk_raws(chunk_order[0]):
                split(p[1])
            for i, j in enumerate(jobs):
                for p in split_at.get(j, ()):
                    split(p)
                if j in e_no:
                    e = e_no[j]
                    pool.wait_ge(s("e_done"), e + 1)
                    for src, name in ((eh, "h"), (el, "l")):
                        for dst, sap in store_of(j, src[:, e % 2, :], name):
                            pool.dma_start(dst, sap.bitcast(F32)).then_inc(s(f"e_st{e % 2}"), 16)
                if j in gs_no:
                    g = gs_no[j]
                    n, v = done_by[j]
                    pool.wait_ge(s(n), v)
                    if j[0] == "gate":
                        _, c, jj, a, n = j
                        row = (0 if c == "ga" else 512) + jj * P
                        a0 = a if layer == 0 else a - CTX
                        pool.dma_start(A[f"gateT{layer}"][row:row + P, a0:a0 + n], gs[:, g % 2, 0:n])\
                            .then_inc(s(f"g_st{g % 2}"), 16)
                    else:
                        t = j[2]
                        pool.dma_start(A["cT"][:, :, t * P:(t + 1) * P].rearrange("k p n -> p k n"),
                                       gs[:, g % 2, 0:384].rearrange("p (k n) -> p k n", k=3))\
                            .then_inc(s(f"g_st{g % 2}"), 16)
                if j[0] == "rowT" and j[1] == "c0":
                    t = j[2]
                    r = item_no["c0", t]
                    pool.dma_start(A["krow"][t * P:(t + 1) * P, :], X[:, r % 2, 384:416])\
                        .then_inc(s(f"kr_st{t % 2}"), 16)
                if j[0] == "mod" and j[2] >= 4:
                    n, v = done_by[j]
                    pool.wait_ge(s(n), v)
                    pool.dma_start(A["grow"][j[1], :, (j[2] - 4) * 512:(j[2] - 3) * 512], mrow[:])\
                        .then_inc(s("grow_st"), 16)
            for b in range(2):
                pool.wait_ge(s(f"e_st{b}"), 32 * len(order_e[b::2]))
                pool.wait_ge(s(f"g_st{b}"), 16 * len(gs_jobs[b::2]))
            if layer == 0:
                for b in range(2):
                    pool.wait_ge(s(f"kr_st{b}"), 16 * NT // 2)
                pool.wait_ge(s("grow_st"), 16 * 4)

        @block.scalar
        def _(act):
            def load_x(t):
                if t >= 2:
                    act.wait_ge(s("job"), ordinal["hT", t - 2, 1] + 1)
                src = (A["x0c"][t * P:(t + 1) * P, :] if t < NCT else A["x0l"][(t - NCT) * P:(t - NCT + 1) * P, :]) \
                    if layer == 0 else A["x1"][t * P:(t + 1) * P, :]
                act.dma_start(xt[:, t % 2, :], src).then_inc(s(f"xt{t % 2}"), 16)

            def norm_x(t):
                act.wait_ge(s(f"xt{t % 2}"), 16 * (t // 2 + 1))
                nc.scalar.activation(junk[:], xt[:, t % 2, :], ACT.Square, accum_out=ssx[:, t % 2, 0:1]).then_inc(s("xss"), 1)
                act.wait_ge(s("xvar"), t + 1)
                nc.scalar.activation(ssx[:, t % 2, 2:3], ssx[:, t % 2, 1:2], ACT.Sqrt).then_inc(s("xsd"), 1)
                act.wait_ge(s("xrs"), t + 1)
                nc.scalar.activation(xt[:, t % 2, :], xt[:, t % 2, :], ACT.Copy, scale=ssx[:, t % 2, 3:4])\
                    .then_inc(s("xn"), 1)

            load_x(0)
            load_x(1)
            norm_x(0)
            for j in jobs:
                i = ordinal[j]
                bank = PS[:, i % 8, :]
                if j[0] == "mod":
                    load_mod(act, j)
                elif j[0] == "hT":
                    _, t, half = j
                    act.wait_ge(s("h_evac"), 2 * t + half + 1)
                    dst = hh[:, 4 * half:4 * half + 4, t * P:(t + 1) * P]
                    nc.scalar.activation(dst, tmpv[:, half * 512:(half + 1) * 512].rearrange("p (k n) -> p k n", k=4),
                                         ACT.Copy).then_inc(s("h_high"), 1)
                    if half == 1 and t + 1 < NT:
                        norm_x(t + 1)
                        if t + 2 < NT:
                            load_x(t + 2)
                elif j[0] == "row":
                    c, t = j[1], j[2]
                    r = item_no[c, t]
                    nh, hd, rd, _ = ITEMS[c]
                    piece = j[3] if len(j) > 3 else 0
                    if piece == 0:
                        row_slot_free(act, r)
                        if c != "c0":
                            load_table(act, c, t, r)
                    x, q = X[:, r % 2, :], SQ[:]
                    act.wait_ge(s("job"), i + 1)
                    if c == "c0":
                        nc.scalar.activation(q[:, 0:384], bank[:, 0:384], ACT.Square)
                        nc.scalar.activation(x[:, 0:W0], bank[:, 0:W0], ACT.Copy).then_inc(s("x_in"), 1)
                    elif c == "uk":
                        kvv = bank.rearrange("p (h n) -> p h n", h=4)
                        xk = x.rearrange("p (h n) -> p h n", h=8)[:, 4 * piece:4 * piece + 4, :]
                        qk = q.rearrange("p (h n) -> p h n", h=8)[:, 4 * piece:4 * piece + 4, :]
                        krb = kr[:, t % 2, :].unsqueeze(1).to_broadcast([P, 4, A_ROPE])
                        nc.scalar.activation(qk[:, :, 0:A_NOPE], kvv[:, :, 0:A_NOPE], ACT.Square)
                        nc.scalar.activation(qk[:, :, A_NOPE:], krb, ACT.Square)
                        nc.scalar.activation(xk[:, :, 0:A_NOPE], kvv[:, :, 0:A_NOPE], ACT.Copy)
                        nc.scalar.activation(xk[:, :, A_NOPE:], krb, ACT.Copy).then_inc(s("x_in"), 1)
                        e = e_no[j]
                        e_free(act, e)
                        nc.scalar.activation(eh[:, e % 2, 0:256].rearrange("p (h n) -> p h n", h=4),
                                             kvv[:, :, A_NOPE:], ACT.Copy).then_inc(s("e_high"), 1)
                    else:
                        n = 384 if c == "uq" else nh * hd
                        o = piece * 384
                        nc.scalar.activation(q[:, o:o + n], bank[:, 0:n], ACT.Square)
                        nc.scalar.activation(x[:, o:o + n], bank[:, 0:n], ACT.Copy).then_inc(s("x_in"), 1)
                        if c == "kv":
                            e = e_no[j]
                            e_free(act, e)
                            nc.scalar.activation(eh[:, e % 2, 0:256], bank[:, 256:512], ACT.Copy)\
                                .then_inc(s("e_high"), 1)
                    if x_in_value[j] == last_piece[c, t]:
                        act.wait_ge(s("var"), r + 1)
                        nc.scalar.activation(st[:, r % 2, 2, 0:nh], st[:, r % 2, 1, 0:nh], ACT.Sqrt)\
                            .then_inc(s("sd"), 1)
                elif j[0] in ("v", "rowT") and j in e_no:
                    e = e_no[j]
                    act.wait_ge(s("job"), i + 1)
                    e_free(act, e)
                    rows, n = (A_QK, 512) if j[1] in ("uq", "uk") else (P, 256 if j[1] == "kv" else 512)
                    nc.scalar.activation(eh[0:rows, e % 2, 0:n], bank[0:rows, 0:n], ACT.Copy).then_inc(s("e_high"), 1)
                elif j[0] == "gate":
                    g = gs_no[j]
                    n = j[4]
                    act.wait_ge(s("job"), i + 1)
                    g_free(act, g)
                    nc.scalar.activation(gs[:, g % 2, 0:n], bank[:, 0:n], ACT.Copy).then_inc(s("gate_out"), 1)
                if layer == 0:
                    t = c_split_at.get(j)
                    if t is not None:
                        act.wait_ge(s(f"c_in{t % 2}"), 32 * (t // 2 + 1))
                        if t:
                            act.wait_ge(s("job"), ordinal["row", "uk", t - 1, 1] + 1)
                        nc.scalar.activation(chh[:], cl[:, t % 2, :], ACT.Copy).then_inc(s("c_high"), 1)
                    t = c_load_at.get(j)
                    if t is not None:
                        load_c(act, t)

        @block.vector
        def _(dve):
            ch = Chain(nc, dve, s("chain"))
            x_stats(dve, ch, 0)
            for j in jobs:
                i = ordinal[j]
                bank = PS[:, i % 8, :]
                if j[0] == "mod":
                    _, l, jj = j
                    m = mods.index(j)
                    dve.wait_ge(s("job"), i + 1)
                    dve.wait_ge(s("mbg"), 16 * sum(2 if x[2] in (2, 3) else 1 for x in mods[:m + 1]))
                    if m:
                        prev = mods[m - 1]
                        if prev[2] < 4:
                            dve.wait_ge(s("job"), ordinal["modT", prev[1], prev[2]] + 1)
                        else:
                            dve.wait_ge(s("grow_st"), 16 * len([x for x in mods[:m] if x[2] >= 4]))
                    last = nc.vector.tensor_tensor(mrow[:], bank[0:2, :], mb[:, 0, :], ALU.add)
                    if jj in (2, 3):
                        ch.link(last)
                        last = nc.vector.scalar_tensor_tensor(mrow[:], mrow[:], 1.0, mb[:, 1, :], ALU.add, ALU.mult)
                    last.then_inc(s("modrow"), 1)
                elif j[0] == "modT":
                    _, l, jj = j
                    dve.wait_ge(s("job"), i + 1)
                    nc.vector.tensor_copy(K["modc"][:, l, jj // 2, 4 * (jj % 2):4 * (jj % 2) + 4, :],
                                          bank[:, 0:8].rearrange("p (k a) -> p k a", a=2)).then_inc(s("modcol"), 1)
                elif j[0] == "hT":
                    _, t, half = j
                    side = 0 if t < NCT else 1
                    if t == 0 and layer == 0:
                        dve.wait_ge(s("modcol"), 4)
                    if t:
                        dve.wait_ge(s("h_low"), 2 * (t - 1) + half + 1)
                    dve.wait_ge(s("job"), i + 1)
                    for k in range(4):
                        kt = 4 * half + k
                        last = nc.vector.tensor_scalar(tmpv[:, kt * P:(kt + 1) * P], bank[:, k * P:(k + 1) * P],
                                                       K["modc"][:, layer, 1, kt, side:side + 1],
                                                       K["modc"][:, layer, 0, kt, side:side + 1], ALU.mult, ALU.add)
                    last.then_inc(s("h_evac"), 1)
                    if half == 1:
                        for b in range(2):
                            dve.wait_ge(s("h_high"), 2 * t + b + 1)
                            hs = (slice(None), slice(4 * b, 4 * b + 4), slice(t * P, (t + 1) * P))
                            nc.vector.tensor_tensor(hl[hs], tmpv[:, b * 512:(b + 1) * 512].rearrange("p (k n) -> p k n", k=4),
                                                    hh[hs].bitcast(F32), ALU.subtract).then_inc(s("h_low"), 1)
                        if t + 1 < NT:
                            x_stats(dve, ch, t + 1)
                elif j[0] == "row":
                    c, t = j[1], j[2]
                    r = item_no[c, t]
                    if j in e_no:
                        e = e_no[j]
                        dve.wait_ge(s("e_high"), e + 1)
                        if c == "uk":
                            src = bank.rearrange("p (h n) -> p h n", h=4)[:, :, A_NOPE:]
                            nc.vector.tensor_tensor(el[:, e % 2, 0:256].rearrange("p (h n) -> p h n", h=4), src,
                                                    eh[:, e % 2, 0:256].rearrange("p (h n) -> p h n", h=4).bitcast(F32),
                                                    ALU.subtract).then_inc(s("e_done"), 1)
                        else:
                            nc.vector.tensor_tensor(el[:, e % 2, 0:256], bank[:, 256:512],
                                                    eh[:, e % 2, 0:256].bitcast(F32), ALU.subtract)\
                                .then_inc(s("e_done"), 1)
                    if x_in_value[j] == last_piece[c, t]:
                        row_norm(dve, ch, c, t, r)
                elif j[0] == "rowT" and j[1] == "c0":
                    g = gs_no[j]
                    dve.wait_ge(s("job"), i + 1)
                    g_free(dve, g)
                    for k in range(3):
                        last = nc.vector.tensor_scalar(gs[:, g % 2, k * P:(k + 1) * P], bank[:, k * P:(k + 1) * P],
                                                       K["gcol"][:, k:k + 1], None, ALU.mult)
                    last.then_inc(s("cq_out"), 1)
                elif j[0] in ("v", "rowT"):
                    e = e_no[j]
                    rows, n = (A_QK, 512) if j[1] in ("uq", "uk") else (P, 256 if j[1] == "kv" else 512)
                    dve.wait_ge(s("e_high"), e + 1)
                    nc.vector.tensor_tensor(el[0:rows, e % 2, 0:n], bank[0:rows, 0:n],
                                            eh[0:rows, e % 2, 0:n].bitcast(F32), ALU.subtract).then_inc(s("e_done"), 1)
                if layer == 0:
                    t = c_split_at.get(j)
                    if t is not None:
                        dve.wait_ge(s("c_high"), t + 1)
                        nc.vector.tensor_tensor(cll[:], cl[:, t % 2, :], chh[:].bitcast(F32), ALU.subtract)\
                            .then_inc(s("c_split"), 1)

        @block.tensor
        def _(pe):
            def landed(c, k):
                pe.wait_ge(s("w_split"), piece_of[c, k] + 1)

            for j in jobs:
                i = ordinal[j]
                bank = PS[:, i % 8, :]
                free_wait(pe, i)
                kind = j[0]
                if kind == "mod":
                    for k in range(KD):
                        n, v = raw_landed(("m", j, k))
                        pe.wait_ge(s(n), v)
                        last = nc.tensor.matmul(bank[0:2, :], K["cT"][:, k:16:8],
                                                raw[:, raw_no["m", j, k] % RAW, :], start=k == 0, stop=k == KD - 1)
                        if k < KD - 1:
                            last.then_inc(s("m_used"), 1)
                    last.then_inc(s("job"), 1)
                elif kind == "modT":
                    pe.wait_ge(s("modrow"), done_by["mod", j[1], j[2]][1])
                    for k in range(4):
                        last = nc.tensor.transpose(bank[:, 2 * k:2 * k + 2], mrow[:, k * P:(k + 1) * P],
                                                   K["idn"][0:2, 0:2])
                    last.then_inc(s("job"), 1)
                elif kind == "hT":
                    _, t, half = j
                    pe.wait_ge(s("xn"), t + 1)
                    for k in range(4):
                        last = nc.tensor.transpose(bank[:, k * P:(k + 1) * P],
                                                   xt[:, t % 2, (4 * half + k) * P:(4 * half + k + 1) * P], K["idn"][:])
                    last.then_inc(s("job"), 1)
                elif kind == "rowT":
                    c, t = j[1], j[2]
                    r = item_no[c, t]
                    pe.wait_ge(s("y_ready"), r + 1)
                    part = j[3] if len(j) > 3 else 0
                    nb, w = (3, P) if c == "c0" else (4, A_QK) if c in ("uq", "uk") else (2, P) if c == "kv" else (4, P)
                    src = X if c == "c0" else Y
                    for k in range(nb):
                        o = (4 * part + k) * w
                        last = nc.tensor.transpose(bank[0:w, k * P:(k + 1) * P], src[:, r % 2, o:o + w], K["idn"][:])
                    last.then_inc(s("job"), 1)
                elif kind in ("row", "v") and j[1] not in ("uq", "uk"):
                    c, t = j[1], j[2]
                    pe.wait_ge(s("h_low"), 2 * t + 2)
                    n = cols[c][1]
                    tok = slice(t * P, (t + 1) * P)
                    for k in range(KD):
                        if j == pos[c][0]:
                            landed(c, k)
                        w = piece_of[c, k] % WR
                        last = three_passes(nc, bank[:, 0:n], (hh[:, k, tok], hl[:, k, tok]),
                                            (wh[:, w, 0:n], wl[:, w, 0:n]), k == 0, k == KD - 1)
                    last.then_inc(s("job"), 1)
                elif kind == "gate":
                    _, c, jj, a, n = j
                    for k in range(KD):
                        if j == pos[c][0]:
                            landed(c, k)
                        w = piece_of[c, k] % WR
                        cs = slice(jj * P, (jj + 1) * P)
                        last = three_passes(nc, bank[:, 0:n], (wh[:, w, cs], wl[:, w, cs]),
                                            (hh[:, k, a:a + n], hl[:, k, a:a + n]), k == 0, k == KD - 1)
                    last.then_inc(s("job"), 1)
                else:
                    c, t, part = j[1:]
                    if c == "uq" and part == 0:
                        pe.wait_ge(s("c_split"), t + 1)
                    if t == 0:
                        landed("u", 5)
                    ks = (0, 1) if c == "uq" else (2,)
                    n = 384 if c == "uq" else 512
                    for k in ks:
                        w = piece_of["u", 2 * k + part] % WR
                        last = three_passes(nc, bank[:, 0:n], (chh[:, k * P:(k + 1) * P], cll[:, k * P:(k + 1) * P]),
                                            (wh[:, w, 0:n], wl[:, w, 0:n]), k == ks[0], k == ks[-1])
                    last.then_inc(s("job"), 1)



class Unit:

    def __init__(self, it, s, R, kv=None):
        self.it, self.s, self.R, self.kv = it, s, R, kv

    def value(self, a, c=0, per=1):
        return self.it * (a * self.R // per) + (a * (self.s // per) + c)

    def next(self, kv=None):
        return Unit(self.it, self.s + 1, self.R, kv)

    def wait(self, eng, sem, a, c=0, per=1):
        v = self.value(a, c, per)
        if not isinstance(v, int) or v > 0:
            eng.wait_ge(sem, v)


class Plan:

    def __init__(self, kind, layer, ctx_queries):
        self.kind, self.ctx = kind, ctx_queries
        self.maps = 2 if kind == "B" else 1
        self.rows = A_QK if kind == "A" else P
        self.queries = CTX if ctx_queries else 512
        self.keys = CTX if ctx_queries else TOK
        self.QT, self.KT = self.queries // P, self.keys // P
        self.SEG = self.keys // 256
        heads = {"A": A_HEADS, "B": B_HEADS, "C": C_HEADS}[kind]
        self.per_head = 1 if ctx_queries else 2
        self.units = heads * self.per_head
        self.R = 2 if kind == "C" else 4
        self.QS = 4 if ctx_queries else 2
        self.KS = 4 if ctx_queries else 2
        self.ring = 4 if ctx_queries else 5
        if ctx_queries:
            self.chunks = [([(q, 0, 256) for q in range(2)], 0)]
            self.NC = 1
        else:
            self.chunks = [([(q, 0, 1024)], 0) for q in range(4)] + [([(q, 1024, 256) for q in range(4)], 1)]
            self.NC = 2
        self.C = len(self.chunks) * self.maps
        self.dve_segs = self.SEG if self.maps == 2 or ctx_queries else 1

    def parts(self, has_next):
        out = [("N", 0)]
        j = 0
        for kt in range(self.KT):
            new = has_next and (kt * self.C) % self.KT < self.C and j < self.C
            if new:
                out += [("S", j), ("M", j)]
            out.append(("T", kt))
            if new:
                out.append(("E", j))
                j += 1
            if kt % 2 == 0 and kt // 2 + 1 < self.SEG:
                out.append(("N", kt // 2 + 1))
            if kt >= 2:
                out.append(("PV", kt - 2))
        if has_next:
            assert j == self.C
            out.append(("STAT", 0))
        for kt in range(max(0, self.KT - 2), self.KT):
            out.append(("PV", kt))
        out.append(("OUT", 0))
        return out

    def walk(self, eng):
        R, n = self.R, self.units // self.R
        if self.kind == "C":
            segs = [(0, 1, False), (1, 3, True), (3, 4, False), (4, 7, True), (7, 8, False)]
        elif n > 2:
            segs = [(0, 1, False), (1, n - 1, True), (n - 1, n, False)]
        else:
            segs = [(0, n, False)]

        def kv(it0, s):
            return (it0 * R + s) // (R * n // 2) if self.kind == "C" else (s // self.per_head) % self.KS

        for a, b, loop in segs:
            if loop:
                with eng.Fori(a, b) as it:
                    for s in range(R):
                        u = Unit(it, s, R, kv(a, s))
                        yield u, u.next(kv(a, s + 1) if self.kind != "C" else kv(a, s))
            else:
                for it in range(a, b):
                    for s in range(R):
                        u = Unit(it, s, R, kv(it, s))
                        yield u, None if it == n - 1 and s == R - 1 else u.next(kv(it, s + 1))


def attention(nc, A, K, sem, PS, kind, layer, ctx_queries):
    pl = Plan(kind, layer, ctx_queries)
    L = f"{kind}{int(ctx_queries)}_"
    QN, QT, KT, C, NC, maps, ring = pl.queries, pl.QT, pl.KT, pl.C, pl.NC, pl.maps, pl.ring
    rows = pl.rows
    packed = kind == "A"
    n_kv = {"A": A_HEADS, "B": B_HEADS, "C": C_KV}[kind]
    nch = len(pl.chunks)
    with ExitStack() as ctx:
        def sb(name, shape, dt=F32):
            return ctx.enter_context(nc.sbuf_tensor(L + name, shape, dt))

        S = {}

        def s(name):
            if name not in S:
                S[name] = sem(L + name)
            return S[name]

        qh = sb("q_hi", [rows, pl.QS, maps, QN], F32R)
        ql = sb("q_lo", [rows, pl.QS, maps, QN], F32R)
        kh = sb("k_hi", [rows, pl.KS, maps, pl.keys], F32R)
        kl = None if kind == "B" else sb("k_lo", [rows, pl.KS, maps, pl.keys], F32R)
        vh = sb("v_hi", [P, pl.KS, KT, P], F32R)
        vl = None if packed else sb("v_lo", [P, pl.KS, KT, P], F32R)
        prob = sb("prob", [P, 2, maps, QT, pl.keys])
        th = sb("probT_hi", [P, ring, QN], F32R)
        tl = sb("probT_lo", [P, ring, QN], F32R)
        nm = sb("neg_max", [P, 2, maps, QT, NC])
        rs = sb("row_sum", [P, 2, maps, QT, NC])
        fc = sb("factor", [P, 2, maps, QT, NC])
        gn = sb("neg_max_all", [P, maps * QT])
        den = sb("denominator", [P, maps * QT])
        low = sb("out_low", [A_V, QN]) if packed else None
        od = sb("out_rows", [P, 2, QN])
        sc = [PS[:, 2 * b:2 * b + 2, :].rearrange("p a n -> p (a n)") for b in range(2)]
        tbank = [PS[:, 4 + b, :] for b in range(2)]
        obank = [PS[:, 6 + b, :] for b in range(2)]
        vrows = A_V if packed else P
        tok0 = 0 if ctx_queries else CTX
        base_q = 0 if kind == "C" else tok0
        n_qdma = 4 * maps if kind == "B" else 2
        n_kdma = 4 if kind == "B" else 2
        n_vdma = 2
        out_row0 = A_WIDTH if kind == "B" else 0
        out_col0 = 0 if kind == "C" else tok0

        block = ctx.enter_context(nc.Block())

        def q_head(u):
            return u.value(1, 0, pl.per_head)

        def load_q(sp, u):
            sl = u.s % pl.QS
            h = q_head(u)
            c0 = base_q + (0 if ctx_queries else 512 * (u.s % 2))
            cs = slice(c0, c0 + QN)
            q_in = s(f"q_in{sl}")
            for half, dst in (("h", qh), ("l", ql)):
                if kind == "A":
                    sp.dma_start(dst[:, sl, 0, :].bitcast(F32), A["qkA" + half][bass.ds(h, 1), :, cs].rearrange("a p n -> (a p) n"))\
                        .then_inc(q_in, 16)
                elif kind == "C":
                    sp.dma_start(dst[:, sl, 0, :].bitcast(F32), A["qC" + half][bass.ds(h, 1), :, cs].rearrange("a p n -> (a p) n"))\
                        .then_inc(q_in, 16)
                else:
                    for m in range(2):
                        for up in range(2):
                            src = A["qkB" + half][0, bass.ds(h, 1), m * B_D:(m + 1) * B_D, cs]
                            sp.dma_start(dst[up * B_D:(up + 1) * B_D, sl, m, :].bitcast(F32), src.rearrange("a p n -> (a p) n"))\
                                .then_inc(q_in, 16)

        def load_kv(sp, h, sl):
            kv_in = s(f"kv_in{sl}")
            ks = slice(0, pl.keys)
            if kind == "A":
                for half, dst in (("h", kh), ("l", kl)):
                    sp.dma_start(dst[:, sl, 0, :].bitcast(F32), A["qkA" + half][bass.ds(h + A_HEADS, 1), :, ks].rearrange("a p n -> (a p) n"))\
                        .then_inc(kv_in, 16)
                for i, half in enumerate("hl"):
                    sp.dma_start(vh[:, sl, :, i * A_V:(i + 1) * A_V].bitcast(F32),
                                 A["vA" + half].rearrange("(k p) (h n) -> p k h n", p=P, h=A_HEADS)[:, 0:KT, bass.ds(h, 1), :]
                                 .rearrange("p k a n -> p k (a n)")).then_inc(kv_in, 16)
            else:
                if kind == "C":
                    for half, dst in (("h", kh), ("l", kl)):
                        sp.dma_start(dst[:, sl, 0, :].bitcast(F32), A["kC" + half][h, :, ks]).then_inc(kv_in, 16)
                else:
                    for m in range(2):
                        for up, half in enumerate("hl"):
                            src = A["qkB" + half][1, bass.ds(h, 1), m * B_D:(m + 1) * B_D, ks]
                            sp.dma_start(kh[up * B_D:(up + 1) * B_D, sl, m, :].bitcast(F32), src.rearrange("a p n -> (a p) n"))\
                                .then_inc(kv_in, 16)
                nh = C_KV if kind == "C" else B_HEADS
                for half, dst in (("h", vh), ("l", vl)):
                    sp.dma_start(dst[:, sl, :, :].bitcast(F32),
                                 A["v" + kind + half].rearrange("(k p) (h n) -> p k h n", p=P, h=nh)[:, 0:KT, bass.ds(h, 1), :]
                                 .rearrange("p k a n -> p k (a n)")).then_inc(kv_in, 16)

        kv_dmas = 16 * (n_kdma + n_vdma)

        def wait_q(eng, u):
            eng.wait_ge(s(f"q_in{u.s % pl.QS}"), u.value(16 * n_qdma, 16 * n_qdma, pl.QS))

        def wait_kv(eng, u):
            if kind == "C":
                eng.wait_ge(s(f"kv_in{u.kv}"), kv_dmas)
            else:
                eng.wait_ge(s(f"kv_in{u.kv}"), u.value(kv_dmas, kv_dmas, pl.per_head * pl.KS))

        @block.sync
        def _(sp):
            for n in range(min(pl.KS, n_kv)):
                if n == 0:
                    load_q(sp, Unit(0, 0, pl.R))
                load_kv(sp, n, n)
            for n in range(1, pl.QS):
                load_q(sp, Unit(0, n, pl.R))

            def store(u):
                u.wait(sp, s("o_out"), 1, 1)
                h = q_head(u)
                c0 = out_col0 + (0 if ctx_queries else 512 * (u.s % 2))
                dst = A[f"oT{layer}"].rearrange("(h n) t -> h n t", n=vrows)[bass.ds(h + out_row0 // vrows, 1), :, c0:c0 + QN]
                sp.dma_start(dst.rearrange("a n t -> (a n) t"), od[0:vrows, u.s % 2, :]).then_inc(s(f"o_st{u.s % 2}"), 16)

            def loads(u):
                v = Unit(u.it, u.s + pl.QS, pl.R)
                known = isinstance(u.it, int)
                if not known or u.it * pl.R + u.s + pl.QS < pl.units:
                    u.wait(sp, s("scored"), C, C)
                    load_q(sp, v)
                if kind != "C" and u.s % pl.per_head == 0:
                    h1 = u.value(1, pl.KS - 1, pl.per_head)
                    first = known and u.it == 0 and u.s == 0
                    if not first and (not known or h1 < n_kv):
                        u.wait(sp, s("multiplied"), KT, 0)
                        load_kv(sp, h1, (u.s // pl.per_head + pl.KS - 1) % pl.KS)

            for u, nxt in pl.walk(sp):
                loads(u)
                store(u)
            for b in range(2):
                sp.wait_ge(s(f"o_st{b}"), 16 * (pl.units // 2))

        def probs_of(u, m, q, k0, n):
            return prob[:, u.s % 2, m, q, k0:k0 + n]

        def chunk_views(buf, pieces):
            n = pieces[0][2]
            return [(q, k0, n, buf[:, i * n:(i + 1) * n]) for i, (q, k0, n) in enumerate(pieces)]

        def both(eng, step):
            first = Unit(0, 0, pl.R, 0)
            for j in range(C):
                for part in ("S", "M", "E"):
                    step(None, first, (part, j))
            step(None, first, ("STAT", 0))
            for u, nxt in pl.walk(eng):
                for part in pl.parts(nxt is not None):
                    step(u, nxt, part)

        @block.tensor
        def _(pe):
            def step(u, nxt, part):
                what, i = part
                if what == "S":
                    m, jj = divmod(i, nch)
                    pieces, _ = pl.chunks[jj]
                    if i == 0:
                        wait_q(pe, nxt)
                        wait_kv(pe, nxt)
                    nxt.wait(pe, s("exped"), C, i - 1)
                    buf = sc[(nxt.s * C + i) % 2]
                    sl = nxt.s % pl.QS
                    for q, k0, n, view in chunk_views(buf, pieces):
                        qs = slice(q * P, (q + 1) * P)
                        for o in range(0, n, 512):
                            w = min(512, n - o)
                            ks = slice(k0 + o, k0 + o + w)
                            out = view[:, o:o + w]
                            if kind == "B":
                                nc.tensor.matmul(out, ql[:, sl, m, qs], kh[:, nxt.kv, m, ks], start=True, stop=False)
                                last = nc.tensor.matmul(out, qh[:, sl, m, qs], kh[:, nxt.kv, m, ks], start=False, stop=True)
                            else:
                                last = three_passes(nc, out, (qh[:, sl, 0, qs], ql[:, sl, 0, qs]),
                                                    (kh[:, nxt.kv, 0, ks], kl[:, nxt.kv, 0, ks]), True, True)
                    last.then_inc(s("scored"), 1)
                elif what == "T":
                    seg = i // 2
                    if seg < pl.dve_segs:
                        u.wait(pe, s("norm_dve"), pl.dve_segs, seg + 1)
                    else:
                        u.wait(pe, s("norm_pool"), pl.SEG - pl.dve_segs, seg - pl.dve_segs + 1)
                    u.wait(pe, s("split"), KT, i - 1)
                    bank = tbank[i % 2]
                    for q in range(QT):
                        last = nc.tensor.transpose(bank[:, q * P:(q + 1) * P], probs_of(u, 0, q, i * P, P), K["idn"][:])
                    last.then_inc(s("turned"), 1)
                elif what == "PV":
                    u.wait(pe, s("split"), KT, i + 1)
                    if i == 0:
                        u.wait(pe, s("o_out"), 1, -1)
                    r = (u.s * KT + i) % ring
                    out = obank[u.s % 2][:, 0:QN]
                    if packed:
                        def full():
                            return nc.tensor.matmul(out, vh[:, u.kv, i, :], th[:, r, :], start=i == 0, stop=i == KT - 1)

                        def top():
                            return nc.tensor.matmul(out[0:A_V], vh[:, u.kv, i, 0:A_V], tl[:, r, :], start=False, stop=False)

                        if i == 0:
                            full()
                            last = top()
                        else:
                            top()
                            last = full()
                    else:
                        last = three_passes(nc, out, (vh[:, u.kv, i, :], vl[:, u.kv, i, :]), (th[:, r, :], tl[:, r, :]),
                                            i == 0, i == KT - 1)
                    last.then_inc(s("multiplied"), 1)

            both(pe, step)

        @block.scalar
        def _(act):
            def step(u, nxt, part):
                what, i = part
                if what == "E":
                    m, jj = divmod(i, nch)
                    pieces, c = pl.chunks[jj]
                    if i == 0:
                        nxt.wait(act, s("turned"), KT, -KT)
                    nxt.wait(act, s("maxed"), C, i + 1)
                    b = nxt.s % 2
                    for q, k0, n, view in chunk_views(sc[(nxt.s * C + i) % 2], pieces):
                        last = nc.scalar.activation(probs_of(nxt, m, q, k0, n), view, ACT.Exp,
                                                    bias=nm[:, b, m, q, c:c + 1], accum_out=rs[:, b, m, q, c:c + 1])
                    last.then_inc(s("exped"), 1)
                elif what == "T":
                    u.wait(act, s("turned"), KT, i + 1)
                    u.wait(act, s("multiplied"), KT, i + 1 - ring)
                    r = (u.s * KT + i) % ring
                    nc.scalar.activation(th[:, r, :], tbank[i % 2][:, 0:QN], ACT.Copy).then_inc(s("high"), 1)
                elif what == "STAT" and NC > 1:
                    nxt.wait(act, s("diff"), 1, 1)
                    b = nxt.s % 2
                    f = fc[:, b].rearrange("p m q c -> p (m q c)")
                    nc.scalar.activation(f, f, ACT.Exp).then_inc(s("diff_exp"), 1)
                elif what == "OUT":
                    b = u.s % 2
                    u.wait(act, s("multiplied"), KT, KT)
                    if packed:
                        u.wait(act, s("o_out"), 1, 0)
                        nc.scalar.activation(low[:], obank[b][A_V:P, 0:QN], ACT.Copy).then_inc(s("o_low"), 1)
                    else:
                        u.wait(act, s(f"o_st{b}"), 16, 0, 2)
                        nc.scalar.activation(od[:, b, :], obank[b][:, 0:QN], ACT.Copy).then_inc(s("o_out"), 1)

            both(act, step)

        @block.gpsimd
        def _(pool):
            def step(u, nxt, part):
                what, i = part
                if what == "N":
                    c = min(i // 4, NC - 1)
                    if maps == 1 and i < pl.dve_segs:
                        return
                    if i == (0 if maps == 2 else pl.dve_segs):
                        u.wait(pool, s("factors"), 1, 1)
                        pool.sem_inc(s("pool_went_on"), 1)
                    for q in range(QT):
                        v = probs_of(u, 0, q, 256 * i, 256)
                        last = nc.gpsimd.tensor_scalar(v, v, fc[:, u.s % 2, 0, q, c:c + 1], None, ALU.mult)
                    last.then_inc(s("norm_pool"), 1)

            both(pool, step)

        @block.vector
        def _(dve):
            per = (4 if NC > 1 else 0) + (maps - 1)

            def step(u, nxt, part):
                what, i = part
                if what == "M":
                    m, jj = divmod(i, nch)
                    pieces, c = pl.chunks[jj]
                    nxt.wait(dve, s("scored"), C, i + 1)
                    n = pieces[0][2]
                    view = sc[(nxt.s * C + i) % 2][:, 0:n * len(pieces)].rearrange("p (q n) -> p q n", n=n)
                    q0 = pieces[0][0]
                    nc.vector.tensor_reduce(nm[:, nxt.s % 2, m, q0:q0 + len(pieces), c], view, AX, ALU.max,
                                            negate=True).then_inc(s("maxed"), 1)
                elif what == "T":
                    u.wait(dve, s("high"), KT, i + 1)
                    r = (u.s * KT + i) % ring
                    nc.vector.tensor_tensor(tl[:, r, :], tbank[i % 2][:, 0:QN], th[:, r, :].bitcast(F32),
                                            ALU.subtract).then_inc(s("split"), 1)
                elif what == "N":
                    c = min(i // 4, NC - 1)
                    if i >= pl.dve_segs:
                        return
                    if i == 0:
                        u.wait(dve, s("factors"), 1, 1)
                    if maps == 2:
                        u.wait(dve, s("norm_pool"), pl.SEG, i + 1)
                    for q in range(QT):
                        v = probs_of(u, 0, q, 256 * i, 256)
                        if maps == 2:
                            last = nc.vector.scalar_tensor_tensor(v, probs_of(u, 1, q, 256 * i, 256),
                                                                  fc[:, u.s % 2, 1, q, c:c + 1], v, ALU.mult, ALU.add)
                        else:
                            last = nc.vector.tensor_scalar(v, v, fc[:, u.s % 2, 0, q, c:c + 1], None, ALU.mult)
                    last.then_inc(s("norm_dve"), 1)
                elif what == "STAT":
                    b = nxt.s % 2
                    k = [0]

                    def link(ins):
                        k[0] += 1
                        ins.then_inc(s("chain"), 1)
                        nxt.wait(dve, s("chain"), per, k[0])

                    nxt.wait(dve, s("exped"), C, C)
                    flat = [t[:, b].rearrange("p m q c -> p (m q) c") for t in (nm, rs, fc)]
                    mq = maps * QT
                    if NC > 1:
                        link(nc.vector.tensor_reduce(gn[:], flat[0], AX, ALU.min))
                        nc.vector.tensor_tensor(flat[2], gn[:].unsqueeze(2).to_broadcast([P, mq, NC]), flat[0],
                                                ALU.subtract).then_inc(s("diff"), 1)
                        nxt.wait(dve, s("diff_exp"), 1, 1)
                        link(nc.vector.tensor_tensor(flat[1], flat[1], flat[2], ALU.mult))
                        link(nc.vector.tensor_reduce(den[:], flat[1], AX, ALU.add))
                        link(nc.vector.reciprocal(den[:], den[:]))
                        last = nc.vector.tensor_tensor(flat[2], flat[2], den[:].unsqueeze(2).to_broadcast([P, mq, NC]),
                                                       ALU.mult)
                    else:
                        last = nc.vector.reciprocal(flat[2], flat[1])
                    if maps == 2:
                        link(last)
                        f1 = fc[:, b, 1].rearrange("p q c -> p (q c)")
                        last = nc.vector.tensor_scalar(f1, f1, K["neglam"][:], None, ALU.mult)
                    last.then_inc(s("factors"), 1)
                    assert k[0] == per, (k, per)
                elif what == "OUT" and packed:
                    b = u.s % 2
                    u.wait(dve, s("o_low"), 1, 1)
                    u.wait(dve, s(f"o_st{b}"), 16, 0, 2)
                    nc.vector.tensor_tensor(od[0:A_V, b, :], obank[b][0:A_V, 0:QN], low[:], ALU.add)\
                        .then_inc(s("o_out"), 1)

            both(dve, step)



def out_project(nc, A, K, sem, PS, layer, out):
    L = f"o{layer}_"
    tiles = NT if layer == 0 else NT - NCT
    t0 = 0 if layer == 0 else NCT
    R = 2
    w_out = A["e_w_out"] if layer == 0 else A["o_w_out"]
    with ExitStack() as ctx:
        def sb(name, shape, dt=F32):
            return ctx.enter_context(nc.sbuf_tensor(L + name, shape, dt))

        S = {}

        def s(name):
            if name not in S:
                S[name] = sem(L + name)
            return S[name]

        wh = sb("w_hi", [P, KD, D], F32R)
        wl = sb("w_lo", [P, KD, D], F32R)
        raw = sb("raw", [P, 4, D])
        o = sb("o", [P, 2, KD, P])
        g = sb("g", [P, 2, KD, P])
        ge = sb("g_exp", [P, KD * P])
        sq = sb("o_sq", [P, 512])
        nrm = sb("o_norm", [P, 512])
        yh = sb("y_hi", [P, 2, KD, P], F32R)
        yl = sb("y_lo", [P, 2, KD, P], F32R)
        xt = sb("x", [P, 2, D])
        res = sb("res", [P, 2, D])
        gb = sb("gate_rows", [P, 2, D])
        ones = sb("ones", [P, P])
        gout = sb("b_gain", [P, 1])
        block = ctx.enter_context(nc.Block())

        def segs(eng):
            n = tiles // R
            if layer == 0:
                parts = [(0, 1, False), (1, n, True)]
            else:
                parts = [(0, 1, False), (1, n, True)]
            for a, b, loop in parts:
                if loop:
                    with eng.Fori(a, b) as it:
                        for q in range(R):
                            yield Unit(it, q, R)
                else:
                    for it in range(a, b):
                        for q in range(R):
                            yield Unit(it, q, R)

        def side(u):
            return 0 if layer == 0 and isinstance(u.it, int) else 1

        @block.sync
        def _(sp):
            def load(u):
                b = u.s
                tok = u.value(P, 0)
                if not (isinstance(u.it, int) and u.it == 0):
                    u.wait(sp, s("y_made"), 1, -1)
                    u.wait(sp, s("added"), 1, -1)
                sp.dma_start(o[:, b], A[f"oT{layer}"].rearrange("(k p) t -> p k t", p=P)[:, :, bass.ds(tok, P)])\
                    .then_inc(s(f"in{b}"), 16)
                sp.dma_start(g[:, b], A[f"gateT{layer}"].rearrange("(k p) t -> p k t", p=P)[:, :, bass.ds(tok, P)])\
                    .then_inc(s(f"in{b}"), 16)
                if layer == 0:
                    if side(u) == 0:
                        src = A["x0c"][u.s * P:(u.s + 1) * P, :]
                    else:
                        src = A["x0l"][bass.ds(u.value(P, -CTX), P), :]
                else:
                    src = A["x1"][bass.ds(u.value(P, CTX), P), :]
                sp.dma_start(xt[:, b], src).then_inc(s(f"in{b}"), 16)

            first = True
            for k in range(KD):
                if k >= 4:
                    sp.wait_ge(s("w_split"), k - 3)
                sp.dma_start(raw[:, k % 4, :], w_out[0, k * P:(k + 1) * P, :]).then_inc(s(f"raw{k % 4}"), 16)
                if k == 0:
                    for side_ in range(2):
                        sp.dma_start(gb[:, side_], A["grow"][layer, side_, :].partition_broadcast(P)).then_inc(s("small"), 16)
                    if layer == 0:
                        sp.dma_start(gout[:], A["b_g_out"][0, :].rearrange("(p a) -> p a", a=1),
                                     allow_slow_non_contiguous=True).then_inc(s("small"), 16)
                if k in (1, 2):
                    load(Unit(0, k - 1, R))
            for u in segs(sp):
                if not (isinstance(u.it, int) and u.it == 0):
                    load(u)
            for b in range(2):
                sp.wait_ge(s(f"st{b}"), 16 * (tiles // 2))

        @block.gpsimd
        def _(pool):
            nc.gpsimd.memset(ones[:], 1.0).then_inc(s("ones"), 1)
            for u in segs(pool):
                b = u.s
                u.wait(pool, s("gated"), 1, 1)
                nc.gpsimd.tensor_tensor(res[:, b], res[:, b], xt[:, b], ALU.add).then_inc(s("added"), 1)
                u.wait(pool, s("added"), 1, 1)
                pool.dma_start(out[bass.ds(u.value(P, 0), P), :], res[:, b]).then_inc(s(f"st{b}"), 16)

        @block.scalar
        def _(act):
            for k in range(KD):
                act.wait_ge(s(f"raw{k % 4}"), 16 * (k // 4 + 1))
                nc.scalar.activation(wh[:, k, :], raw[:, k % 4, :], ACT.Copy).then_inc(s("w_high"), 1)
            for u in segs(act):
                b = u.s
                act.wait_ge(s(f"in{b}"), u.value(48, 48, 2))
                u.wait(act, s("g_made"), 1, 0)
                nc.scalar.activation(ge[:], g[:, b].rearrange("p k n -> p (k n)"), ACT.Exp, scale=-1.0)\
                    .then_inc(s("g_exp"), 1)
                if layer == 0:
                    u.wait(act, s("sq_sum"), 1, 0)
                    nc.scalar.activation(sq[:], o[:, b, 4:8].rearrange("p k n -> p (k n)"), ACT.Square)\
                        .then_inc(s("squared"), 1)
                    u.wait(act, s("var"), 1, 1)
                    nc.scalar.activation(nrm[:], nrm[:], ACT.Sqrt).then_inc(s("sd"), 1)
                u.wait(act, s("y_raw"), 1, 1)
                u.wait(act, s("projected"), 1, -1)
                nc.scalar.activation(yh[:, b], o[:, b], ACT.Copy).then_inc(s("y_high"), 1)

        @block.vector
        def _(dve):
            for k in range(KD):
                dve.wait_ge(s("w_high"), k + 1)
                nc.vector.tensor_tensor(wl[:, k, :], raw[:, k % 4, :], wh[:, k, :].bitcast(F32), ALU.subtract)\
                    .then_inc(s("w_split"), 1)
            per = 2 + (3 if layer == 0 else 0)

            def finish(u, last_links):
                b = u.s
                u.wait(dve, s("projected"), 1, 1)
                u.wait(dve, s(f"st{b}"), 16, 0, 2)
                sd = side(u)
                for n in range(2):
                    last = nc.vector.tensor_tensor(res[:, b, n * 512:(n + 1) * 512], PS[:, 2 * b + n, :],
                                                   gb[:, sd, n * 512:(n + 1) * 512], ALU.mult)
                last.then_inc(s("gated"), 1)

            dve.wait_ge(s("small"), 48 if layer == 0 else 32)
            for u in segs(dve):
                b = u.s
                k = [0]

                def link(ins):
                    k[0] += 1
                    ins.then_inc(s("chain"), 1)
                    u.wait(dve, s("chain"), per, k[0])

                u.wait(dve, s("g_exp"), 1, 1)
                link(nc.vector.tensor_scalar_add(ge[:], ge[:], 1.0))
                link(nc.vector.reciprocal(ge[:], ge[:]))
                gv = g[:, b].rearrange("p k n -> p (k n)")
                nc.vector.tensor_tensor(gv, gv, ge[:], ALU.mult).then_inc(s("g_made"), 1)
                ov = o[:, b].rearrange("p k n -> p (k n)")
                if layer == 0:
                    u.wait(dve, s("sq_sum"), 1, 1)
                    nc.vector.tensor_scalar(nrm[:], PS[:, 4, :], 1.0 / B_V, EPS, ALU.mult, ALU.add).then_inc(s("var"), 1)
                    u.wait(dve, s("sd"), 1, 1)
                    link(nc.vector.reciprocal(nrm[:], nrm[:]))
                    link(nc.vector.tensor_tensor(ov[:, 512:], ov[:, 512:], nrm[:], ALU.mult))
                    link(nc.vector.tensor_scalar(ov[:, 512:], ov[:, 512:], gout[:], 1.0 - LAM_INIT, ALU.mult, ALU.mult))
                u.wait(dve, s("g_made"), 1, 1)
                nc.vector.tensor_tensor(ov, ov, gv, ALU.mult).then_inc(s("y_raw"), 1)
                assert k[0] == per
                u.wait(dve, s("y_high"), 1, 1)
                nc.vector.tensor_tensor(yl[:, b].rearrange("p k n -> p (k n)"), ov,
                                        yh[:, b].rearrange("p k n -> p (k n)").bitcast(F32), ALU.subtract)\
                    .then_inc(s("y_made"), 1)
                finish(u, None)

        @block.tensor
        def _(pe):
            pe.wait_ge(s("ones"), 1)

            def sums(u):
                if layer == 0:
                    u.wait(pe, s("squared"), 1, 1)
                    u.wait(pe, s("var"), 1, 0)
                    nc.tensor.matmul(PS[:, 4, :], ones[:], sq[:], start=True, stop=True).then_inc(s("sq_sum"), 1)

            pe.wait_ge(s("w_split"), KD)
            for u in segs(pe):
                b = u.s
                sums(u)
                u.wait(pe, s("y_made"), 1, 1)
                u.wait(pe, s("gated"), 1, -1)
                for n in range(2):
                    for k in range(KD):
                        last = three_passes(nc, PS[:, 2 * b + n, :], (yh[:, b, k, :], yl[:, b, k, :]),
                                            (wh[:, k, n * 512:(n + 1) * 512], wl[:, k, n * 512:(n + 1) * 512]),
                                            k == 0, k == KD - 1)
                last.then_inc(s("projected"), 1)



def trunk(nc, A, out, debug=None):
    def scratch(name, shape, dt=F32):
        A[name] = nc.dram_tensor(name, shape, dt, kind="Internal").ap()

    for half in "hl":
        scratch("qkA" + half, (2 * A_HEADS, A_QK, TOK))
        scratch("vA" + half, (TOK, A_WIDTH))
        scratch("qkB" + half, (2, B_HEADS, P, TOK))
        scratch("vB" + half, (TOK, B_WIDTH))
        scratch("qC" + half, (C_HEADS, C_HD, LAT))
        scratch("kC" + half, (C_KV, C_HD, TOK))
        scratch("vC" + half, (TOK, C_KV * C_HD))
    scratch("tabA", (TOK, 2, 2, A_ROPE), F32)
    scratch("tabB", (TOK, 2, 2, B_D), F32)
    scratch("tabC", (TOK, 2, 2, C_HD), F32)
    scratch("cT", (3, P, TOK), F32)
    scratch("krow", (TOK, A_ROPE), F32)
    scratch("gateT0", (D, TOK), F32)
    scratch("gateT1", (D, LAT), F32)
    scratch("oT0", (D, TOK), F32)
    scratch("oT1", (D, LAT), F32)
    scratch("x1", (TOK, D), F32)
    scratch("grow", (2, 2, D), F32)
    A["x0c"], A["x0l"] = A["ctx"][0], A["x"][0]

    with ExitStack() as ctx:
        taken = []

        def sem(name):
            taken.append(nc.alloc_semaphore(name=name))
            return taken[-1]

        K = {n: ctx.enter_context(nc.sbuf_tensor("k_" + n, shape, F32)) for n, shape in
             {"idn": [P, P], "cT": [P, 16], "neglam": [P, 1], "gcol": [P, 3], "gnope": [P, 2, A_NOPE],
              "modc": [P, 2, 2, KD, 2]}.items()}
        PS = ctx.enter_context(nc.psum_tensor("psum", [P, 8, 512], F32))
        steps = [
            lambda: setup(nc, A, K, sem, PS),
            lambda: project(nc, A, K, sem, PS, 0),
            lambda: attention(nc, A, K, sem, PS, "B", 0, False),
            lambda: attention(nc, A, K, sem, PS, "B", 0, True),
            lambda: attention(nc, A, K, sem, PS, "A", 0, False),
            lambda: attention(nc, A, K, sem, PS, "A", 0, True),
            lambda: out_project(nc, A, K, sem, PS, 0, A["x1"]),
            lambda: project(nc, A, K, sem, PS, 1),
            lambda: attention(nc, A, K, sem, PS, "C", 1, False),
            lambda: out_project(nc, A, K, sem, PS, 1, out),
        ]
        for f in steps[:debug]:
            f()
            nc.clear_and_free_semaphores(taken)
            nc.all_engine_barrier()
            taken.clear()


_INS = ["x", "c", "ctx", "c_ctx", "e_norm_g", "e_w_mod", "e_b_mod", "e_w_in", "a_g_cq", "a_w_uq", "a_g_ckv",
        "a_w_ukv", "a_g_qn", "a_g_kn", "b_g_qn", "b_g_kn", "b_lam_q1", "b_lam_k1", "b_lam_q2", "b_lam_k2",
        "b_g_out", "e_w_out", "o_norm_g", "o_w_mod", "o_b_mod", "o_w_in", "c_g_qn", "c_g_kn", "o_w_out"]


def rope_table(dim):
    n = dim // 4
    inv = (np.float32(10000.0) ** (-np.arange(n, dtype=np.float32) / np.float32(n))).astype(np.float32)
    t = np.arange(LAT)
    rows, cols = (t // GRID_W).astype(np.float32), (t % GRID_W).astype(np.float32)
    ang = np.concatenate([rows[:, None] * inv, cols[:, None] * inv], axis=-1)
    ang = np.concatenate([np.zeros((CTX, dim // 2), np.float32), ang], axis=0)
    return np.stack([np.cos(ang), np.sin(ang)], axis=1).astype(np.float32)


def kernel(**inputs):
    import concourse.bacc as bacc
    from concourse.bass_utils import run_bass_kernel_spmd

    nc = bacc.Bacc("TRN2", target_bir_lowering=False, num_devices=1)
    arrays, A = {}, {}
    for name in _INS:
        a = np.ascontiguousarray(inputs[name])
        arrays[f"in_{name}"] = a
    for n, dim in (("A", A_ROPE), ("B", B_D), ("C", C_HD)):
        arrays["in_rope" + n] = rope_table(dim)
    for name, a in arrays.items():
        A[name[3:]] = nc.dram_tensor(name, a.shape, mybir.dt.from_np(a.dtype), kind="ExternalInput").ap()
    out = nc.dram_tensor("out_x", (1, LAT, D), F32, kind="ExternalOutput").ap()
    trunk(nc, A, out[0])
    r = run_bass_kernel_spmd(nc, [arrays], core_ids=[0])
    return r.results[0]["out_x"]
```

```python
from contextlib import ExitStack

import numpy as np

import concourse.bass as bass
from concourse import mybir

F32 = mybir.dt.float32
F32R = mybir.dt.float32r
ALU = mybir.AluOpType
ACT = mybir.ActivationFunctionType
AX = mybir.AxisListType.X

P = 128
D = 1024
KD = D // P
CTX = 256
LAT = 1024
TOK = CTX + LAT
NT = TOK // P
NCT = CTX // P
GRID_W = 64
EPS = 1e-6

A_HEADS, A_NOPE, A_ROPE, A_V = 8, 64, 32, 64
A_QK = A_NOPE + A_ROPE
A_Q_LORA, A_KV_LORA = 256, 128
B_HEADS, B_D, B_V = 4, 64, 128
C_HEADS, C_KV, C_HD = 8, 2, 128
A_WIDTH, B_WIDTH = A_HEADS * A_V, B_HEADS * B_V
LAM_INIT = 0.2

W0 = A_Q_LORA + A_KV_LORA + A_ROPE
E_GATE_A = W0
E_BQ = E_GATE_A + A_WIDTH
E_BK = E_BQ + 2 * B_HEADS * B_D
E_BV = E_BK + 2 * B_HEADS * B_D
E_GATE_B = E_BV + B_WIDTH
O_K = C_HEADS * C_HD
O_GATE = O_K + 2 * C_KV * C_HD
WR = 16
RAW = 5


def three_passes(nc, out, lhs, rhs, start, stop):
    nc.tensor.matmul(out, lhs[1], rhs[0], start=start, stop=False)
    nc.tensor.matmul(out, lhs[0], rhs[1], start=False, stop=False)
    return nc.tensor.matmul(out, lhs[0], rhs[0], start=False, stop=stop)


class Chain:

    def __init__(self, nc, eng, sem):
        self.nc, self.eng, self.sem, self.n = nc, eng, sem, 0

    def link(self, ins):
        ins.then_inc(self.sem, 1)
        self.n += 1
        self.eng.wait_ge(self.sem, self.n)



def setup(nc, A, K, sem, PS):
    with ExitStack() as ctx:
        def sb(name, shape, dt=F32):
            return ctx.enter_context(nc.sbuf_tensor(name, shape, dt))

        cc = sb("su_cc", [16, P])
        ce = sb("su_ce", [16, P])
        lam = sb("su_lam", [P, 4, B_D])
        lp = sb("su_lp", [P, 2, B_D])
        ls = sb("su_ls", [P, 2])
        kinds = {"A": (A_ROPE, A_QK), "B": (B_D, B_D), "C": (C_HD, C_HD)}
        gain, cs, tab = {}, {}, {}
        for n, (rd, full) in kinds.items():
            gain[n] = sb(f"su_g{n}", [P, 2, full])
            cs[n] = sb(f"su_cs{n}", [P, NT, 2, rd // 2])
            tab[n] = sb(f"su_t{n}", [P, NT, 2, 2, rd])

        s_in, s_cc, s_id, s_e, s_c, s_v, s_le, s_tab, s_st, s_p = (
            sem(n) for n in ("su_in", "su_ccin", "su_id", "su_exp", "su_silu", "su_chain", "su_lexp",
                             "su_tab", "su_stored", "su_cT"))
        block = ctx.enter_context(nc.Block())

        @block.sync
        def _(sp):
            sp.dma_start(cc[0:8, :], A["c_ctx"].rearrange("(k p) -> k p", p=P)).then_inc(s_cc, 16)
            sp.dma_start(cc[8:16, :], A["c"][0, :].rearrange("(k p) -> k p", p=P)).then_inc(s_cc, 16)
            for j, n in enumerate(("b_lam_q1", "b_lam_k1", "b_lam_q2", "b_lam_k2")):
                sp.dma_start(lam[:, j, :], A[n][0, :].partition_broadcast(P)).then_inc(s_in, 16)
            for n, (q, k) in {"A": ("a_g_qn", "a_g_kn"), "B": ("b_g_qn", "b_g_kn"),
                              "C": ("c_g_qn", "c_g_kn")}.items():
                sp.dma_start(gain[n][:, 0, :], A[q][0, :].partition_broadcast(P)).then_inc(s_in, 16)
                sp.dma_start(gain[n][:, 1, :], A[k][0, :].partition_broadcast(P)).then_inc(s_in, 16)
                sp.dma_start(cs[n][:], A["rope" + n].rearrange("(t p) a f -> p t a f", p=P)).then_inc(s_in, 16)
            sp.dma_start(K["gcol"][:, 0:2], A["a_g_cq"][0, :].rearrange("(k p) -> p k", p=P),
                         allow_slow_non_contiguous=True).then_inc(s_in, 16)
            sp.dma_start(K["gcol"][:, 2:3], A["a_g_ckv"][0, :].rearrange("(k p) -> p k", p=P),
                         allow_slow_non_contiguous=True).then_inc(s_in, 16)
            for i, n in enumerate("ABC"):
                sp.wait_ge(s_tab, i + 1)
                sp.dma_start(A["tab" + n].rearrange("(t p) q a f -> p t q a f", p=P), tab[n][:]).then_inc(s_st, 16)
            sp.wait_ge(s_st, 48)

        @block.gpsimd
        def _(pool):
            nc.gpsimd.memset(K["idn"][:], 0.0).then_inc(s_id, 1)
            pool.wait_ge(s_id, 1)
            nc.gpsimd.affine_select(out=K["idn"][:], in_=K["idn"][:], compare_op=ALU.not_equal, fill=1.0,
                                    base=0, pattern=[[-1, P]], channel_multiplier=1).then_inc(s_id, 1)

        @block.scalar
        def _(act):
            act.wait_ge(s_cc, 32)
            nc.scalar.activation(ce[:], cc[:], ACT.Exp, scale=-1.0).then_inc(s_e, 1)
            act.wait_ge(s_v, 5)
            nc.scalar.activation(ls[:], ls[:], ACT.Exp).then_inc(s_le, 1)

        @block.tensor
        def _(pe):
            pe.wait_ge(s_id, 2)
            pe.wait_ge(s_c, 1)
            nc.tensor.transpose(PS[:, 0, 0:16], cc[:], K["idn"][0:16, 0:16]).then_inc(s_p, 1)

        @block.vector
        def _(dve):
            ch = Chain(nc, dve, s_v)
            dve.wait_ge(s_e, 1)
            ch.link(nc.vector.tensor_scalar_add(ce[:], ce[:], 1.0))
            ch.link(nc.vector.reciprocal(ce[:], ce[:]))
            nc.vector.tensor_tensor(cc[:], cc[:], ce[:], ALU.mult).then_inc(s_c, 1)
            dve.wait_ge(s_in, 16 * 15)
            for j in range(2):
                ch.link(nc.vector.tensor_tensor(lp[:, j, :], lam[:, 2 * j, :], lam[:, 2 * j + 1, :], ALU.mult))
            ch.link(nc.vector.tensor_reduce(ls[:], lp[:], AX, ALU.add))
            dve.wait_ge(s_le, 1)
            ch.link(nc.vector.tensor_tensor(K["neglam"][:], ls[:, 1:2], ls[:, 0:1], ALU.subtract))
            nc.vector.tensor_scalar_add(K["neglam"][:], K["neglam"][:], -LAM_INIT)
            for n, (rd, full) in kinds.items():
                ch.link(nc.vector.tensor_scalar_mul(gain[n][:, 0, :], gain[n][:, 0, :], float(full) ** -0.5))
                for q in range(2):
                    for a in range(2):
                        for half in range(2):
                            o = full - rd + half * rd // 2
                            g = gain[n][:, q, o:o + rd // 2].unsqueeze(1).to_broadcast([P, NT, rd // 2])
                            last = nc.vector.tensor_tensor(tab[n][:, :, q, a, half * rd // 2:(half + 1) * rd // 2],
                                                           cs[n][:, :, a, :], g, ALU.mult)
                last.then_inc(s_tab, 1)
            nc.vector.tensor_copy(K["gnope"][:], gain["A"][:, :, 0:A_NOPE])
            dve.wait_ge(s_p, 1)
            nc.vector.tensor_copy(K["cT"][:], PS[:, 0, 0:16])



def plan_project(layer):
    jobs = []

    def norm(t):
        jobs.extend([("hT", t, 0), ("hT", t, 1)])

    if layer == 0:
        jobs += [("mod", 0, 0), ("mconst",), ("mod", 0, 1), ("modT", 0, 0), ("mod", 0, 2), ("modT", 0, 1),
                 ("mod", 0, 3), ("modT", 0, 2), ("modT", 0, 3)]
    norm(0)
    norm(1)
    first = "c0" if layer == 0 else "kv"
    for t in range(NT):
        if t + 2 < NT:
            norm(t + 2)
        jobs.append(("row", first, t))
        if t:
            jobs.append(("rowT", first, t - 1))
    jobs.append(("rowT", first, NT - 1))
    if layer == 0:
        chunks = ("bq", "bk")
        tiles = range(NT)
        mods = {("bq", 1): (0, 4), ("bq", 4): (0, 5), ("bq", 7): (1, 0), ("bk", 0): (1, 1), ("bk", 3): (1, 2),
                ("bk", 6): (1, 3), ("bv", 0): (1, 4), ("bv", 4): (1, 5)}
    else:
        chunks = ("q0", "q1")
        tiles = range(NCT, NT)
        mods = {}
    prev = late = None
    for c in chunks + (("bv",) if layer == 0 else ()):
        for t in tiles:
            jobs.append(("v" if c == "bv" else "row", c, t))
            if prev:
                jobs.append(("rowT",) + prev)
            prev = None if c == "bv" else (c, t)
            if late:
                jobs.append(("modT",) + late)
            late = mods.get((c, t))
            if late:
                jobs.append(("mod",) + late)
    if prev:
        jobs.append(("rowT",) + prev)
    groups = [(0, 512), (512, 512), (1024, 256)] if layer == 0 else [(256, 512), (768, 512)]
    ga, gb = [[("gate", c, j, a, n) for j in range(4) for a, n in groups] for c in ("ga", "gb")]
    if layer == 1:
        return jobs + ga + gb
    jobs += ga[:3]
    fill = [ga[3:6], ga[6:8], ga[8:10], ga[10:12], [], gb[0:3], gb[3:6], gb[6:8], gb[8:10], gb[10:12]]
    prev = None
    for t in range(NT):
        gates = fill[t]
        jobs += [("row", "uq", t, 0), ("row", "uq", t, 1)] + gates[:1]
        if prev is not None:
            jobs += [("rowT", "uk", prev, 0), ("rowT", "uk", prev, 1)]
        jobs += [("row", "uk", t, 0), ("row", "uk", t, 1)] + gates[1:]
        jobs += [("rowT", "uq", t, 0), ("rowT", "uq", t, 1)]
        prev = t
    jobs += [("rowT", "uk", prev, 0), ("rowT", "uk", prev, 1)]
    return jobs


ITEMS = {"bq": (8, 64, 64, 0), "bk": (8, 64, 64, 1), "uq": (8, 96, 32, 0), "uk": (8, 96, 32, 1),
         "q0": (4, 128, 128, 0), "q1": (4, 128, 128, 0), "kv": (2, 128, 128, 1), "c0": (2, 0, 0, 0)}
TABLE = {"b": "tabB", "u": "tabA", "q": "tabC", "k": "tabC"}


def project(nc, A, K, sem, PS, layer):
    jobs = plan_project(layer)
    L = f"p{layer}_"
    ordinal, done_by = {}, {}
    for i, job in enumerate(jobs):
        ordinal[job] = i
    free_name = {"mod": "modrow", "modT": "modcol", "mconst": "modcol", "hT": "h_evac", "v": "e_done", "gate": "gate_out"}
    counts = {}

    def free_of(job):
        kind = job[0]
        if kind == "row":
            if job[1] == "c0":
                return "x_in"
            return "e_done" if job[1] in ("kv", "uk") else "x_in"
        if kind == "rowT":
            return "cq_out" if job[1] == "c0" else "e_done"
        return free_name[kind]

    for i, job in enumerate(jobs):
        n = free_of(job)
        counts[n] = counts.get(n, 0) + 1
        done_by[job] = (n, counts[n])
    order_e = [j for j in jobs if free_of(j) == "e_done"]
    items = []
    for j in jobs:
        if j[0] == "row" and (j[1], j[2]) not in items:
            items.append((j[1], j[2]))
    item_no = {it: i for i, it in enumerate(items)}
    e_no = {j: i for i, j in enumerate(order_e)}
    gs_jobs = [j for j in jobs if j[0] == "gate" or (j[0] == "rowT" and j[1] == "c0")]
    gs_no = {j: i for i, j in enumerate(gs_jobs)}

    w_in = A["e_w_in"] if layer == 0 else A["o_w_in"]
    if layer == 0:
        cols = {"c0": (0, W0), "bq": (E_BQ, 512), "bk": (E_BK, 512), "bv": (E_BV, 512),
                "ga": (E_GATE_A, 512), "gb": (E_GATE_B, 512)}
        chunk_order = ["c0", "bq", "bk", "bv", "ga", "u", "gb"]
    else:
        cols = {"kv": (O_K, 512), "q0": (0, 512), "q1": (512, 512), "ga": (O_GATE, 512), "gb": (O_GATE + 512, 512)}
        chunk_order = ["kv", "q0", "q1", "ga", "gb"]
    pieces, piece_of = [], {}
    for c in chunk_order:
        if c == "u":
            srcs = [(A["a_w_uq"][0, k * P:(k + 1) * P, h * 384:(h + 1) * 384], 384) for k in range(2) for h in range(2)]
            srcs += [(A["a_w_ukv"][0, :, h * 512:(h + 1) * 512], 512) for h in range(2)]
        else:
            o, n = cols[c]
            srcs = [(w_in[0, k * P:(k + 1) * P, o:o + n], n) for k in range(KD)]
        for k, s in enumerate(srcs):
            piece_of[c, k] = len(pieces)
            pieces.append(s)
    mods = [("mod", l, j) for (k, l, j) in [x for x in jobs if x[0] == "mod"]]

    split_at = {}
    pos = {}
    for i, j in enumerate(jobs):
        if j[0] in ("row", "v", "gate"):
            pos.setdefault(j[1], []).append(j)
    seq = ["c0", "bq", "bk", "bv", "ga"] if layer == 0 else ["kv", "q0", "q1", "ga"]
    nxt = {"c0": ["bq"], "bq": ["bk"], "bk": ["bv"], "bv": ["ga"], "ga": ["u", "gb"]} if layer == 0 else \
        {"kv": ["q0"], "q0": ["q1"], "q1": ["ga"], "ga": ["gb"]}
    for c in seq:
        want = [p for n in nxt[c] for p in range(piece_of[n, 0], piece_of[n, 0] + (6 if n == "u" else KD))]
        at = pos[c]
        for k, p in enumerate(want):
            if layer == 0 and c == "ga":
                split_at.setdefault(at[0 if k < 6 else 1 if k < 8 else -1], []).append(p)
            else:
                split_at.setdefault(at[min(k, len(at) - 1)], []).append(p)

    raws = []

    def chunk_raws(c):
        return [("w", piece_of[c, k]) for k in range(6 if c == "u" else KD)]

    def mod_raws(js):
        return [("m", j, k) for j in js for k in range(KD)]

    first_mods = [j for j in jobs[:9] if j[0] == "mod"]
    w, m = chunk_raws(chunk_order[0]), mod_raws(first_mods)
    if m:
        for i, x in enumerate(m):
            raws.append(x)
            if i % 4 == 1:
                raws.append(w[i // 4])
    else:
        raws += w
    mod_at = {}
    for i, j in enumerate(jobs):
        if j[0] == "mod":
            for k in range(KD):
                mod_at.setdefault(i if j in first_mods else i - max(0, 4 - k // 2 - k // 7), []).append((j, k))
    raw_position = [jobs.index(x[1]) if x[0] == "m" else 0 for x in raws]
    for i, j in enumerate(jobs):
        raws += [("w", p) for p in split_at.get(j, ())]
        raws += [("m",) + x for x in mod_at.get(i, ()) if x[0] not in first_mods]
        raw_position += [i] * (len(raws) - len(raw_position))
    raw_no = {r: i for i, r in enumerate(raws)}
    m_no = {r: i for i, r in enumerate([r for r in raws if r[0] == "m" and r[2] < KD - 1])}
    w_order = [r[1] for r in raws if r[0] == "w"]
    assert w_order == sorted(w_order)

    def raw_landed(r):
        i = raw_no[r]
        return f"raw{i % RAW}", 16 * (i // RAW + 1)

    chunk_of = {p: c for (c, _), p in piece_of.items()}

    with ExitStack() as ctx:
        def sb(name, shape, dt=F32):
            return ctx.enter_context(nc.sbuf_tensor(L + name, shape, dt))

        hh = sb("hT_hi", [P, KD, TOK], F32R)
        hl = sb("hT_lo", [P, KD, TOK], F32R)
        wh = sb("w_hi", [P, WR, 512], F32R)
        wl = sb("w_lo", [P, WR, 512], F32R)
        raw = sb("raw", [P, RAW, 512])
        X = sb("x_rows", [P, 2, 768])
        SQ = sb("squares", [P, 768])
        junk = sb("junk", [P, D], mybir.dt.bfloat16)
        Y = sb("y_rows", [P, 2, 768])
        U = sb("rope_u", [P, 512])
        V = sb("rope_v", [P, 512])
        eh = sb("e_hi", [P, 2, 512], F32R)
        el = sb("e_lo", [P, 2, 512], F32R)
        gs = sb("gate_rows", [P, 2, 512])
        tb = sb("table", [P, 2, 256])
        st = sb("stats", [P, 2, 4, 8])
        ssx = sb("x_stats", [P, 2, 4])
        if layer == 0:
            mrow = sb("mod_row", [2, 512])
            mcol = sb("mod_gate", [P, 4, 2])
            mrows = sb("mod_rows", [8 * KD, P])
            mconst = sb("mod_const", [P, 2, 4 * KD])
            mbias, mgain = mconst[:, :, 0:3 * KD], mconst[:, :, 3 * KD:]
            with nc.sbuf_tensor(L + "x_tiles", [P, 2, D], F32) as xt:
                pass
            cl = sb("c_in", [P, 2, 384])
            chh = sb("c_hi", [P, 2, 384], F32R)
            cll = sb("c_lo", [P, 2, 384], F32R)
            kr = sb("kr_in", [P, 4, A_ROPE])
            tmpv = Y[:].rearrange("p a b -> p (a b)")[:, 0:D]
        else:
            xt = sb("x_tiles", [P, 2, D])
            tmpv = sb("modulated", [P, D])[:]

        S = {}

        def s(name):
            if name not in S:
                S[name] = sem(L + name)
            return S[name]

        block = ctx.enter_context(nc.Block())

        def free_wait(eng, i):
            if i >= 8:
                n, v = done_by[jobs[i - 8]]
                if n == "x_in":
                    v = x_in_value[jobs[i - 8]]
                eng.wait_ge(s(n), v)

        x_in_value, k = {}, 0
        for j in jobs:
            if j[0] == "row":
                k += 1
                x_in_value[j] = k
        last_piece = {}
        for j in jobs:
            if j[0] == "row":
                last_piece[j[1], j[2]] = x_in_value[j]

        c_split_at, c_load_at = {}, {}
        if layer == 0:
            last_ga = [j for j in jobs if j[0] == "gate" and j[1] == "ga"]
            c_load_at[last_ga[0]] = 0
            c_load_at[last_ga[1]] = 1
            c_split_at[last_ga[1]] = 0
            c_split_at[last_ga[2]] = 1
            c_load_at[last_ga[2]] = 2
            for t in range(NT - 2):
                c_split_at["row", "uk", t, 1] = t + 2
                if t + 3 < NT:
                    c_load_at["row", "uk", t, 1] = t + 3

        tab_no, y_user, per_slot = {}, {}, [0, 0]
        rope_items = [it for it in items if it[0] != "c0"]
        for it in rope_items:
            b = item_no[it] % 2
            per_slot[b] += 1
            tab_no[it] = per_slot[b]
        last_T = {}
        for j in jobs:
            if j[0] == "rowT" and j[1] != "c0":
                last_T[j[1], j[2]] = ordinal[j]
        for it in rope_items:
            r = item_no[it]
            if r >= 2 and items[r - 2] in last_T:
                y_user[r] = last_T[items[r - 2]]

        def store_of(j, t_ap, half):
            kind, c, t = j[:3]
            tok = slice(t * P, (t + 1) * P)
            if kind == "v":
                return [(A["vB" + half][tok, :], t_ap)]
            if kind == "row" and c == "uk":
                return [(A["vA" + half][tok, j[3] * 256:(j[3] + 1) * 256], t_ap[:, 0:256])]
            if kind == "row" and c == "kv":
                return [(A["vC" + half][tok, :], t_ap[:, 0:256])]
            v = t_ap.rearrange("p (h n) -> p h n", h=4)
            if c in ("uq", "uk"):
                u = (0 if c == "uq" else 8) + 4 * j[3]
                return [(A["qkA" + half][u:u + 4, :, tok].rearrange("h p n -> p h n"), v[0:A_QK])]
            if c in ("bq", "bk"):
                return [(A["qkB" + half][0 if c == "bq" else 1, :, :, tok].rearrange("h p n -> p h n"), v)]
            if c in ("q0", "q1"):
                u = 0 if c == "q0" else 4
                tk = slice((t - NCT) * P, (t - NCT + 1) * P)
                return [(A["qC" + half][u:u + 4, :, tk].rearrange("h p n -> p h n"), v)]
            return [(A["kC" + half][:, :, tok].rearrange("h p n -> p h n"), v[:, 0:2, :])]

        def e_free(eng, e):
            if e >= 2:
                eng.wait_ge(s(f"e_st{e % 2}"), 32 * (e // 2))

        def g_free(eng, g):
            if g >= 2:
                eng.wait_ge(s(f"g_st{g % 2}"), 16 * (g // 2))

        def row_slot_free(eng, r):
            if r >= 2:
                c, t = items[r - 2]
                eng.wait_ge(s("y_ready"), r - 1)
                if c == "c0":
                    eng.wait_ge(s("job"), ordinal["rowT", "c0", t] + 1)
                    eng.wait_ge(s(f"kr_st{t % 2}"), 16 * (t // 2 + 1))

        def load_mod_rows(act):
            for l, n in enumerate("eo"):
                for o, src in ((0, A[n + "_b_mod"]), (3 * KD, A[n + "_norm_g"])):
                    act.dma_start(mrows[4 * KD * l + o:4 * KD * l + o + src.shape[1] // P, :],
                                  src[0, :].rearrange("(k p) -> k p", p=P)).then_inc(s("mbg"), 16)

        def load_table(act, c, t, r):
            n, qk, rd = TABLE[c[0]], ITEMS[c][3], ITEMS[c][2]
            act.dma_start(tb[:, r % 2, 0:2 * rd], A[n][t * P:(t + 1) * P, qk, :, :].rearrange("p a f -> p (a f)"))\
                .then_inc(s(f"tab{r % 2}"), 16)

        def load_c(act, t):
            if t == 0:
                for b in range(2):
                    act.wait_ge(s(f"g_st{b}"), 16 * (NT // 2))
                for b in range(2):
                    act.wait_ge(s(f"kr_st{b}"), 16 * NT // 2)
            if t >= 2:
                act.wait_ge(s("c_split"), t - 1)
            if t >= 4:
                act.wait_ge(s("x_in"), x_in_value["row", "uk", t - 4, 1])
            act.dma_start(cl[:, t % 2, :].rearrange("p (k n) -> p k n", k=3),
                          A["cT"][:, :, t * P:(t + 1) * P].rearrange("k p n -> p k n")).then_inc(s(f"c_in{t % 2}"), 16)
            act.dma_start(kr[:, t % 4, :], A["krow"][t * P:(t + 1) * P, :]).then_inc(s(f"c_in{t % 2}"), 16)

        def x_stats(dve, ch, t):
            b = t % 2
            dve.wait_ge(s("xss"), t + 1)
            nc.vector.tensor_scalar(ssx[:, b, 1:2], ssx[:, b, 0:1], 1.0 / D, EPS, ALU.mult, ALU.add)\
                .then_inc(s("xvar"), 1)
            dve.wait_ge(s("xsd"), t + 1)
            nc.vector.reciprocal(ssx[:, b, 3:4], ssx[:, b, 2:3]).then_inc(s("xrs"), 1)

        def row_norm(dve, ch, c, t, r):
            nh, hd, rd, qk = ITEMS[c]
            b = r % 2
            x, q, y = X[:, b, :], SQ[:], Y[:, b, :]
            dve.wait_ge(s("x_in"), last_piece[c, t])
            if c == "c0":
                nc.vector.tensor_reduce(st[:, b, 0, 0:1], q[:, 0:256], AX, ALU.add)
                ch.link(nc.vector.tensor_reduce(st[:, b, 0, 1:2], q[:, 256:384], AX, ALU.add))
                nc.vector.tensor_scalar(st[:, b, 1, 0:1], st[:, b, 0, 0:1], 1.0 / A_Q_LORA, EPS, ALU.mult, ALU.add)
                nc.vector.tensor_scalar(st[:, b, 1, 1:2], st[:, b, 0, 1:2], 1.0 / A_KV_LORA, EPS, ALU.mult, ALU.add)\
                    .then_inc(s("var"), 1)
                dve.wait_ge(s("sd"), r + 1)
                ch.link(nc.vector.reciprocal(st[:, b, 3, 0:2], st[:, b, 2, 0:2]))
                nc.vector.tensor_scalar(x[:, 0:256], x[:, 0:256], st[:, b, 3, 0:1], None, ALU.mult)
                nc.vector.tensor_scalar(x[:, 256:384], x[:, 256:384], st[:, b, 3, 1:2], None, ALU.mult)\
                    .then_inc(s("y_ready"), 1)
                return
            w = nh * hd
            x3 = x[:, 0:w].rearrange("p (h n) -> p h n", h=nh)
            y3 = y[:, 0:w].rearrange("p (h n) -> p h n", h=nh)
            q3 = q[:, 0:w].rearrange("p (h n) -> p h n", h=nh)
            ch.link(nc.vector.tensor_reduce(st[:, b, 0, 0:nh], q3, AX, ALU.add))
            nc.vector.tensor_scalar(st[:, b, 1, 0:nh], st[:, b, 0, 0:nh], 1.0 / hd, EPS, ALU.mult, ALU.add)\
                .then_inc(s("var"), 1)
            dve.wait_ge(s("sd"), r + 1)
            ch.link(nc.vector.reciprocal(st[:, b, 3, 0:nh], st[:, b, 2, 0:nh]))
            ch.link(nc.vector.tensor_tensor(x3, x3, st[:, b, 3, 0:nh].unsqueeze(2).to_broadcast([P, nh, hd]), ALU.mult))
            dve.wait_ge(s(f"tab{b}"), 16 * tab_no[c, t])
            prev = y_user.get(r)
            if prev is not None:
                dve.wait_ge(s("job"), prev + 1)
            o, h2 = hd - rd, rd // 2
            tv = tb[:, b, 0:2 * rd].rearrange("p (a f) -> p a f", a=2)
            u3 = U[:, 0:nh * rd].rearrange("p (h n) -> p h n", h=nh)
            v3 = V[:, 0:nh * rd].rearrange("p (h n) -> p h n", h=nh)
            if o:
                nc.vector.tensor_tensor(y3[:, :, 0:o], x3[:, :, 0:o],
                                        K["gnope"][:, qk, :].unsqueeze(1).to_broadcast([P, nh, o]), ALU.mult)
            nc.vector.tensor_tensor(u3, x3[:, :, o:], tv[:, 0, :].unsqueeze(1).to_broadcast([P, nh, rd]), ALU.mult)
            ch.link(nc.vector.tensor_tensor(v3, x3[:, :, o:], tv[:, 1, :].unsqueeze(1).to_broadcast([P, nh, rd]), ALU.mult))
            nc.vector.tensor_tensor(y3[:, :, o:o + h2], u3[:, :, 0:h2], v3[:, :, h2:rd], ALU.subtract)
            nc.vector.tensor_tensor(y3[:, :, o + h2:], u3[:, :, h2:rd], v3[:, :, 0:h2], ALU.add)\
                .then_inc(s("y_ready"), 1)

        @block.sync
        def _(sp):
            def load_raw(i, r):
                if i >= RAW:
                    o = raws[i - RAW]
                    if o[0] == "w":
                        sp.wait_ge(s("w_split"), o[1] + 1)
                    elif o[2] < KD - 1:
                        sp.wait_ge(s("m_used"), m_no[o] + 1)
                    else:
                        sp.wait_ge(s("job"), ordinal[o[1]] + 1)
                if r[0] == "w":
                    src, n = pieces[r[1]]
                else:
                    _, (_, l, j), k = r
                    wm = A["e_w_mod"] if l == 0 else A["o_w_mod"]
                    src, n = wm[0, k * P:(k + 1) * P, j * 512:(j + 1) * 512], 512
                sp.dma_start(raw[:, i % RAW, 0:n], src).then_inc(s(raw_landed(r)[0]), 16)

            def store(j):
                if j in e_no:
                    e = e_no[j]
                    sp.wait_ge(s("e_done"), e + 1)
                    for src, name in ((eh, "h"), (el, "l")):
                        for dst, sap in store_of(j, src[:, e % 2, :], name):
                            sp.dma_start(dst, sap.bitcast(F32)).then_inc(s(f"e_st{e % 2}"), 16)
                if j in gs_no:
                    g = gs_no[j]
                    n, v = done_by[j]
                    sp.wait_ge(s(n), v)
                    if j[0] == "gate":
                        _, c, jj, a, n = j
                        row = (0 if c == "ga" else 512) + jj * P
                        a0 = a if layer == 0 else a - CTX
                        sp.dma_start(A[f"gateT{layer}"][row:row + P, a0:a0 + n], gs[:, g % 2, 0:n])\
                            .then_inc(s(f"g_st{g % 2}"), 16)
                    else:
                        t = j[2]
                        sp.dma_start(A["cT"][:, :, t * P:(t + 1) * P].rearrange("k p n -> p k n"),
                                     gs[:, g % 2, 0:384].rearrange("p (k n) -> p k n", k=3))\
                            .then_inc(s(f"g_st{g % 2}"), 16)
                if j[0] == "row" and j[1] == "c0":
                    t = j[2]
                    sp.wait_ge(s("x_in"), x_in_value[j])
                    sp.dma_start(A["krow"][t * P:(t + 1) * P, :], X[:, item_no["c0", t] % 2, 384:416])\
                        .then_inc(s(f"kr_st{t % 2}"), 16)
                if j[0] == "modT" and j[2] >= 4:
                    n, v = done_by[j]
                    sp.wait_ge(s(n), v)
                    for side in range(2):
                        sp.dma_start(A["grow"][j[1], side, (j[2] - 4) * 512:(j[2] - 3) * 512]
                                     .rearrange("(k p) -> p k", p=P), mcol[:, :, side],
                                     allow_slow_non_contiguous=True).then_inc(s("grow_st"), 16)

            n = 0
            for i, j in enumerate(jobs):
                while n < len(raws) and raw_position[n] <= i + 2:
                    load_raw(n, raws[n])
                    n += 1
                store(j)
            assert n == len(raws)
            for b in range(2):
                sp.wait_ge(s(f"e_st{b}"), 32 * len(order_e[b::2]))
                sp.wait_ge(s(f"g_st{b}"), 16 * len(gs_jobs[b::2]))
            if layer == 0:
                for b in range(2):
                    sp.wait_ge(s(f"kr_st{b}"), 16 * NT // 2)
                sp.wait_ge(s("grow_st"), 32 * 4)

        @block.gpsimd
        def _(pool):
            def split(p):
                name, v = raw_landed(("w", p))
                pool.wait_ge(s(name), v)
                if p >= WR:
                    pool.wait_ge(s("job"), ordinal[pos[chunk_of[p - WR]][-1]] + 1)
                n = pieces[p][1]
                src = raw[:, raw_no["w", p] % RAW, 0:n]
                nc.gpsimd.tensor_scalar(wh[:, p % WR, 0:n], src, 1.0, 1.0, ALU.mult, ALU.mult)\
                    .then_inc(s("w_high"), 1)
                pool.wait_ge(s("w_high"), p + 1)
                nc.gpsimd.tensor_tensor(wl[:, p % WR, 0:n], src, wh[:, p % WR, 0:n].bitcast(F32),
                                        ALU.subtract).then_inc(s("w_split"), 1)

            for p in chunk_raws(chunk_order[0]):
                split(p[1])
            for j in jobs:
                for p in split_at.get(j, ()):
                    split(p)

        @block.scalar
        def _(act):
            def load_x(t):
                if t >= 2:
                    act.wait_ge(s("job"), ordinal["hT", t - 2, 1] + 1)
                src = (A["x0c"][t * P:(t + 1) * P, :] if t < NCT else A["x0l"][(t - NCT) * P:(t - NCT + 1) * P, :]) \
                    if layer == 0 else A["x1"][t * P:(t + 1) * P, :]
                act.dma_start(xt[:, t % 2, :], src).then_inc(s(f"xt{t % 2}"), 16)

            def norm_x(t):
                act.wait_ge(s(f"xt{t % 2}"), 16 * (t // 2 + 1))
                nc.scalar.activation(junk[:], xt[:, t % 2, :], ACT.Square, accum_out=ssx[:, t % 2, 0:1]).then_inc(s("xss"), 1)
                act.wait_ge(s("xvar"), t + 1)
                nc.scalar.activation(ssx[:, t % 2, 2:3], ssx[:, t % 2, 1:2], ACT.Sqrt).then_inc(s("xsd"), 1)
                act.wait_ge(s("xrs"), t + 1)
                nc.scalar.activation(xt[:, t % 2, :], xt[:, t % 2, :], ACT.Copy, scale=ssx[:, t % 2, 3:4])\
                    .then_inc(s("xn"), 1)

            load_x(0)
            load_x(1)
            if layer == 0:
                load_mod_rows(act)
            norm_x(0)
            norm_x(1)
            for j in jobs:
                i = ordinal[j]
                bank = PS[:, i % 8, :]
                if j[0] == "hT":
                    _, t, half = j
                    if half == 0 and t + 2 < NT:
                        load_x(t + 2)
                    act.wait_ge(s("h_evac"), 2 * t + half + 1)
                    dst = hh[:, 4 * half:4 * half + 4, t * P:(t + 1) * P]
                    nc.scalar.activation(dst, tmpv[:, half * 512:(half + 1) * 512].rearrange("p (k n) -> p k n", k=4),
                                         ACT.Copy).then_inc(s("h_high"), 1)
                    if half == 1 and t + 2 < NT:
                        norm_x(t + 2)
                elif j[0] == "row":
                    c, t = j[1], j[2]
                    r = item_no[c, t]
                    nh, hd, rd, _ = ITEMS[c]
                    piece = j[3] if len(j) > 3 else 0
                    if piece == 0:
                        row_slot_free(act, r)
                        if c != "c0":
                            load_table(act, c, t, r)
                    x, q = X[:, r % 2, :], SQ[:]
                    act.wait_ge(s("job"), i + 1)
                    if c == "c0":
                        nc.scalar.activation(q[:, 0:384], bank[:, 0:384], ACT.Square)
                        nc.scalar.activation(x[:, 0:W0], bank[:, 0:W0], ACT.Copy).then_inc(s("x_in"), 1)
                    elif c == "uk":
                        kvv = bank.rearrange("p (h n) -> p h n", h=4)
                        xk = x.rearrange("p (h n) -> p h n", h=8)[:, 4 * piece:4 * piece + 4, :]
                        qk = q.rearrange("p (h n) -> p h n", h=8)[:, 4 * piece:4 * piece + 4, :]
                        krb = kr[:, t % 4, :].unsqueeze(1).to_broadcast([P, 4, A_ROPE])
                        nc.scalar.activation(qk[:, :, 0:A_NOPE], kvv[:, :, 0:A_NOPE], ACT.Square)
                        nc.scalar.activation(qk[:, :, A_NOPE:], krb, ACT.Square)
                        nc.scalar.activation(xk[:, :, 0:A_NOPE], kvv[:, :, 0:A_NOPE], ACT.Copy)
                        nc.scalar.activation(xk[:, :, A_NOPE:], krb, ACT.Copy).then_inc(s("x_in"), 1)
                        e = e_no[j]
                        e_free(act, e)
                        nc.scalar.activation(eh[:, e % 2, 0:256].rearrange("p (h n) -> p h n", h=4),
                                             kvv[:, :, A_NOPE:], ACT.Copy).then_inc(s("e_high"), 1)
                    else:
                        n = 384 if c == "uq" else nh * hd
                        o = piece * 384
                        nc.scalar.activation(q[:, o:o + n], bank[:, 0:n], ACT.Square)
                        nc.scalar.activation(x[:, o:o + n], bank[:, 0:n], ACT.Copy).then_inc(s("x_in"), 1)
                        if c == "kv":
                            e = e_no[j]
                            e_free(act, e)
                            nc.scalar.activation(eh[:, e % 2, 0:256], bank[:, 256:512], ACT.Copy)\
                                .then_inc(s("e_high"), 1)
                    if x_in_value[j] == last_piece[c, t]:
                        act.wait_ge(s("var"), r + 1)
                        nc.scalar.activation(st[:, r % 2, 2, 0:nh], st[:, r % 2, 1, 0:nh], ACT.Sqrt)\
                            .then_inc(s("sd"), 1)
                elif j[0] in ("v", "rowT") and j in e_no:
                    e = e_no[j]
                    act.wait_ge(s("job"), i + 1)
                    e_free(act, e)
                    rows, n = (A_QK, 512) if j[1] in ("uq", "uk") else (P, 256 if j[1] == "kv" else 512)
                    nc.scalar.activation(eh[0:rows, e % 2, 0:n], bank[0:rows, 0:n], ACT.Copy).then_inc(s("e_high"), 1)
                elif j[0] == "gate":
                    g = gs_no[j]
                    n = j[4]
                    act.wait_ge(s("job"), i + 1)
                    g_free(act, g)
                    nc.scalar.activation(gs[:, g % 2, 0:n], bank[:, 0:n], ACT.Copy).then_inc(s("gate_out"), 1)
                if layer == 0:
                    t = c_split_at.get(j)
                    if t is not None:
                        act.wait_ge(s(f"c_in{t % 2}"), 32 * (t // 2 + 1))
                        if t >= 2:
                            act.wait_ge(s("job"), ordinal["row", "uk", t - 2, 1] + 1)
                        nc.scalar.activation(chh[:, t % 2, :], cl[:, t % 2, :], ACT.Copy).then_inc(s("c_high"), 1)
                    t = c_load_at.get(j)
                    if t is not None:
                        load_c(act, t)

        @block.vector
        def _(dve):
            ch = Chain(nc, dve, s("chain"))
            x_stats(dve, ch, 0)
            x_stats(dve, ch, 1)
            for j in jobs:
                i = ordinal[j]
                bank = PS[:, i % 8, :]
                if j[0] == "mconst":
                    dve.wait_ge(s("job"), i + 1)
                    nc.vector.tensor_copy(mconst[:].rearrange("p l k -> p (l k)"), bank[:, 0:8 * KD])\
                        .then_inc(s("modcol"), 1)
                elif j[0] == "mod":
                    dve.wait_ge(s("job"), i + 1)
                    if mods.index(j):
                        dve.wait_ge(s("job"), ordinal[("modT",) + mods[mods.index(j) - 1][1:]] + 1)
                    nc.vector.tensor_copy(mrow[:], bank[0:2, :]).then_inc(s("modrow"), 1)
                elif j[0] == "modT":
                    _, l, jj = j
                    if jj == 0 and l == 0:
                        dve.wait_ge(s("modcol"), 1)
                    dve.wait_ge(s("job"), i + 1)
                    cols4 = bank[:, 0:8].rearrange("p (k a) -> p k a", a=2)
                    bias = mbias[:, l, 4 * jj:4 * jj + 4].unsqueeze(2).to_broadcast([P, 4, 2])
                    k0 = 4 * (jj % 2)
                    if jj < 4:
                        dst = K["modc"][:, l, jj // 2, k0:k0 + 4, :]
                    else:
                        dst = mcol[:]
                        before = len([x for x in mods[:mods.index(("mod", l, jj))] if x[2] >= 4])
                        if before:
                            dve.wait_ge(s("grow_st"), 32 * before)
                    last = nc.vector.tensor_tensor(dst, cols4, bias, ALU.add)
                    if jj in (2, 3):
                        ch.link(last)
                        last = nc.vector.scalar_tensor_tensor(dst, dst, 1.0, mgain[:, l, k0:k0 + 4].unsqueeze(2)
                                                              .to_broadcast([P, 4, 2]), ALU.add, ALU.mult)
                    last.then_inc(s("modcol"), 1)
                elif j[0] == "hT":
                    _, t, half = j
                    side = 0 if t < NCT else 1
                    if t == 0 and layer == 0:
                        dve.wait_ge(s("modcol"), 5)
                    if t:
                        dve.wait_ge(s("h_low"), 2 * (t - 1) + half + 1)
                    dve.wait_ge(s("job"), i + 1)
                    for k in range(4):
                        kt = 4 * half + k
                        last = nc.vector.tensor_scalar(tmpv[:, kt * P:(kt + 1) * P], bank[:, k * P:(k + 1) * P],
                                                       K["modc"][:, layer, 1, kt, side:side + 1],
                                                       K["modc"][:, layer, 0, kt, side:side + 1], ALU.mult, ALU.add)
                    last.then_inc(s("h_evac"), 1)
                    if half == 1:
                        for b in range(2):
                            dve.wait_ge(s("h_high"), 2 * t + b + 1)
                            hs = (slice(None), slice(4 * b, 4 * b + 4), slice(t * P, (t + 1) * P))
                            nc.vector.tensor_tensor(hl[hs], tmpv[:, b * 512:(b + 1) * 512].rearrange("p (k n) -> p k n", k=4),
                                                    hh[hs].bitcast(F32), ALU.subtract).then_inc(s("h_low"), 1)
                        if t + 2 < NT:
                            x_stats(dve, ch, t + 2)
                elif j[0] == "row":
                    c, t = j[1], j[2]
                    r = item_no[c, t]
                    if j in e_no:
                        e = e_no[j]
                        dve.wait_ge(s("e_high"), e + 1)
                        if c == "uk":
                            src = bank.rearrange("p (h n) -> p h n", h=4)[:, :, A_NOPE:]
                            nc.vector.tensor_tensor(el[:, e % 2, 0:256].rearrange("p (h n) -> p h n", h=4), src,
                                                    eh[:, e % 2, 0:256].rearrange("p (h n) -> p h n", h=4).bitcast(F32),
                                                    ALU.subtract).then_inc(s("e_done"), 1)
                        else:
                            nc.vector.tensor_tensor(el[:, e % 2, 0:256], bank[:, 256:512],
                                                    eh[:, e % 2, 0:256].bitcast(F32), ALU.subtract)\
                                .then_inc(s("e_done"), 1)
                    if x_in_value[j] == last_piece[c, t]:
                        row_norm(dve, ch, c, t, r)
                elif j[0] == "rowT" and j[1] == "c0":
                    g = gs_no[j]
                    dve.wait_ge(s("job"), i + 1)
                    g_free(dve, g)
                    for k in range(3):
                        last = nc.vector.tensor_scalar(gs[:, g % 2, k * P:(k + 1) * P], bank[:, k * P:(k + 1) * P],
                                                       K["gcol"][:, k:k + 1], None, ALU.mult)
                    last.then_inc(s("cq_out"), 1)
                elif j[0] in ("v", "rowT"):
                    e = e_no[j]
                    rows, n = (A_QK, 512) if j[1] in ("uq", "uk") else (P, 256 if j[1] == "kv" else 512)
                    dve.wait_ge(s("e_high"), e + 1)
                    nc.vector.tensor_tensor(el[0:rows, e % 2, 0:n], bank[0:rows, 0:n],
                                            eh[0:rows, e % 2, 0:n].bitcast(F32), ALU.subtract).then_inc(s("e_done"), 1)
                if layer == 0:
                    t = c_split_at.get(j)
                    if t is not None:
                        dve.wait_ge(s("c_high"), t + 1)
                        nc.vector.tensor_tensor(cll[:, t % 2, :], cl[:, t % 2, :], chh[:, t % 2, :].bitcast(F32),
                                                ALU.subtract)\
                            .then_inc(s("c_split"), 1)

        @block.tensor
        def _(pe):
            def landed(c, k):
                pe.wait_ge(s("w_split"), piece_of[c, k] + 1)

            for j in jobs:
                i = ordinal[j]
                bank = PS[:, i % 8, :]
                kind = j[0]
                for mj, k in mod_at.get(i, ()):
                    mbank = PS[:, ordinal[mj] % 8, :]
                    if k == 0:
                        free_wait(pe, ordinal[mj])
                    n, v = raw_landed(("m", mj, k))
                    pe.wait_ge(s(n), v)
                    last = nc.tensor.matmul(mbank[0:2, :], K["cT"][:, k:16:8], raw[:, raw_no["m", mj, k] % RAW, :],
                                            start=k == 0, stop=k == KD - 1)
                    last.then_inc(s("m_used" if k < KD - 1 else "job"), 1)
                if kind == "mod":
                    continue
                free_wait(pe, i)
                if kind == "mconst":
                    pe.wait_ge(s("mbg"), 64)
                    nc.tensor.transpose(bank[:, 0:8 * KD], mrows[:], K["idn"][0:8 * KD, 0:8 * KD]).then_inc(s("job"), 1)
                elif kind == "modT":
                    pe.wait_ge(s("modrow"), mods.index(("mod",) + j[1:]) + 1)
                    for k in range(4):
                        last = nc.tensor.transpose(bank[:, 2 * k:2 * k + 2], mrow[:, k * P:(k + 1) * P],
                                                   K["idn"][0:2, 0:2])
                    last.then_inc(s("job"), 1)
                elif kind == "hT":
                    _, t, half = j
                    pe.wait_ge(s("xn"), t + 1)
                    for k in range(4):
                        last = nc.tensor.transpose(bank[:, k * P:(k + 1) * P],
                                                   xt[:, t % 2, (4 * half + k) * P:(4 * half + k + 1) * P], K["idn"][:])
                    last.then_inc(s("job"), 1)
                elif kind == "rowT":
                    c, t = j[1], j[2]
                    r = item_no[c, t]
                    pe.wait_ge(s("y_ready"), r + 1)
                    part = j[3] if len(j) > 3 else 0
                    nb, w = (3, P) if c == "c0" else (4, A_QK) if c in ("uq", "uk") else (2, P) if c == "kv" else (4, P)
                    src = X if c == "c0" else Y
                    for k in range(nb):
                        o = (4 * part + k) * w
                        last = nc.tensor.transpose(bank[0:w, k * P:(k + 1) * P], src[:, r % 2, o:o + w], K["idn"][:])
                    last.then_inc(s("job"), 1)
                elif kind in ("row", "v") and j[1] not in ("uq", "uk"):
                    c, t = j[1], j[2]
                    pe.wait_ge(s("h_low"), 2 * t + 2)
                    n = cols[c][1]
                    tok = slice(t * P, (t + 1) * P)
                    for k in range(KD):
                        if j == pos[c][0]:
                            landed(c, k)
                        w = piece_of[c, k] % WR
                        last = three_passes(nc, bank[:, 0:n], (hh[:, k, tok], hl[:, k, tok]),
                                            (wh[:, w, 0:n], wl[:, w, 0:n]), k == 0, k == KD - 1)
                    last.then_inc(s("job"), 1)
                elif kind == "gate":
                    _, c, jj, a, n = j
                    for k in range(KD):
                        if j == pos[c][0]:
                            landed(c, k)
                        w = piece_of[c, k] % WR
                        cs = slice(jj * P, (jj + 1) * P)
                        last = three_passes(nc, bank[:, 0:n], (wh[:, w, cs], wl[:, w, cs]),
                                            (hh[:, k, a:a + n], hl[:, k, a:a + n]), k == 0, k == KD - 1)
                    last.then_inc(s("job"), 1)
                else:
                    c, t, part = j[1:]
                    if c == "uq" and part == 0:
                        pe.wait_ge(s("c_split"), t + 1)
                    if t == 0:
                        landed("u", 5)
                    ks = (0, 1) if c == "uq" else (2,)
                    n = 384 if c == "uq" else 512
                    for k in ks:
                        w = piece_of["u", 2 * k + part] % WR
                        last = three_passes(nc, bank[:, 0:n], (chh[:, t % 2, k * P:(k + 1) * P], cll[:, t % 2, k * P:(k + 1) * P]),
                                            (wh[:, w, 0:n], wl[:, w, 0:n]), k == ks[0], k == ks[-1])
                    last.then_inc(s("job"), 1)



class Unit:

    def __init__(self, it, s, R, kv=None):
        self.it, self.s, self.R, self.kv = it, s, R, kv

    def value(self, a, c=0, per=1):
        return self.it * (a * self.R // per) + (a * (self.s // per) + c)

    def next(self, kv=None):
        return Unit(self.it, self.s + 1, self.R, kv)

    def wait(self, eng, sem, a, c=0, per=1):
        v = self.value(a, c, per)
        if not isinstance(v, int) or v > 0:
            eng.wait_ge(sem, v)


ORDER = {
    "A": {
        "tensor":
            "S0 T0 T1 S1 P0 T2 T3 S2 T4 P1 S3 T5 T6 S4 P2 T7 P3 P4 P5 T8 T9 P6 P7 P8 P9",
        "scalar":
            "T0 T1 E0a E0b T2 T3 E1 T4 E2 T5 E3 T6 T7 E4 Za T8 T9 O",
        "vector":
            "M0 T0 T1 M1 T2 T3 M2 T4 M3 T5 M4 T6 Za T7 Zb T8 T9 O",
        "gpsimd": "N1 N2 N3 N4 N0",
    },
    "B": {
        "tensor":
            "S0 S1 T0 T1 S2 S3 T2 T3 S4 P0 S5 S6 T4 T5 S7 P1 T6 S8 T7 S9 P2 P3 P4 P5 T8 P6 T9 P7 "
            "P8 P9",
        "scalar":
            "T0 T1 E0a E0b E1 E2 T2 E3 T3 E4 E5a E5b T4 T5 E6 E7 E8 T6 T7 E9 Za T8 T9 O",
        "vector":
            "M0 M1 N1 T0 T1 M2 M3 N2 T2 M4 M5 T3 N3 M6 T4 M7 T5 M8 N4 M9 T6 Za T7 Zb T8 T9 N0",
        "gpsimd": "N1 N2 N3 N4 N0",
    },
    "C": {
        "tensor":
            "S0 T0 T1 S1 T2 P0 T3 S2 T4 S3 P1 T5 T6 S4 P2 T7 P3 P4 T8 P5 T9 P6 P7 P8 P9",
        "scalar":
            "T0 T1 E0a E0b T2 E1 T3 T4 E2 T5 T6 E3 T7 E4 T8 Za T9 O",
        "vector":
            "M0 T0 T1 M1 T2 M2 T3 T4 M3 T5 M4 Za T6 T7 T8 Zb T9",
        "gpsimd": "N1 N2 N3 N4 N0",
    },
}


class Plan:

    def __init__(self, kind, layer, ctx_queries):
        self.kind, self.ctx = kind, ctx_queries
        self.maps = 2 if kind == "B" else 1
        self.rows = A_QK if kind == "A" else P
        self.queries = CTX if ctx_queries else 512
        self.keys = CTX if ctx_queries else TOK
        self.QT, self.KT = self.queries // P, self.keys // P
        self.SEG = self.keys // 256
        heads = {"A": A_HEADS, "B": B_HEADS, "C": C_HEADS}[kind]
        self.per_head = 1 if ctx_queries else 2
        self.units = heads * self.per_head
        self.R = 2 if kind == "C" else 4
        self.QS = 4 if ctx_queries else 2
        self.KS = 4 if ctx_queries else 2
        self.ring = 4 if ctx_queries else 5
        if ctx_queries:
            self.chunks = [([(q, 0, 256) for q in range(2)], 0)]
            self.NC = 1
        else:
            self.chunks = [([(q, 1024, 256) for q in range(4)], 1)] + [([(q, 0, 1024)], 0) for q in range(4)]
            self.NC = 2
        self.C = len(self.chunks) * self.maps
        self.dve_segs = self.SEG if self.maps == 2 or ctx_queries else 0
        self.turn_bank = [kt % 2 for kt in range(self.KT)]
        self.turn_free = []
        for i, b in enumerate(self.turn_bank):
            before = [k - self.KT for k, c in enumerate(self.turn_bank) if c == b]
            before += [k for k, c in enumerate(self.turn_bank[:i]) if c == b]
            self.turn_free.append(before[-1] + 1)
        self.out_banks = 2
        self.lag = 2
        self.stat_parts = (0, 1) if self.NC > 1 else (1,)
        self.fused_segs = 1
        if ctx_queries:
            self.new = [1] * self.C + [0] * (self.KT - self.C)
        elif self.maps == 1:
            self.new = [1, 1, 0, 1, 0, 1, 1, 0, 0, 0]
        else:
            self.new = [1, 1, 1, 1, 2, 1, 1, 1, 1, 0]
        assert len(self.new) == self.KT and sum(self.new) == self.C

    def engine_parts(self, engine, has_next):
        if self.ctx:
            return self.parts(has_next)
        names = {"P": "PV", "Z": "STAT", "O": "OUT"}
        out = []
        for word in ORDER[self.kind][engine].split():
            what, digits = word[0], "".join(c for c in word if c.isdigit())
            half = "ab".index(word[-1]) if word[-1] in "ab" else None
            of_next = what in "SMEZ" or word == "N0"
            if of_next and not has_next:
                continue
            if what == "Z":
                out.append(("STAT", half))
            elif word == "N0":
                out.append(("N0", 0))
            else:
                part = (names.get(what, what), int(digits or 0))
                out.append(part if half is None else part + (half,))
        return out

    def parts(self, has_next):
        out, after = [], []
        j = 0
        for kt in range(self.KT):
            new = range(j, j + self.new[kt]) if has_next else ()
            for i in new:
                out += [("S", i), ("M", i)]
            out.append(("T", kt))
            out += after[:1]
            after = after[1:]
            for i in new:
                wide = len(self.chunks[i % len(self.chunks)][0]) > 2
                out.append(("E", i, 0) if wide else ("E", i))
                if wide:
                    after.append(("E", i, 1))
            j += len(new)
            if new and j == self.C:
                after += [("STAT", p) for p in self.stat_parts] + [("N0", 0)]
            if kt % 2 == 0 and kt // 2 + 1 < self.SEG:
                out.append(("N", kt // 2 + 1))
            if kt >= self.lag:
                out.append(("PV", kt - self.lag))
        for kt in range(max(0, self.KT - self.lag), self.KT):
            out += after[:1]
            after = after[1:]
            out.append(("PV", kt))
        out += after
        out.append(("OUT", 0))
        return out

    def walk(self, eng):
        R, n = self.R, self.units // self.R
        if self.kind == "C":
            segs = [(0, 1, False), (1, 3, True), (3, 4, False), (4, 7, True), (7, 8, False)]
        elif n > 2:
            segs = [(0, 1, False), (1, n - 1, True), (n - 1, n, False)]
        else:
            segs = [(0, n, False)]

        def kv(it0, s):
            return (it0 * R + s) // (R * n // 2) if self.kind == "C" else (s // self.per_head) % self.KS

        for a, b, loop in segs:
            if loop:
                with eng.Fori(a, b) as it:
                    for s in range(R):
                        u = Unit(it, s, R, kv(a, s))
                        yield u, u.next(kv(a, s + 1) if self.kind != "C" else kv(a, s))
            else:
                for it in range(a, b):
                    for s in range(R):
                        u = Unit(it, s, R, kv(it, s))
                        yield u, None if it == n - 1 and s == R - 1 else u.next(kv(it, s + 1))


def attention(nc, A, K, sem, PS, kind, layer, ctx_queries):
    pl = Plan(kind, layer, ctx_queries)
    L = f"{kind}{int(ctx_queries)}_"
    QN, QT, KT, C, NC, maps, ring = pl.queries, pl.QT, pl.KT, pl.C, pl.NC, pl.maps, pl.ring
    rows = pl.rows
    packed = kind == "A"
    n_kv = {"A": A_HEADS, "B": B_HEADS, "C": C_KV}[kind]
    nch = len(pl.chunks)
    with ExitStack() as ctx:
        def sb(name, shape, dt=F32):
            return ctx.enter_context(nc.sbuf_tensor(L + name, shape, dt))

        S = {}

        def s(name):
            if name not in S:
                S[name] = sem(L + name)
            return S[name]

        qh = sb("q_hi", [rows, pl.QS, maps, QN], F32R)
        ql = sb("q_lo", [rows, pl.QS, maps, QN], F32R)
        kh = sb("k_hi", [rows, pl.KS, maps, pl.keys], F32R)
        kl = None if kind == "B" else sb("k_lo", [rows, pl.KS, maps, pl.keys], F32R)
        vh = sb("v_hi", [P, pl.KS, KT, P], F32R)
        vl = None if packed else sb("v_lo", [P, pl.KS, KT, P], F32R)
        prob = sb("prob", [P, 2, maps, QT, pl.keys])
        th = sb("probT_hi", [P, ring, QN], F32R)
        tl = sb("probT_lo", [P, ring, QN], F32R)
        nm = sb("neg_max", [P, 2, maps, QT, NC])
        rs = sb("row_sum", [P, 2, maps, QT, NC])
        fc = sb("factor", [P, 2, maps, QT, NC])
        gn = sb("neg_max_all", [P, maps * QT])
        den = sb("denominator", [P, maps * QT])
        low = sb("out_low", [A_V, QN]) if packed else None
        od = sb("out_rows", [P, 2, QN])
        sc = [PS[:, 2 * b:2 * b + 2, :].rearrange("p a n -> p (a n)") for b in range(2)]
        tbank = [PS[:, 4 + pl.turn_bank[i], :] for i in range(KT)]
        obank = [PS[:, 7 - b % pl.out_banks, :] for b in range(2)]
        vrows = A_V if packed else P
        tok0 = 0 if ctx_queries else CTX
        base_q = 0 if kind == "C" else tok0
        n_qdma = 4 * maps if kind == "B" else 2
        n_kdma = 4 if kind == "B" else 2
        n_vdma = 2
        out_row0 = A_WIDTH if kind == "B" else 0
        out_col0 = 0 if kind == "C" else tok0

        block = ctx.enter_context(nc.Block())

        def q_head(u):
            return u.value(1, 0, pl.per_head)

        def load_q(sp, u):
            sl = u.s % pl.QS
            h = q_head(u)
            c0 = base_q + (0 if ctx_queries else 512 * (u.s % 2))
            cs = slice(c0, c0 + QN)
            q_in = s(f"q_in{sl}")
            for half, dst in (("h", qh), ("l", ql)):
                if kind == "A":
                    sp.dma_start(dst[:, sl, 0, :].bitcast(F32), A["qkA" + half][bass.ds(h, 1), :, cs].rearrange("a p n -> (a p) n"))\
                        .then_inc(q_in, 16)
                elif kind == "C":
                    sp.dma_start(dst[:, sl, 0, :].bitcast(F32), A["qC" + half][bass.ds(h, 1), :, cs].rearrange("a p n -> (a p) n"))\
                        .then_inc(q_in, 16)
                else:
                    for m in range(2):
                        for up in range(2):
                            src = A["qkB" + half][0, bass.ds(h, 1), m * B_D:(m + 1) * B_D, cs]
                            sp.dma_start(dst[up * B_D:(up + 1) * B_D, sl, m, :].bitcast(F32), src.rearrange("a p n -> (a p) n"))\
                                .then_inc(q_in, 16)

        def load_kv(sp, h, sl):
            kv_in = s(f"kv_in{sl}")
            ks = slice(0, pl.keys)
            if kind == "A":
                for half, dst in (("h", kh), ("l", kl)):
                    sp.dma_start(dst[:, sl, 0, :].bitcast(F32), A["qkA" + half][bass.ds(h + A_HEADS, 1), :, ks].rearrange("a p n -> (a p) n"))\
                        .then_inc(kv_in, 16)
                for i, half in enumerate("hl"):
                    sp.dma_start(vh[:, sl, :, i * A_V:(i + 1) * A_V].bitcast(F32),
                                 A["vA" + half].rearrange("(k p) (h n) -> p k h n", p=P, h=A_HEADS)[:, 0:KT, bass.ds(h, 1), :]
                                 .rearrange("p k a n -> p k (a n)")).then_inc(kv_in, 16)
            else:
                if kind == "C":
                    for half, dst in (("h", kh), ("l", kl)):
                        sp.dma_start(dst[:, sl, 0, :].bitcast(F32), A["kC" + half][h, :, ks]).then_inc(kv_in, 16)
                else:
                    for m in range(2):
                        for up, half in enumerate("hl"):
                            src = A["qkB" + half][1, bass.ds(h, 1), m * B_D:(m + 1) * B_D, ks]
                            sp.dma_start(kh[up * B_D:(up + 1) * B_D, sl, m, :].bitcast(F32), src.rearrange("a p n -> (a p) n"))\
                                .then_inc(kv_in, 16)
                nh = C_KV if kind == "C" else B_HEADS
                for half, dst in (("h", vh), ("l", vl)):
                    sp.dma_start(dst[:, sl, :, :].bitcast(F32),
                                 A["v" + kind + half].rearrange("(k p) (h n) -> p k h n", p=P, h=nh)[:, 0:KT, bass.ds(h, 1), :]
                                 .rearrange("p k a n -> p k (a n)")).then_inc(kv_in, 16)

        kv_dmas = 16 * (n_kdma + n_vdma)

        def wait_q(eng, u):
            eng.wait_ge(s(f"q_in{u.s % pl.QS}"), u.value(16 * n_qdma, 16 * n_qdma, pl.QS))

        def wait_kv(eng, u):
            if kind == "C":
                eng.wait_ge(s(f"kv_in{u.kv}"), kv_dmas)
            else:
                eng.wait_ge(s(f"kv_in{u.kv}"), u.value(kv_dmas, kv_dmas, pl.per_head * pl.KS))

        @block.sync
        def _(sp):
            for n in range(min(pl.KS, n_kv)):
                if n == 0:
                    load_q(sp, Unit(0, 0, pl.R))
                load_kv(sp, n, n)
            for n in range(1, pl.QS):
                load_q(sp, Unit(0, n, pl.R))

            def store(u):
                u.wait(sp, s("o_out"), 1, 1)
                h = q_head(u)
                c0 = out_col0 + (0 if ctx_queries else 512 * (u.s % 2))
                dst = A[f"oT{layer}"].rearrange("(h n) t -> h n t", n=vrows)[bass.ds(h + out_row0 // vrows, 1), :, c0:c0 + QN]
                sp.dma_start(dst.rearrange("a n t -> (a n) t"), od[0:vrows, u.s % 2, :]).then_inc(s(f"o_st{u.s % 2}"), 16)

            def loads(u):
                v = Unit(u.it, u.s + pl.QS, pl.R)
                known = isinstance(u.it, int)
                if not known or u.it * pl.R + u.s + pl.QS < pl.units:
                    u.wait(sp, s("scored"), C, C)
                    load_q(sp, v)
                if kind != "C" and u.s % pl.per_head == 0:
                    h1 = u.value(1, pl.KS - 1, pl.per_head)
                    first = known and u.it == 0 and u.s == 0
                    if not first and (not known or h1 < n_kv):
                        u.wait(sp, s("multiplied"), KT, 0)
                        load_kv(sp, h1, (u.s // pl.per_head + pl.KS - 1) % pl.KS)

            for u, nxt in pl.walk(sp):
                loads(u)
                store(u)
            for b in range(2):
                sp.wait_ge(s(f"o_st{b}"), 16 * (pl.units // 2))

        def probs_of(u, m, q, k0, n):
            return prob[:, u.s % 2, m, q, k0:k0 + n]

        def chunk_views(buf, pieces):
            n = pieces[0][2]
            return [(q, k0, n, buf[:, i * n:(i + 1) * n]) for i, (q, k0, n) in enumerate(pieces)]

        def both(eng, name, step):
            first = Unit(0, 0, pl.R, 0)
            for j in range(C):
                for part in ("S", "M", "E"):
                    step(None, first, (part, j))
            for p in pl.stat_parts:
                step(None, first, ("STAT", p))
            step(None, first, ("N0", 0))
            for u, nxt in pl.walk(eng):
                for part in pl.engine_parts(name, nxt is not None):
                    step(u, nxt, part)

        @block.tensor
        def _(pe):
            def step(u, nxt, part):
                what, i = part[:2]
                if what == "S":
                    m, jj = divmod(i, nch)
                    pieces, _ = pl.chunks[jj]
                    if i == 0:
                        wait_q(pe, nxt)
                        wait_kv(pe, nxt)
                    nxt.wait(pe, s("exped"), C, i - 1)
                    buf = sc[(nxt.s * C + i) % 2]
                    sl = nxt.s % pl.QS
                    for q, k0, n, view in chunk_views(buf, pieces):
                        qs = slice(q * P, (q + 1) * P)
                        for o in range(0, n, 512):
                            w = min(512, n - o)
                            ks = slice(k0 + o, k0 + o + w)
                            out = view[:, o:o + w]
                            if kind == "B":
                                nc.tensor.matmul(out, ql[:, sl, m, qs], kh[:, nxt.kv, m, ks], start=True, stop=False)
                                last = nc.tensor.matmul(out, qh[:, sl, m, qs], kh[:, nxt.kv, m, ks], start=False, stop=True)
                            else:
                                last = three_passes(nc, out, (qh[:, sl, 0, qs], ql[:, sl, 0, qs]),
                                                    (kh[:, nxt.kv, 0, ks], kl[:, nxt.kv, 0, ks]), True, True)
                    last.then_inc(s("scored"), 1)
                elif what == "T":
                    seg = i // 2
                    if seg < pl.dve_segs:
                        u.wait(pe, s("norm_dve"), pl.dve_segs, seg + 1)
                    else:
                        u.wait(pe, s("norm_pool"), pl.SEG - pl.dve_segs, seg - pl.dve_segs + 1)
                    u.wait(pe, s("split"), KT, pl.turn_free[i])
                    bank = tbank[i]
                    for q in range(QT):
                        last = nc.tensor.transpose(bank[:, q * P:(q + 1) * P], probs_of(u, 0, q, i * P, P), K["idn"][:])
                    last.then_inc(s("turned"), 1)
                elif what == "PV":
                    u.wait(pe, s("split"), KT, i + 1)
                    if i == 0:
                        u.wait(pe, s("o_out"), 1, 1 - pl.out_banks)
                    r = (u.s * KT + i) % ring
                    out = obank[u.s % 2][:, 0:QN]
                    if packed:
                        def full():
                            return nc.tensor.matmul(out, vh[:, u.kv, i, :], th[:, r, :], start=i == 0, stop=i == KT - 1)

                        def top():
                            return nc.tensor.matmul(out[0:A_V], vh[:, u.kv, i, 0:A_V], tl[:, r, :], start=False, stop=False)

                        if i == 0:
                            full()
                            last = top()
                        else:
                            top()
                            last = full()
                    else:
                        last = three_passes(nc, out, (vh[:, u.kv, i, :], vl[:, u.kv, i, :]), (th[:, r, :], tl[:, r, :]),
                                            i == 0, i == KT - 1)
                    last.then_inc(s("multiplied"), 1)

            both(pe, "tensor", step)

        @block.scalar
        def _(act):
            def step(u, nxt, part):
                what, i = part[:2]
                if what == "E":
                    m, jj = divmod(i, nch)
                    pieces, c = pl.chunks[jj]
                    if i == 0:
                        nxt.wait(act, s("turned"), KT, -KT)
                    nxt.wait(act, s("maxed"), C, i + 1)
                    b = nxt.s % 2
                    views = chunk_views(sc[(nxt.s * C + i) % 2], pieces)
                    half = part[2] if len(part) > 2 else None
                    if half is not None:
                        views = views[2 * half:2 * half + 2]
                    for q, k0, n, view in views:
                        last = nc.scalar.activation(probs_of(nxt, m, q, k0, n), view, ACT.Exp,
                                                    bias=nm[:, b, m, q, c:c + 1], accum_out=rs[:, b, m, q, c:c + 1])
                    if half != 0:
                        last.then_inc(s("exped"), 1)
                elif what == "T":
                    u.wait(act, s("turned"), KT, i + 1)
                    u.wait(act, s("multiplied"), KT, i + 1 - ring)
                    r = (u.s * KT + i) % ring
                    nc.scalar.activation(th[:, r, :], tbank[i][:, 0:QN], ACT.Copy).then_inc(s("high"), 1)
                elif what == "STAT" and i == 0:
                    nxt.wait(act, s("diff"), 1, 1)
                    b = nxt.s % 2
                    f = fc[:, b].rearrange("p m q c -> p (m q c)")
                    nc.scalar.activation(f, f, ACT.Exp).then_inc(s("diff_exp"), 1)
                elif what == "OUT":
                    b = u.s % 2
                    u.wait(act, s("multiplied"), KT, KT)
                    if packed:
                        u.wait(act, s("o_out"), 1, 0)
                        nc.scalar.activation(low[:], obank[b][A_V:P, 0:QN], ACT.Copy).then_inc(s("o_low"), 1)
                    else:
                        u.wait(act, s(f"o_st{b}"), 16, 0, 2)
                        nc.scalar.activation(od[:, b, :], obank[b][:, 0:QN], ACT.Copy).then_inc(s("o_out"), 1)

            both(act, "scalar", step)

        @block.gpsimd
        def _(pool):
            def step(u, nxt, part):
                what, i = part[:2]
                if what == "N0":
                    what, u = "N", nxt
                if what == "N":
                    c = min(i // 4, NC - 1)
                    if maps == 1 and i < pl.dve_segs:
                        return
                    if i == (0 if maps == 2 else pl.dve_segs):
                        u.wait(pool, s("factors"), 1, 1)
                        pool.sem_inc(s("pool_went_on"), 1)
                    for q in range(QT):
                        for m in range(maps if i >= pl.fused_segs else 1):
                            v = probs_of(u, m, q, 256 * i, 256)
                            last = nc.gpsimd.tensor_scalar(v, v, fc[:, u.s % 2, m, q, c:c + 1], 1.0, ALU.mult, ALU.mult)
                    last.then_inc(s("norm_pool"), 1)

            both(pool, "gpsimd", step)

        @block.vector
        def _(dve):
            per = (4 if NC > 1 else 0) + (maps - 1)

            def step(u, nxt, part):
                what, i = part[:2]
                if what == "M":
                    m, jj = divmod(i, nch)
                    pieces, c = pl.chunks[jj]
                    nxt.wait(dve, s("scored"), C, i + 1)
                    n = pieces[0][2]
                    view = sc[(nxt.s * C + i) % 2][:, 0:n * len(pieces)].rearrange("p (q n) -> p q n", n=n)
                    q0 = pieces[0][0]
                    nc.vector.tensor_reduce(nm[:, nxt.s % 2, m, q0:q0 + len(pieces), c], view, AX, ALU.max,
                                            negate=True).then_inc(s("maxed"), 1)
                elif what == "T":
                    u.wait(dve, s("high"), KT, i + 1)
                    r = (u.s * KT + i) % ring
                    nc.vector.tensor_tensor(tl[:, r, :], tbank[i][:, 0:QN], th[:, r, :].bitcast(F32),
                                            ALU.subtract).then_inc(s("split"), 1)
                elif what in ("N", "N0"):
                    if what == "N0":
                        u = nxt
                    c = min(i // 4, NC - 1)
                    if i >= pl.dve_segs:
                        return
                    if i == 0:
                        u.wait(dve, s("factors"), 1, 1)
                    if maps == 2:
                        u.wait(dve, s("norm_pool"), pl.SEG, i + 1)
                    if maps == 2 and i >= pl.fused_segs:
                        v0, v1 = (prob[:, u.s % 2, m, :, 256 * i:256 * i + 256] for m in range(2))
                        nc.vector.tensor_tensor(v0, v0, v1, ALU.add).then_inc(s("norm_dve"), 1)
                        return
                    for q in range(QT):
                        v = probs_of(u, 0, q, 256 * i, 256)
                        if maps == 2:
                            last = nc.vector.scalar_tensor_tensor(v, probs_of(u, 1, q, 256 * i, 256),
                                                                  fc[:, u.s % 2, 1, q, c:c + 1], v, ALU.mult, ALU.add)
                        else:
                            last = nc.vector.tensor_scalar(v, v, fc[:, u.s % 2, 0, q, c:c + 1], None, ALU.mult)
                    last.then_inc(s("norm_dve"), 1)
                elif what == "STAT":
                    b = nxt.s % 2
                    k = [1 if i == 1 and NC > 1 else 0]

                    def link(ins):
                        k[0] += 1
                        ins.then_inc(s("chain"), 1)
                        nxt.wait(dve, s("chain"), per, k[0])

                    flat = [t[:, b].rearrange("p m q c -> p (m q) c") for t in (nm, rs, fc)]
                    mq = maps * QT
                    if i == 0:
                        nxt.wait(dve, s("maxed"), C, C)
                        link(nc.vector.tensor_reduce(gn[:], flat[0], AX, ALU.min))
                        nc.vector.tensor_tensor(flat[2], gn[:].unsqueeze(2).to_broadcast([P, mq, NC]), flat[0],
                                                ALU.subtract).then_inc(s("diff"), 1)
                        return
                    nxt.wait(dve, s("exped"), C, C)
                    if NC > 1:
                        nxt.wait(dve, s("diff_exp"), 1, 1)
                        link(nc.vector.tensor_tensor(flat[1], flat[1], flat[2], ALU.mult))
                        link(nc.vector.tensor_reduce(den[:], flat[1], AX, ALU.add))
                        link(nc.vector.reciprocal(den[:], den[:]))
                        last = nc.vector.tensor_tensor(flat[2], flat[2], den[:].unsqueeze(2).to_broadcast([P, mq, NC]),
                                                       ALU.mult)
                    else:
                        last = nc.vector.reciprocal(flat[2], flat[1])
                    if maps == 2:
                        link(last)
                        f1 = fc[:, b, 1].rearrange("p q c -> p (q c)")
                        last = nc.vector.tensor_scalar(f1, f1, K["neglam"][:], None, ALU.mult)
                    last.then_inc(s("factors"), 1)
                    assert k[0] == per, (k, per)
                elif what == "OUT" and packed:
                    b = u.s % 2
                    u.wait(dve, s("o_low"), 1, 1)
                    u.wait(dve, s(f"o_st{b}"), 16, 0, 2)
                    nc.vector.tensor_tensor(od[0:A_V, b, :], obank[b][0:A_V, 0:QN], low[:], ALU.add)\
                        .then_inc(s("o_out"), 1)

            both(dve, "vector", step)



def out_project(nc, A, K, sem, PS, layer, out):
    L = f"o{layer}_"
    tiles = NT if layer == 0 else NT - NCT
    R = 2
    n_out = tiles * P
    w_out = A["e_w_out"] if layer == 0 else A["o_w_out"]
    KB = A_WIDTH // P
    with ExitStack() as ctx:
        def sb(name, shape, dt=F32):
            return ctx.enter_context(nc.sbuf_tensor(L + name, shape, dt))

        S = {}

        def s(name):
            if name not in S:
                S[name] = sem(L + name)
            return S[name]

        wh = sb("w_hi", [P, KD, D], F32R)
        wl = sb("w_lo", [P, KD, D], F32R)
        raw = sb("raw", [P, 4, D])
        o = sb("o", [P, 2, KD, P])
        g = sb("g", [P, 2, KD, P])
        y = sb("y", [P, KD, P])
        yh = sb("y_hi", [P, 2, KD, P], F32R)
        yl = sb("y_lo", [P, 2, KD, P], F32R)
        xt = sb("x", [P, 2, D])
        res = sb("res", [P, 2, D])
        gb = sb("gate_rows", [P, 2, D])
        if layer == 0:
            ob = sb("o_b", [P, n_out])
            sq = sb("o_sq", [P, n_out])
            ones = sb("ones", [P, P])
            var = sb("b_var", [P, NT, B_HEADS])
            rstd = sb("b_rstd", [P, NT, B_HEADS])
            diag = sb("b_diag", [P, B_HEADS, P])
            gout = sb("b_gain", [P, 1])
            VAR = PS[:, 5, 0:NT * B_HEADS].rearrange("p (t h) -> p t h", h=B_HEADS)
        block = ctx.enter_context(nc.Block())

        def walk(eng):
            n = tiles // R
            for a, b, loop in [(0, 2, False), (2, n - 1, True), (n - 1, n, False)] if layer == 0 else \
                    [(0, 1, False), (1, n - 1, True), (n - 1, n, False)]:
                if loop:
                    with eng.Fori(a, b) as it:
                        for q in range(R):
                            yield Unit(it, q, R), Unit(it, q - 1, R), Unit(it, q + 1, R)
                else:
                    for it in range(a, b):
                        for q in range(R):
                            yield (Unit(it, q, R), Unit(it, q - 1, R) if it or q else None,
                                   Unit(it, q + 1, R) if it < n - 1 or q < R - 1 else None)

        last_tiles = [Unit(tiles // R - 1, q, R) for q in range(R)]

        def side(u):
            return 0 if layer == 0 and isinstance(u.it, int) and u.it * R + u.s < NCT else 1

        @block.sync
        def _(sp):
            def store(u):
                u.wait(sp, s("added"), 1, 1)
                sp.dma_start(out[bass.ds(u.value(P, 0), P), :], res[:, u.s % 2]).then_inc(s(f"st{u.s % 2}"), 16)

            def load(u):
                b = u.s % 2
                tok = u.value(P, 0)
                u.wait(sp, s("y_made"), 1, -1)
                sp.dma_start(o[:, b], A[f"oT{layer}"].rearrange("(k p) t -> p k t", p=P)[:, :, bass.ds(tok, P)])\
                    .then_inc(s(f"in{b}"), 16)
                sp.dma_start(g[:, b], A[f"gateT{layer}"].rearrange("(k p) t -> p k t", p=P)[:, :, bass.ds(tok, P)])\
                    .then_inc(s(f"in{b}"), 16)
                if not (isinstance(u.it, int) and u.it == 0):
                    store(Unit(u.it, u.s - 2, R))
                if layer == 0:
                    if side(u) == 0:
                        src = A["x0c"][u.s * P:(u.s + 1) * P, :]
                    else:
                        src = A["x0l"][bass.ds(u.value(P, -CTX), P), :]
                else:
                    src = A["x1"][bass.ds(u.value(P, CTX), P), :]
                sp.dma_start(xt[:, b], src).then_inc(s(f"x_in{b}"), 16)

            if layer == 0:
                for h in range(B_HEADS):
                    if h:
                        sp.wait_ge(s("squared"), h)
                    sp.dma_start(ob[:], A["oT0"][A_WIDTH + h * P:A_WIDTH + (h + 1) * P, :]).then_inc(s("b_in"), 16)
            for k in range(KD):
                if k >= 4:
                    sp.wait_ge(s("w_split"), k - 3)
                sp.dma_start(raw[:, k % 4, :], w_out[0, k * P:(k + 1) * P, :]).then_inc(s(f"raw{k % 4}"), 16)
                if k == 0 and layer == 0:
                    sp.dma_start(gout[:], A["b_g_out"][0, :].rearrange("(p a) -> p a", a=1),
                                 allow_slow_non_contiguous=True).then_inc(s("b_gain"), 16)
                if k in (1, 2):
                    load(Unit(0, k - 1, R))
                if k == 3:
                    for side_ in range(2):
                        sp.dma_start(gb[:, side_], A["grow"][layer, side_, :].partition_broadcast(P))\
                            .then_inc(s("gate_in"), 16)

            for u, _, _ in walk(sp):
                if not (isinstance(u.it, int) and u.it == 0):
                    load(u)
            for u in last_tiles:
                store(u)
            for b in range(2):
                sp.wait_ge(s(f"st{b}"), 16 * (tiles // 2))

        @block.gpsimd
        def _(pool):
            def add(u):
                b = u.s % 2
                u.wait(pool, s(f"x_in{b}"), 16, 16, 2)
                u.wait(pool, s("gated"), 1, 1)
                nc.gpsimd.tensor_tensor(res[:, b], res[:, b], xt[:, b], ALU.add).then_inc(s("added"), 1)

            if layer == 0:
                nc.gpsimd.memset(ones[:], 1.0).then_inc(s("ones"), 1)
            for u, prev, _ in walk(pool):
                if prev is not None:
                    add(prev)
            add(last_tiles[-1])

        @block.scalar
        def _(act):
            if layer == 0:
                for h in range(B_HEADS):
                    act.wait_ge(s("b_in"), 16 * (h + 1))
                    if h:
                        act.wait_ge(s("sq_sum"), h)
                    nc.scalar.activation(sq[:], ob[:], ACT.Square).then_inc(s("squared"), 1)
                act.wait_ge(s("var"), 1)
                nc.scalar.activation(var[:], var[:], ACT.Sqrt).then_inc(s("sd"), 1)

            def high_w(k):
                act.wait_ge(s(f"raw{k % 4}"), 16 * (k // 4 + 1))
                nc.scalar.activation(wh[:, k, :], raw[:, k % 4, :], ACT.Copy).then_inc(s("w_high"), 1)

            for k in range(4):
                high_w(k)
            for u, prev, _ in walk(act):
                b = u.s % 2
                u.wait(act, s(f"in{b}"), 32, 32, 2)
                nc.scalar.activation(g[:, b], g[:, b], ACT.Silu).then_inc(s("g_made"), 1)
                u.wait(act, s("y_raw"), 1, 1)
                u.wait(act, s("projected"), 1, -1)
                nc.scalar.activation(yh[:, b], y[:], ACT.Copy).then_inc(s("y_high"), 1)
                if prev is None:
                    for k in range(4, KD):
                        high_w(k)

        @block.vector
        def _(dve):
            def low_w(k):
                dve.wait_ge(s("w_high"), k + 1)
                nc.vector.tensor_tensor(wl[:, k, :], raw[:, k % 4, :], wh[:, k, :].bitcast(F32), ALU.subtract)\
                    .then_inc(s("w_split"), 1)

            def make_diag(u):
                if layer == 0:
                    u.wait(dve, s("spread"), 1, 0)
                    nc.vector.tensor_tensor(diag[:], K["idn"][:].unsqueeze(1).to_broadcast([P, B_HEADS, P]),
                                            rstd[:, bass.ds(u.value(1, 0), 1), :].rearrange("p a h -> p (a h)")
                                            .unsqueeze(2).to_broadcast([P, B_HEADS, P]), ALU.mult)\
                        .then_inc(s("diag"), 1)

            def finish(u):
                b = u.s % 2
                u.wait(dve, s("projected"), 1, 1)
                u.wait(dve, s(f"st{b}"), 16, 0, 2)
                nc.vector.tensor_tensor(res[:, b], PS[:, 2 * b:2 * b + 2, :].rearrange("p a n -> p (a n)"),
                                        gb[:, side(u)], ALU.mult).then_inc(s("gated"), 1)

            if layer == 0:
                ch = Chain(nc, dve, s("chain"))
                dve.wait_ge(s("sq_sum"), B_HEADS)
                nc.vector.tensor_scalar(var[:], VAR, 1.0 / B_V, EPS, ALU.mult, ALU.add).then_inc(s("var"), 1)
                dve.wait_ge(s("sd"), 1)
                ch.link(nc.vector.reciprocal(rstd[:], var[:]))
                dve.wait_ge(s("b_gain"), 16)
                ch.link(nc.vector.tensor_scalar_mul(gout[:], gout[:], 1.0 - LAM_INIT))
            for k in range(4):
                low_w(k)
            make_diag(Unit(0, 0, R))
            for u, prev, nxt in walk(dve):
                b = u.s % 2
                ov, yv, gv = o[:, b], y[:], g[:, b]
                u.wait(dve, s("g_made"), 1, 1)
                u.wait(dve, s("y_made"), 1, 0)
                if layer == 0:
                    nc.vector.tensor_tensor(yv[:, 0:KB], ov[:, 0:KB], gv[:, 0:KB], ALU.mult)
                    nc.vector.scalar_tensor_tensor(gv[:, KB:], ov[:, KB:], gout[:], gv[:, KB:], ALU.mult, ALU.mult)\
                        .then_inc(s("b_gated"), 1)
                    u.wait(dve, s("b_gated"), 1, 1)
                    u.wait(dve, s("spread"), 1, 1)
                    nc.vector.tensor_tensor(yv[:, KB:], gv[:, KB:], PS[:, 4, :].rearrange("p (h n) -> p h n", h=B_HEADS),
                                            ALU.mult).then_inc(s("y_raw"), 1)
                else:
                    nc.vector.tensor_tensor(yv, ov, gv, ALU.mult).then_inc(s("y_raw"), 1)
                u.wait(dve, s("y_high"), 1, 1)
                nc.vector.tensor_tensor(yl[:, b], yv, yh[:, b].bitcast(F32), ALU.subtract).then_inc(s("y_made"), 1)
                if nxt is not None:
                    make_diag(nxt)
                if prev is None:
                    for k in range(4, KD):
                        low_w(k)
                    dve.wait_ge(s("gate_in"), 32)
                else:
                    finish(prev)
            finish(last_tiles[-1])

        @block.tensor
        def _(pe):
            def spread(u):
                if layer == 0:
                    u.wait(pe, s("diag"), 1, 1)
                    u.wait(pe, s("y_raw"), 1, 0)
                    nc.tensor.matmul(PS[:, 4, :], ones[:], diag[:].rearrange("p h n -> p (h n)"),
                                     start=True, stop=True).then_inc(s("spread"), 1)

            if layer == 0:
                pe.wait_ge(s("ones"), 1)
                for h in range(B_HEADS):
                    pe.wait_ge(s("squared"), h + 1)
                    for t in range(NT):
                        last = nc.tensor.matmul(VAR[:, t, h:h + 1], sq[:, t * P:(t + 1) * P], ones[:, 0:1],
                                                start=h == 0 and t == 0, stop=h == B_HEADS - 1 and t == NT - 1,
                                                skip_group_check=True)
                    last.then_inc(s("sq_sum"), 1)
            spread(Unit(0, 0, R))
            for u, prev, nxt in walk(pe):
                b = u.s % 2
                u.wait(pe, s("y_made"), 1, 1)
                u.wait(pe, s("gated"), 1, -1)
                for n in range(2):
                    for k in range(KD):
                        if prev is None and n == 0:
                            pe.wait_ge(s("w_split"), k + 1)
                        last = three_passes(nc, PS[:, 2 * b + n, :], (yh[:, b, k, :], yl[:, b, k, :]),
                                            (wh[:, k, n * 512:(n + 1) * 512], wl[:, k, n * 512:(n + 1) * 512]),
                                            k == 0, k == KD - 1)
                    if n == 0 and nxt is not None:
                        spread(nxt)
                last.then_inc(s("projected"), 1)



def trunk(nc, A, out, debug=None):
    def scratch(name, shape, dt=F32):
        A[name] = nc.dram_tensor(name, shape, dt, kind="Internal").ap()

    for half in "hl":
        scratch("qkA" + half, (2 * A_HEADS, A_QK, TOK))
        scratch("vA" + half, (TOK, A_WIDTH))
        scratch("qkB" + half, (2, B_HEADS, P, TOK))
        scratch("vB" + half, (TOK, B_WIDTH))
        scratch("qC" + half, (C_HEADS, C_HD, LAT))
        scratch("kC" + half, (C_KV, C_HD, TOK))
        scratch("vC" + half, (TOK, C_KV * C_HD))
    scratch("tabA", (TOK, 2, 2, A_ROPE), F32)
    scratch("tabB", (TOK, 2, 2, B_D), F32)
    scratch("tabC", (TOK, 2, 2, C_HD), F32)
    scratch("cT", (3, P, TOK), F32)
    scratch("krow", (TOK, A_ROPE), F32)
    scratch("gateT0", (D, TOK), F32)
    scratch("gateT1", (D, LAT), F32)
    scratch("oT0", (D, TOK), F32)
    scratch("oT1", (D, LAT), F32)
    scratch("x1", (TOK, D), F32)
    scratch("grow", (2, 2, D), F32)
    A["x0c"], A["x0l"] = A["ctx"][0], A["x"][0]

    with ExitStack() as ctx:
        taken = []

        def sem(name):
            taken.append(nc.alloc_semaphore(name=name))
            return taken[-1]

        K = {n: ctx.enter_context(nc.sbuf_tensor("k_" + n, shape, F32)) for n, shape in
             {"idn": [P, P], "cT": [P, 16], "neglam": [P, 1], "gcol": [P, 3], "gnope": [P, 2, A_NOPE],
              "modc": [P, 2, 2, KD, 2]}.items()}
        PS = ctx.enter_context(nc.psum_tensor("psum", [P, 8, 512], F32))
        steps = [
            lambda: setup(nc, A, K, sem, PS),
            lambda: project(nc, A, K, sem, PS, 0),
            lambda: attention(nc, A, K, sem, PS, "B", 0, False),
            lambda: attention(nc, A, K, sem, PS, "B", 0, True),
            lambda: attention(nc, A, K, sem, PS, "A", 0, False),
            lambda: attention(nc, A, K, sem, PS, "A", 0, True),
            lambda: out_project(nc, A, K, sem, PS, 0, A["x1"]),
            lambda: project(nc, A, K, sem, PS, 1),
            lambda: attention(nc, A, K, sem, PS, "C", 1, False),
            lambda: out_project(nc, A, K, sem, PS, 1, out),
        ]
        for f in steps[:debug]:
            f()
            nc.clear_and_free_semaphores(taken)
            nc.all_engine_barrier()
            taken.clear()


_INS = ["x", "c", "ctx", "c_ctx", "e_norm_g", "e_w_mod", "e_b_mod", "e_w_in", "a_g_cq", "a_w_uq", "a_g_ckv",
        "a_w_ukv", "a_g_qn", "a_g_kn", "b_g_qn", "b_g_kn", "b_lam_q1", "b_lam_k1", "b_lam_q2", "b_lam_k2",
        "b_g_out", "e_w_out", "o_norm_g", "o_w_mod", "o_b_mod", "o_w_in", "c_g_qn", "c_g_kn", "o_w_out"]


def rope_table(dim):
    n = dim // 4
    inv = (np.float32(10000.0) ** (-np.arange(n, dtype=np.float32) / np.float32(n))).astype(np.float32)
    t = np.arange(LAT)
    rows, cols = (t // GRID_W).astype(np.float32), (t % GRID_W).astype(np.float32)
    ang = np.concatenate([rows[:, None] * inv, cols[:, None] * inv], axis=-1)
    ang = np.concatenate([np.zeros((CTX, dim // 2), np.float32), ang], axis=0)
    return np.stack([np.cos(ang), np.sin(ang)], axis=1).astype(np.float32)


def kernel(**inputs):
    import concourse.bacc as bacc
    from concourse.bass_utils import run_bass_kernel_spmd

    nc = bacc.Bacc("TRN2", target_bir_lowering=False, num_devices=1)
    arrays, A = {}, {}
    for name in _INS:
        a = np.ascontiguousarray(inputs[name])
        arrays[f"in_{name}"] = a
    for n, dim in (("A", A_ROPE), ("B", B_D), ("C", C_HD)):
        arrays["in_rope" + n] = rope_table(dim)
    for name, a in arrays.items():
        A[name[3:]] = nc.dram_tensor(name, a.shape, mybir.dt.from_np(a.dtype), kind="ExternalInput").ap()
    out = nc.dram_tensor("out_x", (1, LAT, D), F32, kind="ExternalOutput").ap()
    trunk(nc, A, out[0])
    r = run_bass_kernel_spmd(nc, [arrays], core_ids=[0])
    return r.results[0]["out_x"]
```

```python
from contextlib import ExitStack

import numpy as np

import concourse.bass as bass
from concourse import mybir

F32 = mybir.dt.float32
F32R = mybir.dt.float32r
ALU = mybir.AluOpType
ACT = mybir.ActivationFunctionType
AX = mybir.AxisListType.X

P = 128
D = 1024
KD = D // P
CTX = 256
LAT = 1024
TOK = CTX + LAT
NT = TOK // P
NCT = CTX // P
GRID_W = 64
EPS = 1e-6

A_HEADS, A_NOPE, A_ROPE, A_V = 8, 64, 32, 64
A_QK = A_NOPE + A_ROPE
A_Q_LORA, A_KV_LORA = 256, 128
B_HEADS, B_D, B_V = 4, 64, 128
C_HEADS, C_KV, C_HD = 8, 2, 128
A_WIDTH, B_WIDTH = A_HEADS * A_V, B_HEADS * B_V
LAM_INIT = 0.2

W0 = A_Q_LORA + A_KV_LORA + A_ROPE
E_GATE_A = W0
E_BQ = E_GATE_A + A_WIDTH
E_BK = E_BQ + 2 * B_HEADS * B_D
E_BV = E_BK + 2 * B_HEADS * B_D
E_GATE_B = E_BV + B_WIDTH
O_K = C_HEADS * C_HD
O_GATE = O_K + 2 * C_KV * C_HD
WR = 16
RAW = 5


def three_passes(nc, out, lhs, rhs, start, stop):
    nc.tensor.matmul(out, lhs[1], rhs[0], start=start, stop=False)
    nc.tensor.matmul(out, lhs[0], rhs[1], start=False, stop=False)
    return nc.tensor.matmul(out, lhs[0], rhs[0], start=False, stop=stop)


class Chain:

    def __init__(self, nc, eng, sem):
        self.nc, self.eng, self.sem, self.n = nc, eng, sem, 0

    def link(self, ins):
        ins.then_inc(self.sem, 1)
        self.n += 1
        self.eng.wait_ge(self.sem, self.n)



class Setup:

    def __init__(self, nc, A, K, sem, PS, sb):
        self.nc, self.A, self.K, self.PS = nc, A, K, PS
        self.cc = sb("su_cc", [16, P])
        self.lam = sb("su_lam", [P, 4, B_D])
        self.lp = sb("su_lp", [P, 2, B_D])
        self.ls = sb("su_ls", [P, 2])
        self.kinds = {"A": (A_ROPE, A_QK), "B": (B_D, B_D), "C": (C_HD, C_HD)}
        self.gain, self.cs, self.tab = {}, {}, {}
        for n, (rd, full) in self.kinds.items():
            self.gain[n] = sb(f"su_g{n}", [P, 2, full])
            self.cs[n] = sb(f"su_cs{n}", [P, NT, 2, rd // 2])
            self.tab[n] = sb(f"su_t{n}", [P, NT, 2, 2, rd])
        (self.s_in, self.s_cc, self.s_id, self.s_silu, self.s_chain, self.s_sums, self.s_exp, self.s_tab,
         self.stored, self.s_turned, self.s_columns) = (
            sem("su_" + n) for n in ("in", "ccin", "id", "silu", "chain", "sums", "exp", "tab", "stored",
                                     "turned", "columns"))

    def load_conditioning(self, eng):
        eng.dma_start(self.cc[0:8, :], self.A["c_ctx"].rearrange("(k p) -> k p", p=P)).then_inc(self.s_cc, 16)
        eng.dma_start(self.cc[8:16, :], self.A["c"][0, :].rearrange("(k p) -> k p", p=P)).then_inc(self.s_cc, 16)

    def load_rest(self, eng):
        A, K = self.A, self.K
        for j, n in enumerate(("b_lam_q1", "b_lam_k1", "b_lam_q2", "b_lam_k2")):
            eng.dma_start(self.lam[:, j, :], A[n][0, :].partition_broadcast(P)).then_inc(self.s_in, 16)
        for n, (q, k) in {"A": ("a_g_qn", "a_g_kn"), "B": ("b_g_qn", "b_g_kn"),
                          "C": ("c_g_qn", "c_g_kn")}.items():
            eng.dma_start(self.gain[n][:, 0, :], A[q][0, :].partition_broadcast(P)).then_inc(self.s_in, 16)
            eng.dma_start(self.gain[n][:, 1, :], A[k][0, :].partition_broadcast(P)).then_inc(self.s_in, 16)
            eng.dma_start(self.cs[n][:], A["rope" + n].rearrange("(t p) a f -> p t a f", p=P)).then_inc(self.s_in, 16)
        eng.dma_start(K["gcol"][:, 0:2], A["a_g_cq"][0, :].rearrange("(k p) -> p k", p=P),
                      allow_slow_non_contiguous=True).then_inc(self.s_in, 16)
        eng.dma_start(K["gcol"][:, 2:3], A["a_g_ckv"][0, :].rearrange("(k p) -> p k", p=P),
                      allow_slow_non_contiguous=True).then_inc(self.s_in, 16)

    def store_tables(self, eng):
        for i, n in enumerate("CBA"):
            eng.wait_ge(self.s_tab, i + 1)
            eng.dma_start(self.A["tab" + n].rearrange("(t p) q a f -> p t q a f", p=P), self.tab[n][:])\
                .then_inc(self.stored, 16)

    def identity(self, pool):
        nc, idn = self.nc, self.K["idn"]
        nc.gpsimd.memset(idn[:], 0.0).then_inc(self.s_id, 1)
        pool.wait_ge(self.s_id, 1)
        nc.gpsimd.affine_select(out=idn[:], in_=idn[:], compare_op=ALU.not_equal, fill=1.0, base=0,
                                pattern=[[-1, P]], channel_multiplier=1).then_inc(self.s_id, 1)

    def silu(self, act):
        act.wait_ge(self.s_cc, 32)
        self.nc.scalar.activation(self.cc[:], self.cc[:], ACT.Silu).then_inc(self.s_silu, 1)

    def exp_lambda(self, act):
        act.wait_ge(self.s_sums, 1)
        self.nc.scalar.activation(self.ls[:], self.ls[:], ACT.Exp).then_inc(self.s_exp, 1)

    def turn_conditioning(self, pe):
        pe.wait_ge(self.s_id, 2)
        pe.wait_ge(self.s_silu, 1)
        self.nc.tensor.transpose(self.PS[:, 7, 0:16], self.cc[:], self.K["idn"][0:16, 0:16]).then_inc(self.s_turned, 1)
        pe.wait_ge(self.s_columns, 1)

    def columns(self, dve):
        dve.wait_ge(self.s_turned, 1)
        self.nc.vector.tensor_copy(self.K["cT"][:], self.PS[:, 7, 0:16]).then_inc(self.s_columns, 1)

    def lambda_sums(self, dve, ch):
        nc, lam = self.nc, self.lam
        dve.wait_ge(self.s_in, 16 * 15)
        for j in range(2):
            last = nc.vector.tensor_tensor(self.lp[:, j, :], lam[:, 2 * j, :], lam[:, 2 * j + 1, :], ALU.mult)
        ch.link(last)
        nc.vector.tensor_reduce(self.ls[:], self.lp[:], AX, ALU.add).then_inc(self.s_sums, 1)

    def neg_lambda(self, dve, ch):
        nc, ls, neg = self.nc, self.ls, self.K["neglam"]
        dve.wait_ge(self.s_exp, 1)
        ch.link(nc.vector.tensor_tensor(neg[:], ls[:, 1:2], ls[:, 0:1], ALU.subtract))
        nc.vector.tensor_scalar_add(neg[:], neg[:], -LAM_INIT)

    def table(self, ch, n):
        nc = self.nc
        rd, full = self.kinds[n]
        gain, cs, tab = self.gain[n], self.cs[n], self.tab[n]
        ch.link(nc.vector.tensor_scalar_mul(gain[:, 0, :], gain[:, 0, :], float(full) ** -0.5))
        for q in range(2):
            for a in range(2):
                for half in range(2):
                    o = full - rd + half * rd // 2
                    g = gain[:, q, o:o + rd // 2].unsqueeze(1).to_broadcast([P, NT, rd // 2])
                    last = nc.vector.tensor_tensor(tab[:, :, q, a, half * rd // 2:(half + 1) * rd // 2],
                                                   cs[:, :, a, :], g, ALU.mult)
        last.then_inc(self.s_tab, 1)
        if n == "A":
            nc.vector.tensor_copy(self.K["gnope"][:], gain[:, :, 0:A_NOPE])



def plan_project(layer):
    jobs = []

    def norm(t):
        jobs.extend([("hT", t, 0), ("hT", t, 1)])

    if layer == 0:
        jobs += [("mod", 0, 0), ("mconst",), ("mod", 0, 1), ("modT", 0, 0), ("mod", 0, 2), ("modT", 0, 1),
                 ("mod", 0, 3), ("modT", 0, 2), ("modT", 0, 3)]
    norm(0)
    norm(1)
    first = "c0" if layer == 0 else "kv"
    for t in range(NT):
        if t + 2 < NT:
            norm(t + 2)
        jobs.append(("row", first, t))
        if t:
            jobs.append(("rowT", first, t - 1))
    jobs.append(("rowT", first, NT - 1))
    if layer == 0:
        chunks = ("bq", "bk")
        tiles = range(NT)
        mods = {("bq", 1): (0, 4), ("bq", 4): (0, 5), ("bq", 7): (1, 0), ("bk", 0): (1, 1), ("bk", 3): (1, 2),
                ("bk", 6): (1, 3), ("bv", 0): (1, 4), ("bv", 4): (1, 5)}
    else:
        chunks = ("q0", "q1")
        tiles = range(NCT, NT)
        mods = {}
    prev = late = None
    for c in chunks + (("bv",) if layer == 0 else ()):
        for t in tiles:
            jobs.append(("v" if c == "bv" else "row", c, t))
            if prev:
                jobs.append(("rowT",) + prev)
            prev = None if c == "bv" else (c, t)
            if late:
                jobs.append(("modT",) + late)
            late = mods.get((c, t))
            if late:
                jobs.append(("mod",) + late)
    if prev:
        jobs.append(("rowT",) + prev)
    groups = [(0, 512), (512, 512), (1024, 256)] if layer == 0 else [(256, 512), (768, 512)]
    ga, gb = [[("gate", c, j, a, n) for j in range(4) for a, n in groups] for c in ("ga", "gb")]
    if layer == 1:
        return jobs + ga + gb
    jobs += ga[:3]
    fill = [ga[3:6], ga[6:8], ga[8:10], ga[10:12], [], gb[0:3], gb[3:5], gb[5:7], gb[7:9], gb[9:12]]
    prev = None
    for t in range(NT):
        gates = fill[t]
        jobs += [("row", "uq", t, 0), ("row", "uq", t, 1)] + gates[:1]
        if prev is not None:
            jobs += [("rowT", "uk", prev, 0), ("rowT", "uk", prev, 1)]
        jobs += [("row", "uk", t, 0), ("row", "uk", t, 1)] + gates[1:2 if t == NT - 1 else None]
        jobs += [("rowT", "uq", t, 0), ("rowT", "uq", t, 1)]
        prev = t
    jobs += fill[-1][2:] + [("rowT", "uk", prev, 0), ("rowT", "uk", prev, 1)]
    return jobs


ITEMS = {"bq": (8, 64, 64, 0), "bk": (8, 64, 64, 1), "uq": (8, 96, 32, 0), "uk": (8, 96, 32, 1),
         "q0": (4, 128, 128, 0), "q1": (4, 128, 128, 0), "kv": (2, 128, 128, 1), "c0": (2, 0, 0, 0)}
TABLE = {"b": "tabB", "u": "tabA", "q": "tabC", "k": "tabC"}


def project(nc, A, K, sem, PS, layer):
    jobs = plan_project(layer)
    L = f"p{layer}_"
    ordinal, done_by = {}, {}
    for i, job in enumerate(jobs):
        ordinal[job] = i
    free_name = {"mod": "modrow", "modT": "modcol", "mconst": "modcol", "hT": "h_evac", "v": "e_done", "gate": "gate_out"}
    counts = {}

    def free_of(job):
        kind = job[0]
        if kind == "hT" and job[2] == 1:
            return "h_evac_act"
        if kind == "row":
            if job[1] == "c0":
                return "x_in"
            return "e_done" if job[1] in ("kv", "uk") else "x_in"
        if kind == "rowT":
            return "cq_out" if job[1] == "c0" else "e_done"
        return free_name[kind]

    for i, job in enumerate(jobs):
        n = free_of(job)
        counts[n] = counts.get(n, 0) + 1
        done_by[job] = (n, counts[n])
    order_e = [j for j in jobs if free_of(j) == "e_done"]
    items = []
    for j in jobs:
        if j[0] == "row" and (j[1], j[2]) not in items:
            items.append((j[1], j[2]))
    item_no = {it: i for i, it in enumerate(items)}
    e_no = {j: i for i, j in enumerate(order_e)}
    gs_jobs = [j for j in jobs if j[0] == "gate" or (j[0] == "rowT" and j[1] == "c0")]
    gs_no = {j: i for i, j in enumerate(gs_jobs)}

    w_in = A["e_w_in"] if layer == 0 else A["o_w_in"]
    if layer == 0:
        cols = {"c0": (0, W0), "bq": (E_BQ, 512), "bk": (E_BK, 512), "bv": (E_BV, 512),
                "ga": (E_GATE_A, 512), "gb": (E_GATE_B, 512)}
        chunk_order = ["c0", "bq", "bk", "bv", "ga", "u", "gb"]
    else:
        cols = {"kv": (O_K, 512), "q0": (0, 512), "q1": (512, 512), "ga": (O_GATE, 512), "gb": (O_GATE + 512, 512)}
        chunk_order = ["kv", "q0", "q1", "ga", "gb"]
    pieces, piece_of = [], {}
    for c in chunk_order:
        if c == "u":
            srcs = [(A["a_w_uq"][0, k * P:(k + 1) * P, h * 384:(h + 1) * 384], 384) for k in range(2) for h in range(2)]
            srcs += [(A["a_w_ukv"][0, :, h * 512:(h + 1) * 512], 512) for h in range(2)]
        else:
            o, n = cols[c]
            srcs = [(w_in[0, k * P:(k + 1) * P, o:o + n], n) for k in range(KD)]
        for k, s in enumerate(srcs):
            piece_of[c, k] = len(pieces)
            pieces.append(s)
    mods = [("mod", l, j) for (k, l, j) in [x for x in jobs if x[0] == "mod"]]

    split_at = {}
    pos = {}
    for i, j in enumerate(jobs):
        if j[0] in ("row", "v", "gate"):
            pos.setdefault(j[1], []).append(j)
    seq = ["c0", "bq", "bk", "bv", "ga"] if layer == 0 else ["kv", "q0", "q1", "ga"]
    nxt = {"c0": ["bq"], "bq": ["bk"], "bk": ["bv"], "bv": ["ga"], "ga": ["u", "gb"]} if layer == 0 else \
        {"kv": ["q0"], "q0": ["q1"], "q1": ["ga"], "ga": ["gb"]}
    for c in seq:
        want = [p for n in nxt[c] for p in range(piece_of[n, 0], piece_of[n, 0] + (6 if n == "u" else KD))]
        at = pos[c]
        for k, p in enumerate(want):
            if layer == 0 and c == "ga":
                split_at.setdefault(at[0 if k < 6 else 1 if k < 8 else -1], []).append(p)
            else:
                split_at.setdefault(at[min(k, len(at) - 1)], []).append(p)

    raws = []

    def chunk_raws(c):
        return [("w", piece_of[c, k]) for k in range(6 if c == "u" else KD)]

    def mod_raws(js):
        return [("m", j, k) for j in js for k in range(KD)]

    first_mods = [j for j in jobs[:9] if j[0] == "mod"]
    w, m = chunk_raws(chunk_order[0]), mod_raws(first_mods)
    if m:
        for i, x in enumerate(m):
            raws.append(x)
            if i >= len(m) // 2 and i % 2:
                raws.append(w[(i - len(m) // 2) // 2])
    else:
        raws += w
    mod_at = {}
    for i, j in enumerate(jobs):
        if j[0] == "mod":
            for k in range(KD):
                mod_at.setdefault(i if j in first_mods else i - max(0, 4 - k // 2 - k // 7), []).append((j, k))
    raw_position = [jobs.index(x[1]) if x[0] == "m" else 0 for x in raws]
    for i, j in enumerate(jobs):
        raws += [("w", p) for p in split_at.get(j, ())]
        raws += [("m",) + x for x in mod_at.get(i, ()) if x[0] not in first_mods]
        raw_position += [i] * (len(raws) - len(raw_position))
    raw_no = {r: i for i, r in enumerate(raws)}
    m_no = {r: i for i, r in enumerate([r for r in raws if r[0] == "m" and r[2] < KD - 1])}
    w_order = [r[1] for r in raws if r[0] == "w"]
    assert w_order == sorted(w_order)

    def raw_landed(r):
        i = raw_no[r]
        return f"raw{i % RAW}", 16 * (i // RAW + 1)

    chunk_of = {p: c for (c, _), p in piece_of.items()}

    with ExitStack() as ctx:
        def sb(name, shape, dt=F32):
            return ctx.enter_context(nc.sbuf_tensor(L + name, shape, dt))

        setup = None
        if layer == 0:
            with ExitStack() as early:
                setup = Setup(nc, A, K, sem, PS, lambda n, sh: early.enter_context(nc.sbuf_tensor(n, sh, F32)))
        hh = sb("hT_hi", [P, KD, TOK], F32R)
        hl = sb("hT_lo", [P, KD, TOK], F32R)
        wh = sb("w_hi", [P, WR, 512], F32R)
        wl = sb("w_lo", [P, WR, 512], F32R)
        raw = sb("raw", [P, RAW, 512])
        X = sb("x_rows", [P, 2, 768])
        SQ = sb("squares", [P, 768])
        junk = sb("junk", [P, D], mybir.dt.bfloat16)
        Y = sb("y_rows", [P, 2, 768])
        U = sb("rope_u", [P, 512])
        V = sb("rope_v", [P, 512])
        eh = sb("e_hi", [P, 2, 512], F32R)
        el = sb("e_lo", [P, 2, 512], F32R)
        gs = sb("gate_rows", [P, 2, 512])
        tb = sb("table", [P, 2, 256])
        st = sb("stats", [P, 2, 4, 8])
        ssx = sb("x_stats", [P, 2, 4])
        if layer == 0:
            mrow = sb("mod_row", [2, 512])
            mcol = sb("mod_gate", [P, 4, 2])
            mrows = sb("mod_rows", [8 * KD, P])
            mconst = sb("mod_const", [P, 2, 4 * KD])
            mbias, mgain = mconst[:, :, 0:3 * KD], mconst[:, :, 3 * KD:]
            with nc.sbuf_tensor(L + "x_tiles", [P, 2, D], F32) as xt:
                pass
            cl = sb("c_in", [P, 2, 384])
            chh = sb("c_hi", [P, 2, 384], F32R)
            cll = sb("c_lo", [P, 2, 384], F32R)
            kr = sb("kr_in", [P, 4, A_ROPE])
            tmpv = Y[:].rearrange("p a b -> p (a b)")[:, 0:D]
        else:
            xt = sb("x_tiles", [P, 2, D])
            tmpv = sb("modulated", [P, D])[:]

        S = {}

        def s(name):
            if name not in S:
                S[name] = sem(L + name)
            return S[name]

        block = ctx.enter_context(nc.Block())

        def free_wait(eng, i):
            if i >= 8:
                n, v = done_by[jobs[i - 8]]
                if n == "x_in":
                    v = x_in_value[jobs[i - 8]]
                eng.wait_ge(s(n), v)

        x_in_value, k = {}, 0
        for j in jobs:
            if j[0] == "row":
                k += 1
                x_in_value[j] = k
        last_piece = {}
        for j in jobs:
            if j[0] == "row":
                last_piece[j[1], j[2]] = x_in_value[j]

        c_split_at, c_load_at = {}, {}
        if layer == 0:
            last_ga = [j for j in jobs if j[0] == "gate" and j[1] == "ga"]
            c_load_at[last_ga[0]] = 0
            c_load_at[last_ga[1]] = 1
            c_split_at[last_ga[1]] = 0
            c_split_at[last_ga[2]] = 1
            c_load_at[last_ga[2]] = 2
            for t in range(NT - 2):
                c_split_at["row", "uk", t, 1] = t + 2
                if t + 3 < NT:
                    c_load_at["row", "uk", t, 1] = t + 3

        tab_no, y_user, per_slot = {}, {}, [0, 0]
        rope_items = [it for it in items if it[0] != "c0"]
        for it in rope_items:
            b = item_no[it] % 2
            per_slot[b] += 1
            tab_no[it] = per_slot[b]
        last_T = {}
        for j in jobs:
            if j[0] == "rowT" and j[1] != "c0":
                last_T[j[1], j[2]] = ordinal[j]
        for it in rope_items:
            r = item_no[it]
            if r >= 2 and items[r - 2] in last_T:
                y_user[r] = last_T[items[r - 2]]

        def store_of(j, t_ap, half):
            kind, c, t = j[:3]
            tok = slice(t * P, (t + 1) * P)
            if kind == "v":
                return [(A["vB" + half][tok, :], t_ap)]
            if kind == "row" and c == "uk":
                return [(A["vA" + half][tok, j[3] * 256:(j[3] + 1) * 256], t_ap[:, 0:256])]
            if kind == "row" and c == "kv":
                return [(A["vC" + half][tok, :], t_ap[:, 0:256])]
            v = t_ap.rearrange("p (h n) -> p h n", h=4)
            if c in ("uq", "uk"):
                u = (0 if c == "uq" else 8) + 4 * j[3]
                return [(A["qkA" + half][u:u + 4, :, tok].rearrange("h p n -> p h n"), v[0:A_QK])]
            if c in ("bq", "bk"):
                return [(A["qkB" + half][0 if c == "bq" else 1, :, :, tok].rearrange("h p n -> p h n"), v)]
            if c in ("q0", "q1"):
                u = 0 if c == "q0" else 4
                tk = slice((t - NCT) * P, (t - NCT + 1) * P)
                return [(A["qC" + half][u:u + 4, :, tk].rearrange("h p n -> p h n"), v)]
            return [(A["kC" + half][:, :, tok].rearrange("h p n -> p h n"), v[:, 0:2, :])]

        def e_free(eng, e):
            if e >= 2:
                eng.wait_ge(s(f"e_st{e % 2}"), 32 * (e // 2))

        def g_free(eng, g):
            if g >= 2:
                eng.wait_ge(s(f"g_st{g % 2}"), 16 * (g // 2))

        def row_slot_free(eng, r):
            if r >= 2:
                c, t = items[r - 2]
                eng.wait_ge(s("y_ready"), r - 1)
                if c == "c0":
                    eng.wait_ge(s("job"), ordinal["rowT", "c0", t] + 1)
                    eng.wait_ge(s(f"kr_st{t % 2}"), 16 * (t // 2 + 1))

        def load_mod_rows(act):
            for l, n in enumerate("eo"):
                for o, src in ((0, A[n + "_b_mod"]), (3 * KD, A[n + "_norm_g"])):
                    act.dma_start(mrows[4 * KD * l + o:4 * KD * l + o + src.shape[1] // P, :],
                                  src[0, :].rearrange("(k p) -> k p", p=P)).then_inc(s("mbg"), 16)

        def load_table(act, c, t, r):
            n, qk, rd = TABLE[c[0]], ITEMS[c][3], ITEMS[c][2]
            act.dma_start(tb[:, r % 2, 0:2 * rd], A[n][t * P:(t + 1) * P, qk, :, :].rearrange("p a f -> p (a f)"))\
                .then_inc(s(f"tab{r % 2}"), 16)

        def load_c(act, t):
            if t == 0:
                for b in range(2):
                    act.wait_ge(s(f"g_st{b}"), 16 * (NT // 2))
                for b in range(2):
                    act.wait_ge(s(f"kr_st{b}"), 16 * NT // 2)
            if t >= 2:
                act.wait_ge(s("c_split"), t - 1)
            if t >= 4:
                act.wait_ge(s("x_in"), x_in_value["row", "uk", t - 4, 1])
            act.dma_start(cl[:, t % 2, :].rearrange("p (k n) -> p k n", k=3),
                          A["cT"][:, :, t * P:(t + 1) * P].rearrange("k p n -> p k n")).then_inc(s(f"c_in{t % 2}"), 16)
            act.dma_start(kr[:, t % 4, :], A["krow"][t * P:(t + 1) * P, :]).then_inc(s(f"c_in{t % 2}"), 16)

        def x_stats(dve, ch, t):
            b = t % 2
            dve.wait_ge(s("xss"), t + 1)
            nc.vector.tensor_scalar(ssx[:, b, 1:2], ssx[:, b, 0:1], 1.0 / D, EPS, ALU.mult, ALU.add)\
                .then_inc(s("xvar"), 1)
            dve.wait_ge(s("xsd"), t + 1)
            nc.vector.reciprocal(ssx[:, b, 3:4], ssx[:, b, 2:3]).then_inc(s("xrs"), 1)

        def row_norm(dve, ch, c, t, r):
            nh, hd, rd, qk = ITEMS[c]
            b = r % 2
            x, q, y = X[:, b, :], SQ[:], Y[:, b, :]
            dve.wait_ge(s("x_in"), last_piece[c, t])
            if c == "c0":
                nc.vector.tensor_reduce(st[:, b, 0, 0:1], q[:, 0:256], AX, ALU.add)
                ch.link(nc.vector.tensor_reduce(st[:, b, 0, 1:2], q[:, 256:384], AX, ALU.add))
                nc.vector.tensor_scalar(st[:, b, 1, 0:1], st[:, b, 0, 0:1], 1.0 / A_Q_LORA, EPS, ALU.mult, ALU.add)
                nc.vector.tensor_scalar(st[:, b, 1, 1:2], st[:, b, 0, 1:2], 1.0 / A_KV_LORA, EPS, ALU.mult, ALU.add)\
                    .then_inc(s("var"), 1)
                dve.wait_ge(s("sd"), r + 1)
                ch.link(nc.vector.reciprocal(st[:, b, 3, 0:2], st[:, b, 2, 0:2]))
                nc.vector.tensor_scalar(x[:, 0:256], x[:, 0:256], st[:, b, 3, 0:1], None, ALU.mult)
                nc.vector.tensor_scalar(x[:, 256:384], x[:, 256:384], st[:, b, 3, 1:2], None, ALU.mult)\
                    .then_inc(s("y_ready"), 1)
                return
            w = nh * hd
            x3 = x[:, 0:w].rearrange("p (h n) -> p h n", h=nh)
            y3 = y[:, 0:w].rearrange("p (h n) -> p h n", h=nh)
            q3 = q[:, 0:w].rearrange("p (h n) -> p h n", h=nh)
            ch.link(nc.vector.tensor_reduce(st[:, b, 0, 0:nh], q3, AX, ALU.add))
            nc.vector.tensor_scalar(st[:, b, 1, 0:nh], st[:, b, 0, 0:nh], 1.0 / hd, EPS, ALU.mult, ALU.add)\
                .then_inc(s("var"), 1)
            dve.wait_ge(s("sd"), r + 1)
            ch.link(nc.vector.reciprocal(st[:, b, 3, 0:nh], st[:, b, 2, 0:nh]))
            ch.link(nc.vector.tensor_tensor(x3, x3, st[:, b, 3, 0:nh].unsqueeze(2).to_broadcast([P, nh, hd]), ALU.mult))
            dve.wait_ge(s(f"tab{b}"), 16 * tab_no[c, t])
            prev = y_user.get(r)
            if prev is not None:
                dve.wait_ge(s("job"), prev + 1)
            o, h2 = hd - rd, rd // 2
            tv = tb[:, b, 0:2 * rd].rearrange("p (a f) -> p a f", a=2)
            u3 = U[:, 0:nh * rd].rearrange("p (h n) -> p h n", h=nh)
            v3 = V[:, 0:nh * rd].rearrange("p (h n) -> p h n", h=nh)
            if o:
                nc.vector.tensor_tensor(y3[:, :, 0:o], x3[:, :, 0:o],
                                        K["gnope"][:, qk, :].unsqueeze(1).to_broadcast([P, nh, o]), ALU.mult)
            nc.vector.tensor_tensor(u3, x3[:, :, o:], tv[:, 0, :].unsqueeze(1).to_broadcast([P, nh, rd]), ALU.mult)
            ch.link(nc.vector.tensor_tensor(v3, x3[:, :, o:], tv[:, 1, :].unsqueeze(1).to_broadcast([P, nh, rd]), ALU.mult))
            nc.vector.tensor_tensor(y3[:, :, o:o + h2], u3[:, :, 0:h2], v3[:, :, h2:rd], ALU.subtract)
            nc.vector.tensor_tensor(y3[:, :, o + h2:], u3[:, :, h2:rd], v3[:, :, 0:h2], ALU.add)\
                .then_inc(s("y_ready"), 1)

        @block.sync
        def _(sp):
            def load_raw(i, r):
                if i >= RAW:
                    o = raws[i - RAW]
                    if o[0] == "w":
                        sp.wait_ge(s("w_split"), o[1] + 1)
                    elif o[2] < KD - 1:
                        sp.wait_ge(s("m_used"), m_no[o] + 1)
                    else:
                        sp.wait_ge(s("job"), ordinal[o[1]] + 1)
                if r[0] == "w":
                    src, n = pieces[r[1]]
                else:
                    _, (_, l, j), k = r
                    wm = A["e_w_mod"] if l == 0 else A["o_w_mod"]
                    src, n = wm[0, k * P:(k + 1) * P, j * 512:(j + 1) * 512], 512
                sp.dma_start(raw[:, i % RAW, 0:n], src).then_inc(s(raw_landed(r)[0]), 16)

            def store(j):
                if j in e_no:
                    e = e_no[j]
                    sp.wait_ge(s("e_done"), e + 1)
                    for src, name in ((eh, "h"), (el, "l")):
                        for dst, sap in store_of(j, src[:, e % 2, :], name):
                            sp.dma_start(dst, sap.bitcast(F32)).then_inc(s(f"e_st{e % 2}"), 16)
                if j in gs_no:
                    g = gs_no[j]
                    n, v = done_by[j]
                    sp.wait_ge(s(n), v)
                    if j[0] == "gate":
                        _, c, jj, a, n = j
                        row = (0 if c == "ga" else 512) + jj * P
                        a0 = a if layer == 0 else a - CTX
                        sp.dma_start(A[f"gateT{layer}"][row:row + P, a0:a0 + n], gs[:, g % 2, 0:n])\
                            .then_inc(s(f"g_st{g % 2}"), 16)
                    else:
                        t = j[2]
                        sp.dma_start(A["cT"][:, :, t * P:(t + 1) * P].rearrange("k p n -> p k n"),
                                     gs[:, g % 2, 0:384].rearrange("p (k n) -> p k n", k=3))\
                            .then_inc(s(f"g_st{g % 2}"), 16)
                if j[0] == "row" and j[1] == "c0":
                    t = j[2]
                    sp.wait_ge(s("x_in"), x_in_value[j])
                    sp.dma_start(A["krow"][t * P:(t + 1) * P, :], X[:, item_no["c0", t] % 2, 384:416])\
                        .then_inc(s(f"kr_st{t % 2}"), 16)
                if j[0] == "modT" and j[2] >= 4:
                    n, v = done_by[j]
                    sp.wait_ge(s(n), v)
                    for side in range(2):
                        sp.dma_start(A["grow"][j[1], side, (j[2] - 4) * 512:(j[2] - 3) * 512]
                                     .rearrange("(k p) -> p k", p=P), mcol[:, :, side],
                                     allow_slow_non_contiguous=True).then_inc(s("grow_st"), 16)

            if setup:
                setup.load_conditioning(sp)
            n = 0
            for i, j in enumerate(jobs):
                while n < len(raws) and raw_position[n] <= i + 6:
                    load_raw(n, raws[n])
                    n += 1
                store(j)
            assert n == len(raws)
            for b in range(2):
                sp.wait_ge(s(f"e_st{b}"), 32 * len(order_e[b::2]))
                sp.wait_ge(s(f"g_st{b}"), 16 * len(gs_jobs[b::2]))
            if layer == 0:
                for b in range(2):
                    sp.wait_ge(s(f"kr_st{b}"), 16 * NT // 2)
                sp.wait_ge(s("grow_st"), 32 * 4)

        @block.gpsimd
        def _(pool):
            def split(p):
                name, v = raw_landed(("w", p))
                pool.wait_ge(s(name), v)
                if p >= WR:
                    pool.wait_ge(s("job"), ordinal[pos[chunk_of[p - WR]][-1]] + 1)
                n = pieces[p][1]
                src = raw[:, raw_no["w", p] % RAW, 0:n]
                nc.gpsimd.tensor_scalar(wh[:, p % WR, 0:n], src, 1.0, 1.0, ALU.mult, ALU.mult)\
                    .then_inc(s("w_high"), 1)
                pool.wait_ge(s("w_high"), p + 1)
                nc.gpsimd.tensor_tensor(wl[:, p % WR, 0:n], src, wh[:, p % WR, 0:n].bitcast(F32),
                                        ALU.subtract).then_inc(s("w_split"), 1)

            if setup:
                setup.identity(pool)
                setup.load_rest(pool)
            for p in chunk_raws(chunk_order[0]):
                split(p[1])
            for j in jobs:
                for p in split_at.get(j, ()):
                    split(p)

        @block.scalar
        def _(act):
            def load_x(t):
                if t >= 2:
                    act.wait_ge(s("job"), ordinal["hT", t - 2, 1] + 1)
                src = (A["x0c"][t * P:(t + 1) * P, :] if t < NCT else A["x0l"][(t - NCT) * P:(t - NCT + 1) * P, :]) \
                    if layer == 0 else A["x1"][t * P:(t + 1) * P, :]
                act.dma_start(xt[:, t % 2, :], src).then_inc(s(f"xt{t % 2}"), 16)

            def norm_x(t):
                act.wait_ge(s(f"xt{t % 2}"), 16 * (t // 2 + 1))
                nc.scalar.activation(junk[:], xt[:, t % 2, :], ACT.Square, accum_out=ssx[:, t % 2, 0:1])\
                    .then_inc(s("xss"), 1)
                act.wait_ge(s("xvar"), t + 1)
                nc.scalar.activation(ssx[:, t % 2, 2:3], ssx[:, t % 2, 1:2], ACT.Sqrt).then_inc(s("xsd"), 1)
                act.wait_ge(s("xrs"), t + 1)
                nc.scalar.activation(xt[:, t % 2, :], xt[:, t % 2, :], ACT.Copy, scale=ssx[:, t % 2, 3:4])\
                    .then_inc(s("xn"), 1)

            load_x(0)
            load_x(1)
            if layer == 0:
                load_mod_rows(act)
                setup.silu(act)
            norm_x(0)
            norm_x(1)
            if setup:
                setup.exp_lambda(act)
                setup.store_tables(act)
            for j in jobs:
                i = ordinal[j]
                bank = PS[:, i % 8, :]
                if j[0] == "hT":
                    _, t, half = j
                    if half == 0:
                        if t + 2 < NT:
                            load_x(t + 2)
                        side = 0 if t < NCT else 1
                        if t == 0 and layer == 0:
                            act.wait_ge(s("modcol"), 5)
                        if t:
                            act.wait_ge(s("h_low"), 2 * t - 1)
                        act.wait_ge(s("job"), i + 2)
                        for k in range(4, 8):
                            last = nc.scalar.activation(tmpv[:, k * P:(k + 1) * P],
                                                        PS[:, (i + 1) % 8, (k - 4) * P:(k - 3) * P], ACT.Identity,
                                                        scale=K["modc"][:, layer, 1, k, side:side + 1],
                                                        bias=K["modc"][:, layer, 0, k, side:side + 1])
                        last.then_inc(s("h_evac_act"), 1)
                        act.wait_ge(s("h_evac_act"), t + 1)
                        if setup and t == 0:
                            act.wait_ge(setup.stored, 48)
                    else:
                        act.wait_ge(s("h_evac"), t + 1)
                    of = 1 - half
                    dst = hh[:, 4 * of:4 * of + 4, t * P:(t + 1) * P]
                    nc.scalar.activation(dst, tmpv[:, of * 512:(of + 1) * 512].rearrange("p (k n) -> p k n", k=4),
                                         ACT.Copy).then_inc(s("h_high"), 1)
                    if half == 1 and t + 2 < NT:
                        norm_x(t + 2)
                elif j[0] == "row":
                    c, t = j[1], j[2]
                    r = item_no[c, t]
                    nh, hd, rd, _ = ITEMS[c]
                    piece = j[3] if len(j) > 3 else 0
                    if piece == 0:
                        row_slot_free(act, r)
                        if c != "c0":
                            load_table(act, c, t, r)
                    x, q = X[:, r % 2, :], SQ[:]
                    act.wait_ge(s("job"), i + 1)
                    if c == "c0":
                        nc.scalar.activation(q[:, 0:384], bank[:, 0:384], ACT.Square)
                        nc.scalar.activation(x[:, 0:W0], bank[:, 0:W0], ACT.Copy).then_inc(s("x_in"), 1)
                    elif c == "uk":
                        kvv = bank.rearrange("p (h n) -> p h n", h=4)
                        xk = x.rearrange("p (h n) -> p h n", h=8)[:, 4 * piece:4 * piece + 4, :]
                        qk = q.rearrange("p (h n) -> p h n", h=8)[:, 4 * piece:4 * piece + 4, :]
                        krb = kr[:, t % 4, :].unsqueeze(1).to_broadcast([P, 4, A_ROPE])
                        nc.scalar.activation(qk[:, :, 0:A_NOPE], kvv[:, :, 0:A_NOPE], ACT.Square)
                        nc.scalar.activation(qk[:, :, A_NOPE:], krb, ACT.Square)
                        nc.scalar.activation(xk[:, :, 0:A_NOPE], kvv[:, :, 0:A_NOPE], ACT.Copy)
                        nc.scalar.activation(xk[:, :, A_NOPE:], krb, ACT.Copy).then_inc(s("x_in"), 1)
                        e = e_no[j]
                        e_free(act, e)
                        nc.scalar.activation(eh[:, e % 2, 0:256].rearrange("p (h n) -> p h n", h=4),
                                             kvv[:, :, A_NOPE:], ACT.Copy).then_inc(s("e_high"), 1)
                    else:
                        n = 384 if c == "uq" else nh * hd
                        o = piece * 384
                        nc.scalar.activation(q[:, o:o + n], bank[:, 0:n], ACT.Square)
                        nc.scalar.activation(x[:, o:o + n], bank[:, 0:n], ACT.Copy).then_inc(s("x_in"), 1)
                        if c == "kv":
                            e = e_no[j]
                            e_free(act, e)
                            nc.scalar.activation(eh[:, e % 2, 0:256], bank[:, 256:512], ACT.Copy)\
                                .then_inc(s("e_high"), 1)
                    if x_in_value[j] == last_piece[c, t]:
                        act.wait_ge(s("var"), r + 1)
                        nc.scalar.activation(st[:, r % 2, 2, 0:nh], st[:, r % 2, 1, 0:nh], ACT.Sqrt)\
                            .then_inc(s("sd"), 1)
                elif j[0] in ("v", "rowT") and j in e_no:
                    e = e_no[j]
                    act.wait_ge(s("job"), i + 1)
                    e_free(act, e)
                    rows, n = (A_QK, 512) if j[1] in ("uq", "uk") else (P, 256 if j[1] == "kv" else 512)
                    nc.scalar.activation(eh[0:rows, e % 2, 0:n], bank[0:rows, 0:n], ACT.Copy).then_inc(s("e_high"), 1)
                elif j[0] == "gate":
                    g = gs_no[j]
                    n = j[4]
                    act.wait_ge(s("job"), i + 1)
                    g_free(act, g)
                    nc.scalar.activation(gs[:, g % 2, 0:n], bank[:, 0:n], ACT.Copy).then_inc(s("gate_out"), 1)
                if layer == 0:
                    t = c_split_at.get(j)
                    if t is not None:
                        act.wait_ge(s(f"c_in{t % 2}"), 32 * (t // 2 + 1))
                        if t >= 2:
                            act.wait_ge(s("job"), ordinal["row", "uk", t - 2, 1] + 1)
                        nc.scalar.activation(chh[:, t % 2, :], cl[:, t % 2, :], ACT.Copy).then_inc(s("c_high"), 1)
                    t = c_load_at.get(j)
                    if t is not None:
                        load_c(act, t)

        @block.vector
        def _(dve):
            ch = Chain(nc, dve, s("chain"))
            if setup:
                setup.columns(dve)
            x_stats(dve, ch, 0)
            x_stats(dve, ch, 1)
            if setup:
                setup.lambda_sums(dve, ch)
                setup.table(ch, "C")
            for j in jobs:
                i = ordinal[j]
                bank = PS[:, i % 8, :]
                if j[0] == "mconst":
                    dve.wait_ge(s("job"), i + 1)
                    nc.vector.tensor_copy(mconst[:].rearrange("p l k -> p (l k)"), bank[:, 0:8 * KD])\
                        .then_inc(s("modcol"), 1)
                elif j[0] == "mod":
                    dve.wait_ge(s("job"), i + 1)
                    if mods.index(j):
                        dve.wait_ge(s("job"), ordinal[("modT",) + mods[mods.index(j) - 1][1:]] + 1)
                    nc.vector.tensor_copy(mrow[:], bank[0:2, :]).then_inc(s("modrow"), 1)
                    if mods.index(j) < 2:
                        setup.table(ch, "BA"[mods.index(j)])
                    elif mods.index(j) == 2:
                        setup.neg_lambda(dve, ch)
                elif j[0] == "modT":
                    _, l, jj = j
                    if jj == 0 and l == 0:
                        dve.wait_ge(s("modcol"), 1)
                    dve.wait_ge(s("job"), i + 1)
                    cols4 = bank[:, 0:8].rearrange("p (k a) -> p k a", a=2)
                    bias = mbias[:, l, 4 * jj:4 * jj + 4].unsqueeze(2).to_broadcast([P, 4, 2])
                    k0 = 4 * (jj % 2)
                    if jj < 4:
                        dst = K["modc"][:, l, jj // 2, k0:k0 + 4, :]
                    else:
                        dst = mcol[:]
                        before = len([x for x in mods[:mods.index(("mod", l, jj))] if x[2] >= 4])
                        if before:
                            dve.wait_ge(s("grow_st"), 32 * before)
                    last = nc.vector.tensor_tensor(dst, cols4, bias, ALU.add)
                    if jj in (2, 3):
                        ch.link(last)
                        last = nc.vector.scalar_tensor_tensor(dst, dst, 1.0, mgain[:, l, k0:k0 + 4].unsqueeze(2)
                                                              .to_broadcast([P, 4, 2]), ALU.add, ALU.mult)
                    last.then_inc(s("modcol"), 1)
                elif j[0] == "hT":
                    _, t, half = j
                    side = 0 if t < NCT else 1
                    if t == 0 and layer == 0:
                        dve.wait_ge(s("modcol"), 5)
                    if t:
                        dve.wait_ge(s("h_low"), 2 * t)
                    if half == 0:
                        dve.wait_ge(s("job"), i + 1)
                        for k in range(4):
                            last = nc.vector.tensor_scalar(tmpv[:, k * P:(k + 1) * P], bank[:, k * P:(k + 1) * P],
                                                           K["modc"][:, layer, 1, k, side:side + 1],
                                                           K["modc"][:, layer, 0, k, side:side + 1],
                                                           ALU.mult, ALU.add)
                        last.then_inc(s("h_evac"), 1)
                    else:
                        if setup and t == 0:
                            dve.wait_ge(setup.stored, 48)
                        for b in (1, 0):
                            dve.wait_ge(s("h_high"), 2 * t + 2 - b)
                            hs = (slice(None), slice(4 * b, 4 * b + 4), slice(t * P, (t + 1) * P))
                            nc.vector.tensor_tensor(hl[hs], tmpv[:, b * 512:(b + 1) * 512].rearrange("p (k n) -> p k n", k=4),
                                                    hh[hs].bitcast(F32), ALU.subtract).then_inc(s("h_low"), 1)
                        if t + 2 < NT:
                            x_stats(dve, ch, t + 2)
                elif j[0] == "row":
                    c, t = j[1], j[2]
                    r = item_no[c, t]
                    if j in e_no:
                        e = e_no[j]
                        dve.wait_ge(s("e_high"), e + 1)
                        if c == "uk":
                            src = bank.rearrange("p (h n) -> p h n", h=4)[:, :, A_NOPE:]
                            nc.vector.tensor_tensor(el[:, e % 2, 0:256].rearrange("p (h n) -> p h n", h=4), src,
                                                    eh[:, e % 2, 0:256].rearrange("p (h n) -> p h n", h=4).bitcast(F32),
                                                    ALU.subtract).then_inc(s("e_done"), 1)
                        else:
                            nc.vector.tensor_tensor(el[:, e % 2, 0:256], bank[:, 256:512],
                                                    eh[:, e % 2, 0:256].bitcast(F32), ALU.subtract)\
                                .then_inc(s("e_done"), 1)
                    if x_in_value[j] == last_piece[c, t]:
                        row_norm(dve, ch, c, t, r)
                elif j[0] == "rowT" and j[1] == "c0":
                    g = gs_no[j]
                    dve.wait_ge(s("job"), i + 1)
                    g_free(dve, g)
                    for k in range(3):
                        last = nc.vector.tensor_scalar(gs[:, g % 2, k * P:(k + 1) * P], bank[:, k * P:(k + 1) * P],
                                                       K["gcol"][:, k:k + 1], None, ALU.mult)
                    last.then_inc(s("cq_out"), 1)
                elif j[0] in ("v", "rowT"):
                    e = e_no[j]
                    rows, n = (A_QK, 512) if j[1] in ("uq", "uk") else (P, 256 if j[1] == "kv" else 512)
                    dve.wait_ge(s("e_high"), e + 1)
                    nc.vector.tensor_tensor(el[0:rows, e % 2, 0:n], bank[0:rows, 0:n],
                                            eh[0:rows, e % 2, 0:n].bitcast(F32), ALU.subtract).then_inc(s("e_done"), 1)
                if layer == 0:
                    t = c_split_at.get(j)
                    if t is not None:
                        dve.wait_ge(s("c_high"), t + 1)
                        nc.vector.tensor_tensor(cll[:, t % 2, :], cl[:, t % 2, :], chh[:, t % 2, :].bitcast(F32),
                                                ALU.subtract)\
                            .then_inc(s("c_split"), 1)

        @block.tensor
        def _(pe):
            if setup:
                setup.turn_conditioning(pe)

            def landed(c, k):
                pe.wait_ge(s("w_split"), piece_of[c, k] + 1)

            for j in jobs:
                i = ordinal[j]
                bank = PS[:, i % 8, :]
                kind = j[0]
                for mj, k in mod_at.get(i, ()):
                    mbank = PS[:, ordinal[mj] % 8, :]
                    if k == 0:
                        free_wait(pe, ordinal[mj])
                    n, v = raw_landed(("m", mj, k))
                    pe.wait_ge(s(n), v)
                    last = nc.tensor.matmul(mbank[0:2, :], K["cT"][:, k:16:8], raw[:, raw_no["m", mj, k] % RAW, :],
                                            start=k == 0, stop=k == KD - 1)
                    last.then_inc(s("m_used" if k < KD - 1 else "job"), 1)
                if kind == "mod":
                    continue
                free_wait(pe, i)
                if kind == "mconst":
                    pe.wait_ge(s("mbg"), 64)
                    nc.tensor.transpose(bank[:, 0:8 * KD], mrows[:], K["idn"][0:8 * KD, 0:8 * KD]).then_inc(s("job"), 1)
                elif kind == "modT":
                    pe.wait_ge(s("modrow"), mods.index(("mod",) + j[1:]) + 1)
                    for k in range(4):
                        last = nc.tensor.transpose(bank[:, 2 * k:2 * k + 2], mrow[:, k * P:(k + 1) * P],
                                                   K["idn"][0:2, 0:2])
                    last.then_inc(s("job"), 1)
                elif kind == "hT":
                    _, t, half = j
                    pe.wait_ge(s("xn"), t + 1)
                    for k in range(4):
                        last = nc.tensor.transpose(bank[:, k * P:(k + 1) * P],
                                                   xt[:, t % 2, (4 * half + k) * P:(4 * half + k + 1) * P], K["idn"][:])
                    last.then_inc(s("job"), 1)
                elif kind == "rowT":
                    c, t = j[1], j[2]
                    r = item_no[c, t]
                    pe.wait_ge(s("y_ready"), r + 1)
                    part = j[3] if len(j) > 3 else 0
                    nb, w = (3, P) if c == "c0" else (4, A_QK) if c in ("uq", "uk") else (2, P) if c == "kv" else (4, P)
                    src = X if c == "c0" else Y
                    for k in range(nb):
                        o = (4 * part + k) * w
                        last = nc.tensor.transpose(bank[0:w, k * P:(k + 1) * P], src[:, r % 2, o:o + w], K["idn"][:])
                    last.then_inc(s("job"), 1)
                elif kind in ("row", "v") and j[1] not in ("uq", "uk"):
                    c, t = j[1], j[2]
                    pe.wait_ge(s("h_low"), 2 * t + 2)
                    n = cols[c][1]
                    tok = slice(t * P, (t + 1) * P)
                    for k in range(KD):
                        if j == pos[c][0]:
                            landed(c, k)
                        w = piece_of[c, k] % WR
                        last = three_passes(nc, bank[:, 0:n], (hh[:, k, tok], hl[:, k, tok]),
                                            (wh[:, w, 0:n], wl[:, w, 0:n]), k == 0, k == KD - 1)
                    last.then_inc(s("job"), 1)
                elif kind == "gate":
                    _, c, jj, a, n = j
                    for k in range(KD):
                        if j == pos[c][0]:
                            landed(c, k)
                        w = piece_of[c, k] % WR
                        cs = slice(jj * P, (jj + 1) * P)
                        last = three_passes(nc, bank[:, 0:n], (wh[:, w, cs], wl[:, w, cs]),
                                            (hh[:, k, a:a + n], hl[:, k, a:a + n]), k == 0, k == KD - 1)
                    last.then_inc(s("job"), 1)
                else:
                    c, t, part = j[1:]
                    if c == "uq" and part == 0:
                        pe.wait_ge(s("c_split"), t + 1)
                    if t == 0:
                        landed("u", 5)
                    ks = (0, 1) if c == "uq" else (2,)
                    n = 384 if c == "uq" else 512
                    for k in ks:
                        w = piece_of["u", 2 * k + part] % WR
                        last = three_passes(nc, bank[:, 0:n], (chh[:, t % 2, k * P:(k + 1) * P], cll[:, t % 2, k * P:(k + 1) * P]),
                                            (wh[:, w, 0:n], wl[:, w, 0:n]), k == ks[0], k == ks[-1])
                    last.then_inc(s("job"), 1)



class Unit:

    def __init__(self, it, s, R, kv=None):
        self.it, self.s, self.R, self.kv = it, s, R, kv

    def value(self, a, c=0, per=1):
        return self.it * (a * self.R // per) + (a * (self.s // per) + c)

    def next(self, kv=None):
        return Unit(self.it, self.s + 1, self.R, kv)

    def wait(self, eng, sem, a, c=0, per=1):
        v = self.value(a, c, per)
        if not isinstance(v, int) or v > 0:
            eng.wait_ge(sem, v)


ORDER = {
    "A": {
        "tensor":
            "S0 T0 T1 S1 P0 T2 T3 S2 T4 P1 S3 T5 T6 S4 P2 T7 P3 P4 P5 T8 T9 P6 P7 P8 P9",
        "scalar":
            "T0 T1 E0a E0b T2 T3 E1 T4 E2 T5 E3 T6 T7 E4 Za T8 T9 O",
        "vector":
            "M0 T0 T1 M1 T2 T3 M2 T4 M3 T5 M4 T6 Za T7 Zb T8 T9 O",
        "gpsimd": "N1 N2 N3 N4 N0",
    },
    "B": {
        "tensor":
            "S0 S1 T0 T1 S2 S3 T2 T3 S4 S5 P0 P1 S6 T4 P2 S7 T5 S8 P3 T6 S9 T7 P4 P5 T8 P6 T9 P7 "
            "P8 P9",
        "scalar":
            "T0 T1 E0a E0b E1 E2 E3 T2 T3 E4 E5a E5b T4 E6 T5 E7 T6 E8 T7 E9 Za T8 T9 O",
        "vector":
            "M0 M1 N1 T0 T1 M2 M3 N2 M4 M5 T2 T3 M6 M7 T4 M8 T5 M9 T6 Za T7 Zb T8 T9 N0",
        "gpsimd": "N1 N2 N3 N4 N0",
    },
    "C": {
        "tensor":
            "S0 T0 T1 S1 T2 P0 T3 S2 T4 S3 P1 T5 T6 S4 P2 T7 P3 P4 T8 P5 T9 P6 P7 P8 P9",
        "scalar":
            "T0 T1 E0a E0b T2 E1 T3 T4 E2 T5 T6 E3 T7 E4 T8 Za T9 O",
        "vector":
            "M0 T0 T1 M1 T2 M2 T3 T4 M3 T5 M4 Za T6 T7 T8 Zb T9",
        "gpsimd": "N1 N2 N3 N4 N0",
    },
}


CONTEXT_ORDER = {
    "A": "S0 M0 T0 E0 T1 Zb N0 P0 P1 O",
    "B": "S0 M0 T0 E0 S1 M1 T1 E1 Zb P0 N0 P1 O",
}


class Plan:

    def __init__(self, kind, layer, ctx_queries):
        self.kind, self.ctx = kind, ctx_queries
        self.maps = 2 if kind == "B" else 1
        self.rows = A_QK if kind == "A" else P
        self.queries = CTX if ctx_queries else 512
        self.keys = CTX if ctx_queries else TOK
        self.QT, self.KT = self.queries // P, self.keys // P
        self.SEG = self.keys // 256
        heads = {"A": A_HEADS, "B": B_HEADS, "C": C_HEADS}[kind]
        self.per_head = 1 if ctx_queries else 2
        self.units = heads * self.per_head
        self.R = self.units if ctx_queries else 2 if kind == "C" else 4
        self.QS = self.KS = self.units if ctx_queries else 2
        self.ring = 4 if ctx_queries else 5
        if ctx_queries:
            self.chunks = [([(q, 0, 256) for q in range(2)], 0)]
            self.NC = 1
        else:
            self.chunks = [([(q, 1024, 256) for q in range(4)], 1)] + [([(q, 0, 1024)], 0) for q in range(4)]
            self.NC = 2
        self.C = len(self.chunks) * self.maps
        self.dve_segs = (self.SEG if ctx_queries else 3) if self.maps == 2 else self.SEG if ctx_queries else 0
        self.turn_bank = [0 if ctx_queries else kt % 2 for kt in range(self.KT)]
        self.turn_free = []
        for i, b in enumerate(self.turn_bank):
            before = [k - self.KT for k, c in enumerate(self.turn_bank) if c == b]
            before += [k for k, c in enumerate(self.turn_bank[:i]) if c == b]
            self.turn_free.append(before[-1] + 1)
        self.out_banks = 1 if ctx_queries else 2
        self.stat_parts = (0, 1) if self.NC > 1 else (1,)
        self.fused_segs = 1
        self.pool_adds = (3, 4) if self.maps == 2 and not ctx_queries else ()

    def engine_parts(self, engine, has_next):
        names = {"P": "PV", "Z": "STAT", "O": "OUT"}
        out = []
        order = CONTEXT_ORDER[self.kind] if self.ctx else ORDER[self.kind][engine]
        for word in order.split():
            what, digits = word[0], "".join(c for c in word if c.isdigit())
            half = "ab".index(word[-1]) if word[-1] in "ab" else None
            of_next = what in "SMEZ" or word == "N0"
            if of_next and not has_next:
                continue
            if what == "Z":
                out.append(("STAT", half))
            elif word == "N0":
                out.append(("N0", 0))
            else:
                part = (names.get(what, what), int(digits or 0))
                out.append(part if half is None else part + (half,))
        return out

    def walk(self, eng):
        R, n = self.R, self.units // self.R
        if self.kind == "C":
            segs = [(0, 1, False), (1, 3, True), (3, 4, False), (4, 7, True), (7, 8, False)]
        elif n > 2:
            segs = [(0, 1, False), (1, n - 1, True), (n - 1, n, False)]
        else:
            segs = [(0, n, False)]

        def kv(it0, s):
            return (it0 * R + s) // (R * n // 2) if self.kind == "C" else (s // self.per_head) % self.KS

        for a, b, loop in segs:
            if loop:
                with eng.Fori(a, b) as it:
                    for s in range(R):
                        u = Unit(it, s, R, kv(a, s))
                        yield u, u.next(kv(a, s + 1) if self.kind != "C" else kv(a, s))
            else:
                for it in range(a, b):
                    for s in range(R):
                        u = Unit(it, s, R, kv(it, s))
                        yield u, None if it == n - 1 and s == R - 1 else u.next(kv(it, s + 1))


def attention_programs(nc, A, K, PS, early, early_sem, kind, layer, ctx_queries, bank0):
    pl = Plan(kind, layer, ctx_queries)
    L = f"{kind}{int(ctx_queries)}_"
    QN, QT, KT, C, NC, maps, ring = pl.queries, pl.QT, pl.KT, pl.C, pl.NC, pl.maps, pl.ring
    rows = pl.rows
    packed = kind == "A"
    n_kv = {"A": A_HEADS, "B": B_HEADS, "C": C_KV}[kind]
    nch = len(pl.chunks)
    stack, new_sem = early, early_sem

    def sb(name, shape, dt=F32):
        return stack.enter_context(nc.sbuf_tensor(L + name, shape, dt))

    S = {}

    def s(name):
        if name not in S:
            S[name] = new_sem(L + name)
        return S[name]

    qh = sb("q_hi", [rows, pl.QS, maps, QN], F32R)
    ql = sb("q_lo", [rows, pl.QS, maps, QN], F32R)
    kh = sb("k_hi", [rows, pl.KS, maps, pl.keys], F32R)
    kl = None if kind == "B" else sb("k_lo", [rows, pl.KS, maps, pl.keys], F32R)
    vh = sb("v_hi", [P, pl.KS, KT, P], F32R)
    vl = None if packed else sb("v_lo", [P, pl.KS, KT, P], F32R)
    vrows = A_V if packed else P
    tok0 = 0 if ctx_queries else CTX
    base_q = 0 if kind == "C" else tok0
    n_qdma = 4 if kind == "B" else 2
    n_kdma = 2
    n_vdma = 2 * KT if ctx_queries else 2
    out_row0 = A_WIDTH if kind == "B" else 0
    out_col0 = 0 if kind == "C" else tok0

    def q_head(u):
        return u.value(1, 0, pl.per_head)

    def load_q(sp, u):
        sl = u.s % pl.QS
        h = q_head(u)
        c0 = base_q + (0 if ctx_queries else 512 * (u.s % 2))
        cs = slice(c0, c0 + QN)
        q_in = s(f"q_in{sl}")
        for half, dst in (("h", qh), ("l", ql)):
            if kind == "A":
                sp.dma_start(dst[:, sl, 0, :].bitcast(F32), A["qkA" + half][bass.ds(h, 1), :, cs].rearrange("a p n -> (a p) n"))\
                    .then_inc(q_in, 16)
            elif kind == "C":
                sp.dma_start(dst[:, sl, 0, :].bitcast(F32), A["qC" + half][bass.ds(h, 1), :, cs].rearrange("a p n -> (a p) n"))\
                    .then_inc(q_in, 16)
            else:
                for up in range(2):
                    src = A["qkB" + half][0, bass.ds(h, 1), :, cs]
                    sp.dma_start(dst[up * B_D:(up + 1) * B_D, sl, :, :].bitcast(F32),
                                 src.rearrange("a (m p) n -> p (a m) n", m=2)).then_inc(q_in, 16)

    def load_kv(sp, h, sl):
        k_in, v_in = s(f"k_in{sl}"), s(f"v_in{sl}")
        ks = slice(0, pl.keys)
        if kind == "A":
            for half, dst in (("h", kh), ("l", kl)):
                sp.dma_start(dst[:, sl, 0, :].bitcast(F32), A["qkA" + half][bass.ds(h + A_HEADS, 1), :, ks].rearrange("a p n -> (a p) n"))\
                    .then_inc(k_in, 16)
            for i, half in enumerate("hl"):
                sp.dma_start(vh[:, sl, :, i * A_V:(i + 1) * A_V].bitcast(F32),
                             A["vA" + half].rearrange("(k p) (h n) -> p k h n", p=P, h=A_HEADS)[:, 0:KT, bass.ds(h, 1), :]
                             .rearrange("p k a n -> p k (a n)")).then_inc(v_in, 16)
        else:
            if kind == "C":
                for half, dst in (("h", kh), ("l", kl)):
                    sp.dma_start(dst[:, sl, 0, :].bitcast(F32), A["kC" + half][h, :, ks]).then_inc(k_in, 16)
            else:
                for up, half in enumerate("hl"):
                    src = A["qkB" + half][1, bass.ds(h, 1), :, ks]
                    sp.dma_start(kh[up * B_D:(up + 1) * B_D, sl, :, :].bitcast(F32),
                                 src.rearrange("a (m p) n -> p (a m) n", m=2)).then_inc(k_in, 16)
            nh = C_KV if kind == "C" else B_HEADS
            for half, dst in (("h", vh), ("l", vl)):
                sp.dma_start(dst[:, sl, :, :].bitcast(F32),
                             A["v" + kind + half].rearrange("(k p) (h n) -> p k h n", p=P, h=nh)[:, 0:KT, bass.ds(h, 1), :]
                             .rearrange("p k a n -> p k (a n)")).then_inc(v_in, 16)


    def load_context(sp):
        cs = slice(0, CTX)
        for i, half in enumerate("hl"):
            if kind == "A":
                rows_of = A["qkA" + half].rearrange("h p n -> p h n")
                sp.dma_start((qh, ql)[i][:, :, 0, :].bitcast(F32), rows_of[:, 0:A_HEADS, cs]).then_inc(s("q_in"), 16)
                sp.dma_start((kh, kl)[i][:, :, 0, :].bitcast(F32), rows_of[:, A_HEADS:, cs]).then_inc(s("k_in"), 16)
            else:
                q_of, k_of = (A["qkB" + half][j].rearrange("h (m p) n -> p (h m) n", m=2)[:, :, cs] for j in range(2))
                for up in range(2):
                    sp.dma_start((qh, ql)[i][up * B_D:(up + 1) * B_D].rearrange("p s m n -> p (s m) n").bitcast(F32),
                                 q_of).then_inc(s("q_in"), 16)
                sp.dma_start(kh[i * B_D:(i + 1) * B_D].rearrange("p s m n -> p (s m) n").bitcast(F32), k_of)\
                    .then_inc(s("k_in"), 16)
            for k in range(KT):
                v_of = A["v" + kind + half][k * P:(k + 1) * P, :].rearrange("p (h n) -> p h n", h=n_kv)
                dst = vh[:, :, k, i * A_V:(i + 1) * A_V] if packed else (vh, vl)[i][:, :, k, :]
                sp.dma_start(dst.bitcast(F32), v_of).then_inc(s("v_in"), 16)

    def first_loads(sp):
        if ctx_queries:
            load_context(sp)
            return
        for n in range(min(pl.KS, n_kv)):
            if n == 0:
                load_q(sp, Unit(0, 0, pl.R))
            load_kv(sp, n, n)
        for n in range(1, pl.QS):
            load_q(sp, Unit(0, n, pl.R))

    for slot in ("",) if ctx_queries else range(2):
        s(f"q_in{slot}")
        s(f"k_in{slot}")
        s(f"v_in{slot}")
    stack, new_sem = yield first_loads

    prob = sb("prob", [P, 2, maps, QT, pl.keys])
    th = sb("probT_hi", [P, ring, QN], F32R)
    tl = sb("probT_lo", [P, ring, QN], F32R)
    nm = sb("neg_max", [P, 2, maps, QT, NC])
    rs = sb("row_sum", [P, 2, maps, QT, NC])
    fc = sb("factor", [P, 2, maps, QT, NC])
    gn = sb("neg_max_all", [P, maps * QT])
    den = sb("denominator", [P, maps * QT])
    low = sb("out_low", [A_V, QN]) if packed else None
    od = sb("out_rows", [P, 2, QN])
    sw = 1 if ctx_queries else 2
    sc = [PS[:, bank0 + sw * b:bank0 + sw * (b + 1), :].rearrange("p a n -> p (a n)") for b in range(2)]
    tbank = [PS[:, bank0 + 2 * sw + pl.turn_bank[i], :] for i in range(KT)]
    obank = [PS[:, bank0 + (3 if ctx_queries else 6) + b % pl.out_banks, :] for b in range(2)]

    def wait_q(eng, u):
        if ctx_queries:
            eng.wait_ge(s("q_in"), 16 * n_qdma)
            return
        eng.wait_ge(s(f"q_in{u.s % pl.QS}"), u.value(16 * n_qdma, 16 * n_qdma, pl.QS))

    def wait_kv(eng, u, name, dmas):
        if ctx_queries:
            eng.wait_ge(s(name), 16 * dmas)
        elif kind == "C":
            eng.wait_ge(s(f"{name}{u.kv}"), 16 * dmas)
        else:
            eng.wait_ge(s(f"{name}{u.kv}"), u.value(16 * dmas, 16 * dmas, pl.per_head * pl.KS))

    def sync_program(sp):
        def store(u):
            u.wait(sp, s("o_out"), 1, 1)
            h = q_head(u)
            c0 = out_col0 + (0 if ctx_queries else 512 * (u.s % 2))
            dst = A[f"oT{layer}"].rearrange("(h n) t -> h n t", n=vrows)[bass.ds(h + out_row0 // vrows, 1), :, c0:c0 + QN]
            sp.dma_start(dst.rearrange("a n t -> (a n) t"), od[0:vrows, u.s % 2, :]).then_inc(s(f"o_st{u.s % 2}"), 16)

        def loads(u):
            v = Unit(u.it, u.s + pl.QS, pl.R)
            known = isinstance(u.it, int)
            if not known or u.it * pl.R + u.s + pl.QS < pl.units:
                u.wait(sp, s("scored"), C, C)
                load_q(sp, v)
            if kind != "C" and u.s % pl.per_head == 0:
                h1 = u.value(1, pl.KS - 1, pl.per_head)
                first = known and u.it == 0 and u.s == 0
                if not first and (not known or h1 < n_kv):
                    u.wait(sp, s("multiplied"), KT, 0)
                    load_kv(sp, h1, (u.s // pl.per_head + pl.KS - 1) % pl.KS)

        for u, nxt in pl.walk(sp):
            if not ctx_queries:
                loads(u)
            store(u)
            yield
        for b in range(2):
            sp.wait_ge(s(f"o_st{b}"), 16 * (pl.units // 2))

    def probs_of(u, m, q, k0, n):
        return prob[:, u.s % 2, m, q, k0:k0 + n]

    def chunk_views(buf, pieces):
        n = pieces[0][2]
        return [(q, k0, n, buf[:, i * n:(i + 1) * n]) for i, (q, k0, n) in enumerate(pieces)]

    def both(eng, name, step):
        first = Unit(0, 0, pl.R, 0)
        for j in range(C):
            for part in ("S", "M", "E"):
                step(None, first, (part, j))
                yield False
        for p in pl.stat_parts:
            step(None, first, ("STAT", p))
        step(None, first, ("N0", 0))
        yield True
        for u, nxt in pl.walk(eng):
            for part in pl.engine_parts(name, nxt is not None):
                step(u, nxt, part)
                yield False
            yield True

    def tensor_program(pe):
        def step(u, nxt, part):
            what, i = part[:2]
            if what == "S":
                m, jj = divmod(i, nch)
                pieces, _ = pl.chunks[jj]
                if i == 0:
                    wait_q(pe, nxt)
                    wait_kv(pe, nxt, "k_in", n_kdma)
                nxt.wait(pe, s("exped"), C, i - 1)
                buf = sc[(nxt.s * C + i) % 2]
                sl = nxt.s % pl.QS
                for q, k0, n, view in chunk_views(buf, pieces):
                    qs = slice(q * P, (q + 1) * P)
                    for o in range(0, n, 512):
                        w = min(512, n - o)
                        ks = slice(k0 + o, k0 + o + w)
                        out = view[:, o:o + w]
                        if kind == "B":
                            nc.tensor.matmul(out, ql[:, sl, m, qs], kh[:, nxt.kv, m, ks], start=True, stop=False)
                            last = nc.tensor.matmul(out, qh[:, sl, m, qs], kh[:, nxt.kv, m, ks], start=False, stop=True)
                        else:
                            last = three_passes(nc, out, (qh[:, sl, 0, qs], ql[:, sl, 0, qs]),
                                                (kh[:, nxt.kv, 0, ks], kl[:, nxt.kv, 0, ks]), True, True)
                last.then_inc(s("scored"), 1)
            elif what == "T":
                seg = i // 2
                if seg in pl.pool_adds:
                    u.wait(pe, s("added_pool"), len(pl.pool_adds), pl.pool_adds.index(seg) + 1)
                elif seg < pl.dve_segs:
                    u.wait(pe, s("norm_dve"), pl.dve_segs, seg + 1)
                else:
                    u.wait(pe, s("norm_pool"), pl.SEG - pl.dve_segs, seg - pl.dve_segs + 1)
                u.wait(pe, s("split"), KT, pl.turn_free[i])
                bank = tbank[i]
                for q in range(QT):
                    last = nc.tensor.transpose(bank[:, q * P:(q + 1) * P], probs_of(u, 0, q, i * P, P), K["idn"][:])
                last.then_inc(s("turned"), 1)
            elif what == "PV":
                u.wait(pe, s("split"), KT, i + 1)
                if i == 0:
                    wait_kv(pe, u, "v_in", n_vdma)
                    u.wait(pe, s("o_out"), 1, 1 - pl.out_banks)
                r = (u.s * KT + i) % ring
                out = obank[u.s % 2][:, 0:QN]
                if packed:
                    def full():
                        return nc.tensor.matmul(out, vh[:, u.kv, i, :], th[:, r, :], start=i == 0, stop=i == KT - 1)

                    def top():
                        return nc.tensor.matmul(out[0:A_V], vh[:, u.kv, i, 0:A_V], tl[:, r, :], start=False, stop=False)

                    if i == 0:
                        full()
                        last = top()
                    else:
                        top()
                        last = full()
                else:
                    last = three_passes(nc, out, (vh[:, u.kv, i, :], vl[:, u.kv, i, :]), (th[:, r, :], tl[:, r, :]),
                                        i == 0, i == KT - 1)
                last.then_inc(s("multiplied"), 1)

        yield from both(pe, "tensor", step)

    def scalar_program(act):
        def step(u, nxt, part):
            what, i = part[:2]
            if what == "E":
                m, jj = divmod(i, nch)
                pieces, c = pl.chunks[jj]
                if i == 0:
                    nxt.wait(act, s("turned"), KT, -KT)
                nxt.wait(act, s("maxed"), C, i + 1)
                b = nxt.s % 2
                views = chunk_views(sc[(nxt.s * C + i) % 2], pieces)
                half = part[2] if len(part) > 2 else None
                if half is not None:
                    views = views[2 * half:2 * half + 2]
                for q, k0, n, view in views:
                    last = nc.scalar.activation(probs_of(nxt, m, q, k0, n), view, ACT.Exp,
                                                bias=nm[:, b, m, q, c:c + 1], accum_out=rs[:, b, m, q, c:c + 1])
                if half != 0:
                    last.then_inc(s("exped"), 1)
            elif what == "T":
                u.wait(act, s("turned"), KT, i + 1)
                u.wait(act, s("multiplied"), KT, i + 1 - ring)
                r = (u.s * KT + i) % ring
                nc.scalar.activation(th[:, r, :], tbank[i][:, 0:QN], ACT.Copy).then_inc(s("high"), 1)
            elif what == "STAT" and i == 0:
                nxt.wait(act, s("diff"), 1, 1)
                b = nxt.s % 2
                f = fc[:, b].rearrange("p m q c -> p (m q c)")
                nc.scalar.activation(f, f, ACT.Exp).then_inc(s("diff_exp"), 1)
            elif what == "OUT":
                b = u.s % 2
                u.wait(act, s("multiplied"), KT, KT)
                if packed:
                    u.wait(act, s("o_out"), 1, 0)
                    nc.scalar.activation(low[:], obank[b][A_V:P, 0:QN], ACT.Copy).then_inc(s("o_low"), 1)
                else:
                    u.wait(act, s(f"o_st{b}"), 16, 0, 2)
                    nc.scalar.activation(od[:, b, :], obank[b][:, 0:QN], ACT.Copy).then_inc(s("o_out"), 1)

        yield from both(act, "scalar", step)

    def gpsimd_program(pool):
        def step(u, nxt, part):
            what, i = part[:2]
            if what == "N0":
                what, u = "N", nxt
            if what == "N":
                c = min(i // 4, NC - 1)
                if maps == 1 and i < pl.dve_segs:
                    return
                if i == (0 if maps == 2 else pl.dve_segs):
                    u.wait(pool, s("factors"), 1, 1)
                    pool.sem_inc(s("pool_went_on"), 1)
                for q in range(QT):
                    for m in range(maps if i >= pl.fused_segs else 1):
                        v = probs_of(u, m, q, 256 * i, 256)
                        last = nc.gpsimd.tensor_scalar(v, v, fc[:, u.s % 2, m, q, c:c + 1], 1.0, ALU.mult, ALU.mult)
                last.then_inc(s("norm_pool"), 1)
                if i in pl.pool_adds:
                    u.wait(pool, s("norm_pool"), pl.SEG, i + 1)
                    v0, v1 = (prob[:, u.s % 2, m, :, 256 * i:256 * i + 256] for m in range(2))
                    nc.gpsimd.tensor_tensor(v0, v0, v1, ALU.add).then_inc(s("added_pool"), 1)

        yield from both(pool, "gpsimd", step)

    def vector_program(dve):
        per = (4 if NC > 1 else 0) + (maps - 1)

        def step(u, nxt, part):
            what, i = part[:2]
            if what == "M":
                m, jj = divmod(i, nch)
                pieces, c = pl.chunks[jj]
                nxt.wait(dve, s("scored"), C, i + 1)
                n = pieces[0][2]
                view = sc[(nxt.s * C + i) % 2][:, 0:n * len(pieces)].rearrange("p (q n) -> p q n", n=n)
                q0 = pieces[0][0]
                nc.vector.tensor_reduce(nm[:, nxt.s % 2, m, q0:q0 + len(pieces), c], view, AX, ALU.max,
                                        negate=True).then_inc(s("maxed"), 1)
            elif what == "T":
                u.wait(dve, s("high"), KT, i + 1)
                r = (u.s * KT + i) % ring
                nc.vector.tensor_tensor(tl[:, r, :], tbank[i][:, 0:QN], th[:, r, :].bitcast(F32),
                                        ALU.subtract).then_inc(s("split"), 1)
            elif what in ("N", "N0"):
                if what == "N0":
                    u = nxt
                c = min(i // 4, NC - 1)
                if i >= pl.dve_segs:
                    return
                if i == 0:
                    u.wait(dve, s("factors"), 1, 1)
                if maps == 2:
                    u.wait(dve, s("norm_pool"), pl.SEG, i + 1)
                if maps == 2 and i >= pl.fused_segs:
                    v0, v1 = (prob[:, u.s % 2, m, :, 256 * i:256 * i + 256] for m in range(2))
                    nc.vector.tensor_tensor(v0, v0, v1, ALU.add).then_inc(s("norm_dve"), 1)
                    return
                for q in range(QT):
                    v = probs_of(u, 0, q, 256 * i, 256)
                    if maps == 2:
                        last = nc.vector.scalar_tensor_tensor(v, probs_of(u, 1, q, 256 * i, 256),
                                                              fc[:, u.s % 2, 1, q, c:c + 1], v, ALU.mult, ALU.add)
                    else:
                        last = nc.vector.tensor_scalar(v, v, fc[:, u.s % 2, 0, q, c:c + 1], None, ALU.mult)
                last.then_inc(s("norm_dve"), 1)
            elif what == "STAT":
                b = nxt.s % 2
                k = [1 if i == 1 and NC > 1 else 0]

                def link(ins):
                    k[0] += 1
                    ins.then_inc(s("chain"), 1)
                    nxt.wait(dve, s("chain"), per, k[0])

                flat = [t[:, b].rearrange("p m q c -> p (m q) c") for t in (nm, rs, fc)]
                mq = maps * QT
                if i == 0:
                    nxt.wait(dve, s("maxed"), C, C)
                    link(nc.vector.tensor_reduce(gn[:], flat[0], AX, ALU.min))
                    nc.vector.tensor_tensor(flat[2], gn[:].unsqueeze(2).to_broadcast([P, mq, NC]), flat[0],
                                            ALU.subtract).then_inc(s("diff"), 1)
                    return
                nxt.wait(dve, s("exped"), C, C)
                if NC > 1:
                    nxt.wait(dve, s("diff_exp"), 1, 1)
                    link(nc.vector.tensor_tensor(flat[1], flat[1], flat[2], ALU.mult))
                    link(nc.vector.tensor_reduce(den[:], flat[1], AX, ALU.add))
                    link(nc.vector.reciprocal(den[:], den[:]))
                    last = nc.vector.tensor_tensor(flat[2], flat[2], den[:].unsqueeze(2).to_broadcast([P, mq, NC]),
                                                   ALU.mult)
                else:
                    last = nc.vector.reciprocal(flat[2], flat[1])
                if maps == 2:
                    link(last)
                    f1 = fc[:, b, 1].rearrange("p q c -> p (q c)")
                    last = nc.vector.tensor_scalar(f1, f1, K["neglam"][:], None, ALU.mult)
                last.then_inc(s("factors"), 1)
                assert k[0] == per, (k, per)
            elif what == "OUT" and packed:
                b = u.s % 2
                u.wait(dve, s("o_low"), 1, 1)
                u.wait(dve, s(f"o_st{b}"), 16, 0, 2)
                nc.vector.tensor_tensor(od[0:A_V, b, :], obank[b][0:A_V, 0:QN], low[:], ALU.add)\
                    .then_inc(s("o_out"), 1)

        yield from both(dve, "vector", step)

    yield dict(sync=sync_program, tensor=tensor_program, scalar=scalar_program, gpsimd=gpsimd_program,
               vector=vector_program)


def attention(nc, sem, prepared, loads, next_loads=()):
    with ExitStack() as ctx:
        prog = prepared.send((ctx, sem))
        block = ctx.enter_context(nc.Block())

        def run(name):
            def whole(eng):
                for _ in prog[name](eng):
                    pass
            return whole

        @block.sync
        def _(sp):
            for load in tuple(loads) + tuple(next_loads):
                load(sp)
            for _ in prog["sync"](sp):
                pass

        block.tensor(run("tensor"))
        block.scalar(run("scalar"))
        block.gpsimd(run("gpsimd"))
        block.vector(run("vector"))


def context_attention(nc, sem, prepared_b, prepared_a):
    with ExitStack() as ctx:
        prog_b, prog_a = prepared_b.send((ctx, sem)), prepared_a.send((ctx, sem))
        block = ctx.enter_context(nc.Block())

        def run(name):
            def merged(eng):
                b, a = prog_b[name](eng), prog_a[name](eng)
                open_b = open_a = True
                while open_b or open_a:
                    open_b = open_b and not next(b)
                    open_a = open_a and not next(a)
                for _ in range(B_HEADS):
                    open_b, left_a = True, A_HEADS // B_HEADS
                    while open_b or left_a:
                        open_b = open_b and not next(b)
                        if left_a:
                            left_a -= next(a)
                for rest in (b, a):
                    for _ in rest:
                        pass
            return merged

        @block.sync
        def _(sp):
            b, a = prog_b["sync"](sp), prog_a["sync"](sp)
            for _ in range(B_HEADS):
                next(b)
                for _ in range(A_HEADS // B_HEADS):
                    next(a)
            for rest in (b, a):
                for _ in rest:
                    pass

        block.tensor(run("tensor"))
        block.scalar(run("scalar"))
        block.gpsimd(run("gpsimd"))
        block.vector(run("vector"))



def out_project(nc, A, K, PS, early, early_sem, layer, out):
    L = f"o{layer}_"
    tiles = NT if layer == 0 else NT - NCT
    R = 2
    n_out = tiles * P
    w_out = A["e_w_out"] if layer == 0 else A["o_w_out"]
    KB = A_WIDTH // P
    raw = early.enter_context(nc.sbuf_tensor(L + "raw", [P, KD, D], F32))
    raw_in = [early_sem(f"{L}raw{k}") for k in range(KD)]

    def load_weights(sp, pieces=range(KD)):
        for k in pieces:
            sp.dma_start(raw[:, k, :], w_out[0, k * P:(k + 1) * P, :]).then_inc(raw_in[k], 16)

    sem, loaded = yield load_weights
    with ExitStack() as ctx:
        def sb(name, shape, dt=F32):
            return ctx.enter_context(nc.sbuf_tensor(L + name, shape, dt))

        S = {}

        def s(name):
            if name not in S:
                S[name] = sem(L + name)
            return S[name]

        wh = sb("w_hi", [P, KD, D], F32R)
        wl = sb("w_lo", [P, KD, D], F32R)
        o = sb("o", [P, 2, KD, P])
        g = sb("g", [P, 2, KD, P])
        y = sb("y", [P, KD, P])
        yh = sb("y_hi", [P, 2, KD, P], F32R)
        yl = sb("y_lo", [P, 2, KD, P], F32R)
        xt = sb("x", [P, 2, D])
        res = sb("res", [P, 2, D])
        gb = sb("gate_rows", [P, 2, D])
        if layer == 0:
            ob = sb("o_b", [P, B_HEADS, n_out])
            sq = sb("o_sq", [P, 2, n_out])
            ones = sb("ones", [P, P])
            var = sb("b_var", [P, NT, B_HEADS])
            rstd = sb("b_rstd", [P, NT, B_HEADS])
            diag = sb("b_diag", [P, B_HEADS, P])
            gout = sb("b_gain", [P, 1])
            VAR = PS[:, 5, 0:NT * B_HEADS].rearrange("p (t h) -> p t h", h=B_HEADS)
        block = ctx.enter_context(nc.Block())

        def walk(eng):
            n = tiles // R
            for a, b, loop in [(0, 2, False), (2, n - 1, True), (n - 1, n, False)] if layer == 0 else \
                    [(0, 1, False), (1, n - 1, True), (n - 1, n, False)]:
                if loop:
                    with eng.Fori(a, b) as it:
                        for q in range(R):
                            yield Unit(it, q, R), Unit(it, q - 1, R), Unit(it, q + 1, R)
                else:
                    for it in range(a, b):
                        for q in range(R):
                            yield (Unit(it, q, R), Unit(it, q - 1, R) if it or q else None,
                                   Unit(it, q + 1, R) if it < n - 1 or q < R - 1 else None)

        last_tiles = [Unit(tiles // R - 1, q, R) for q in range(R)]

        def side(u):
            return 0 if layer == 0 and isinstance(u.it, int) and u.it * R + u.s < NCT else 1

        @block.sync
        def _(sp):
            def store(u):
                u.wait(sp, s("added"), 1, 1)
                sp.dma_start(out[bass.ds(u.value(P, 0), P), :], res[:, u.s % 2]).then_inc(s(f"st{u.s % 2}"), 16)

            def load(u):
                b = u.s % 2
                tok = u.value(P, 0)
                u.wait(sp, s("y_made"), 1, -1)
                sp.dma_start(o[:, b], A[f"oT{layer}"].rearrange("(k p) t -> p k t", p=P)[:, :, bass.ds(tok, P)])\
                    .then_inc(s(f"in{b}"), 16)
                sp.dma_start(g[:, b], A[f"gateT{layer}"].rearrange("(k p) t -> p k t", p=P)[:, :, bass.ds(tok, P)])\
                    .then_inc(s(f"in{b}"), 16)
                if not (isinstance(u.it, int) and u.it == 0):
                    store(Unit(u.it, u.s - 2, R))
                if layer == 0:
                    if side(u) == 0:
                        src = A["x0c"][u.s * P:(u.s + 1) * P, :]
                    else:
                        src = A["x0l"][bass.ds(u.value(P, -CTX), P), :]
                else:
                    src = A["x1"][bass.ds(u.value(P, CTX), P), :]
                sp.dma_start(xt[:, b], src).then_inc(s(f"x_in{b}"), 16)

            if layer == 0:
                for h in range(B_HEADS):
                    sp.dma_start(ob[:, h, :], A["oT0"][A_WIDTH + h * P:A_WIDTH + (h + 1) * P, :])\
                        .then_inc(s(f"b_in{h}"), 16)
            if not loaded:
                load_weights(sp, range(0, 4))
            load(Unit(0, 0, R))
            if layer == 0:
                sp.dma_start(gout[:], A["b_g_out"][0, :].rearrange("(p a) -> p a", a=1),
                             allow_slow_non_contiguous=True).then_inc(s("b_gain"), 16)
            if not loaded:
                load_weights(sp, range(4, KD))
            load(Unit(0, 1, R))
            for side_ in range(2):
                sp.dma_start(gb[:, side_], A["grow"][layer, side_, :].partition_broadcast(P)).then_inc(s("gate_in"), 16)

            for u, _, _ in walk(sp):
                if not (isinstance(u.it, int) and u.it == 0):
                    load(u)
            for u in last_tiles:
                store(u)
            for b in range(2):
                sp.wait_ge(s(f"st{b}"), 16 * (tiles // 2))

        @block.gpsimd
        def _(pool):
            def add(u):
                b = u.s % 2
                u.wait(pool, s(f"x_in{b}"), 16, 16, 2)
                u.wait(pool, s("gated"), 1, 1)
                nc.gpsimd.tensor_tensor(res[:, b], res[:, b], xt[:, b], ALU.add).then_inc(s("added"), 1)

            if layer == 0:
                nc.gpsimd.memset(ones[:], 1.0).then_inc(s("ones"), 1)
            for u, prev, _ in walk(pool):
                if prev is not None:
                    add(prev)
            add(last_tiles[-1])

        @block.scalar
        def _(act):
            if layer == 0:
                for h in range(B_HEADS):
                    act.wait_ge(s(f"b_in{h}"), 16)
                    if h >= 2:
                        act.wait_ge(s("sq_sum"), h - 1)
                    nc.scalar.activation(sq[:, h % 2, :], ob[:, h, :], ACT.Square).then_inc(s("squared"), 1)

            def high_w(k):
                act.wait_ge(raw_in[k], 16)
                nc.scalar.activation(wh[:, k, :], raw[:, k, :], ACT.Copy).then_inc(s("w_high"), 1)

            for k in range(4):
                high_w(k)
            if layer == 0:
                act.wait_ge(s("var"), 1)
                nc.scalar.activation(var[:], var[:], ACT.Sqrt).then_inc(s("sd"), 1)
            for u, prev, _ in walk(act):
                b = u.s % 2
                u.wait(act, s(f"in{b}"), 32, 32, 2)
                nc.scalar.activation(g[:, b], g[:, b], ACT.Silu).then_inc(s("g_made"), 1)
                u.wait(act, s("y_raw"), 1, 1)
                u.wait(act, s("projected"), 1, -1)
                nc.scalar.activation(yh[:, b], y[:], ACT.Copy).then_inc(s("y_high"), 1)
                if prev is None:
                    for k in range(4, KD):
                        high_w(k)

        @block.vector
        def _(dve):
            def low_w(k):
                dve.wait_ge(s("w_high"), k + 1)
                nc.vector.tensor_tensor(wl[:, k, :], raw[:, k, :], wh[:, k, :].bitcast(F32), ALU.subtract)\
                    .then_inc(s("w_split"), 1)

            def make_diag(u):
                if layer == 0:
                    u.wait(dve, s("spread"), 1, 0)
                    nc.vector.tensor_tensor(diag[:], K["idn"][:].unsqueeze(1).to_broadcast([P, B_HEADS, P]),
                                            rstd[:, bass.ds(u.value(1, 0), 1), :].rearrange("p a h -> p (a h)")
                                            .unsqueeze(2).to_broadcast([P, B_HEADS, P]), ALU.mult)\
                        .then_inc(s("diag"), 1)

            def finish(u):
                b = u.s % 2
                u.wait(dve, s("projected"), 1, 1)
                u.wait(dve, s(f"st{b}"), 16, 0, 2)
                nc.vector.tensor_tensor(res[:, b], PS[:, 2 * b:2 * b + 2, :].rearrange("p a n -> p (a n)"),
                                        gb[:, side(u)], ALU.mult).then_inc(s("gated"), 1)

            for k in range(4):
                low_w(k)
            if layer == 0:
                ch = Chain(nc, dve, s("chain"))
                dve.wait_ge(s("sq_sum"), B_HEADS)
                nc.vector.tensor_scalar(var[:], VAR, 1.0 / B_V, EPS, ALU.mult, ALU.add).then_inc(s("var"), 1)
                dve.wait_ge(s("sd"), 1)
                ch.link(nc.vector.reciprocal(rstd[:], var[:]))
                dve.wait_ge(s("b_gain"), 16)
                ch.link(nc.vector.tensor_scalar_mul(gout[:], gout[:], 1.0 - LAM_INIT))
            make_diag(Unit(0, 0, R))
            for u, prev, nxt in walk(dve):
                b = u.s % 2
                ov, yv, gv = o[:, b], y[:], g[:, b]
                u.wait(dve, s("g_made"), 1, 1)
                u.wait(dve, s("y_made"), 1, 0)
                if layer == 0:
                    nc.vector.tensor_tensor(yv[:, 0:KB], ov[:, 0:KB], gv[:, 0:KB], ALU.mult)
                    nc.vector.scalar_tensor_tensor(gv[:, KB:], ov[:, KB:], gout[:], gv[:, KB:], ALU.mult, ALU.mult)\
                        .then_inc(s("b_gated"), 1)
                    u.wait(dve, s("b_gated"), 1, 1)
                    u.wait(dve, s("spread"), 1, 1)
                    nc.vector.tensor_tensor(yv[:, KB:], gv[:, KB:], PS[:, 4, :].rearrange("p (h n) -> p h n", h=B_HEADS),
                                            ALU.mult).then_inc(s("y_raw"), 1)
                else:
                    nc.vector.tensor_tensor(yv, ov, gv, ALU.mult).then_inc(s("y_raw"), 1)
                u.wait(dve, s("y_high"), 1, 1)
                nc.vector.tensor_tensor(yl[:, b], yv, yh[:, b].bitcast(F32), ALU.subtract).then_inc(s("y_made"), 1)
                if nxt is not None:
                    make_diag(nxt)
                if prev is None:
                    for k in range(4, KD):
                        low_w(k)
                    dve.wait_ge(s("gate_in"), 32)
                else:
                    finish(prev)
            finish(last_tiles[-1])

        @block.tensor
        def _(pe):
            def spread(u):
                if layer == 0:
                    u.wait(pe, s("diag"), 1, 1)
                    u.wait(pe, s("y_raw"), 1, 0)
                    nc.tensor.matmul(PS[:, 4, :], ones[:], diag[:].rearrange("p h n -> p (h n)"),
                                     start=True, stop=True).then_inc(s("spread"), 1)

            if layer == 0:
                pe.wait_ge(s("ones"), 1)
                for h in range(B_HEADS):
                    pe.wait_ge(s("squared"), h + 1)
                    for t in range(NT):
                        last = nc.tensor.matmul(VAR[:, t, h:h + 1], sq[:, h % 2, t * P:(t + 1) * P], ones[:, 0:1],
                                                start=h == 0 and t == 0, stop=h == B_HEADS - 1 and t == NT - 1,
                                                skip_group_check=True)
                    last.then_inc(s("sq_sum"), 1)
            spread(Unit(0, 0, R))
            for u, prev, nxt in walk(pe):
                b = u.s % 2
                u.wait(pe, s("y_made"), 1, 1)
                u.wait(pe, s("gated"), 1, -1)
                for n in range(2):
                    for k in range(KD):
                        if prev is None and n == 0:
                            pe.wait_ge(s("w_split"), k + 1)
                        last = three_passes(nc, PS[:, 2 * b + n, :], (yh[:, b, k, :], yl[:, b, k, :]),
                                            (wh[:, k, n * 512:(n + 1) * 512], wl[:, k, n * 512:(n + 1) * 512]),
                                            k == 0, k == KD - 1)
                    if n == 0 and nxt is not None:
                        spread(nxt)
                last.then_inc(s("projected"), 1)
    yield



def trunk(nc, A, out):
    def scratch(name, shape, dt=F32):
        A[name] = nc.dram_tensor(name, shape, dt, kind="Internal").ap()

    for half in "hl":
        scratch("qkA" + half, (2 * A_HEADS, A_QK, TOK))
        scratch("vA" + half, (TOK, A_WIDTH))
        scratch("qkB" + half, (2, B_HEADS, P, TOK))
        scratch("vB" + half, (TOK, B_WIDTH))
        scratch("qC" + half, (C_HEADS, C_HD, LAT))
        scratch("kC" + half, (C_KV, C_HD, TOK))
        scratch("vC" + half, (TOK, C_KV * C_HD))
    scratch("tabA", (TOK, 2, 2, A_ROPE), F32)
    scratch("tabB", (TOK, 2, 2, B_D), F32)
    scratch("tabC", (TOK, 2, 2, C_HD), F32)
    scratch("cT", (3, P, TOK), F32)
    scratch("krow", (TOK, A_ROPE), F32)
    scratch("gateT0", (D, TOK), F32)
    scratch("gateT1", (D, LAT), F32)
    scratch("oT0", (D, TOK), F32)
    scratch("oT1", (D, LAT), F32)
    scratch("x1", (TOK, D), F32)
    scratch("grow", (2, 2, D), F32)
    A["x0c"], A["x0l"] = A["ctx"][0], A["x"][0]

    with ExitStack() as ctx:
        taken, kept = [], []

        def sem(name):
            taken.append(nc.alloc_semaphore(name=name))
            return taken[-1]

        def kept_sem(name):
            kept.append(nc.alloc_semaphore(name=name))
            return kept[-1]

        def join():
            nc.clear_and_free_semaphores(taken)
            nc.all_engine_barrier()
            taken[:] = kept
            kept.clear()

        K = {n: ctx.enter_context(nc.sbuf_tensor("k_" + n, shape, F32)) for n, shape in
             {"idn": [P, P], "cT": [P, 16], "neglam": [P, 1], "gcol": [P, 3], "gnope": [P, 2, A_NOPE],
              "modc": [P, 2, 2, KD, 2]}.items()}
        PS = ctx.enter_context(nc.psum_tensor("psum", [P, 8, 512], F32))
        def prepare(early, new_sem, kind, layer, ctx_queries, bank0=0):
            prepared = attention_programs(nc, A, K, PS, early, new_sem, kind, layer, ctx_queries, bank0)
            return prepared, next(prepared)

        project(nc, A, K, sem, PS, 0)
        join()
        with ExitStack() as early:
            mla, mla_loads = prepare(early, kept_sem, "A", 0, False)
            with ExitStack() as own:
                diff, diff_loads = prepare(own, sem, "B", 0, False)
                attention(nc, sem, diff, [diff_loads], [mla_loads])
                join()
            ctx_diff, ctx_diff_loads = prepare(early, kept_sem, "B", 0, True, 0)
            ctx_mla, ctx_mla_loads = prepare(early, kept_sem, "A", 0, True, 4)
            attention(nc, sem, mla, [], [ctx_diff_loads, ctx_mla_loads])
            join()
            context_attention(nc, sem, ctx_diff, ctx_mla)
            join()
        with ExitStack() as own:
            projection = out_project(nc, A, K, PS, own, sem, 0, A["x1"])
            next(projection)
            projection.send((sem, False))
            join()

        project(nc, A, K, sem, PS, 1)
        join()
        with ExitStack() as early:
            projection = out_project(nc, A, K, PS, early, kept_sem, 1, out)
            weight_loads = next(projection)
            with ExitStack() as own:
                gqa, gqa_loads = prepare(own, sem, "C", 1, False)
                attention(nc, sem, gqa, [gqa_loads], [weight_loads])
                join()
            projection.send((sem, True))
            join()


_INS = ["x", "c", "ctx", "c_ctx", "e_norm_g", "e_w_mod", "e_b_mod", "e_w_in", "a_g_cq", "a_w_uq", "a_g_ckv",
        "a_w_ukv", "a_g_qn", "a_g_kn", "b_g_qn", "b_g_kn", "b_lam_q1", "b_lam_k1", "b_lam_q2", "b_lam_k2",
        "b_g_out", "e_w_out", "o_norm_g", "o_w_mod", "o_b_mod", "o_w_in", "c_g_qn", "c_g_kn", "o_w_out"]


def rope_table(dim):
    n = dim // 4
    inv = (np.float32(10000.0) ** (-np.arange(n, dtype=np.float32) / np.float32(n))).astype(np.float32)
    t = np.arange(LAT)
    rows, cols = (t // GRID_W).astype(np.float32), (t % GRID_W).astype(np.float32)
    ang = np.concatenate([rows[:, None] * inv, cols[:, None] * inv], axis=-1)
    ang = np.concatenate([np.zeros((CTX, dim // 2), np.float32), ang], axis=0)
    return np.stack([np.cos(ang), np.sin(ang)], axis=1).astype(np.float32)


def kernel(**inputs):
    import concourse.bacc as bacc
    from concourse.bass_utils import run_bass_kernel_spmd

    nc = bacc.Bacc("TRN2", target_bir_lowering=False, num_devices=1)
    arrays, A = {}, {}
    for name in _INS:
        a = np.ascontiguousarray(inputs[name])
        arrays[f"in_{name}"] = a
    for n, dim in (("A", A_ROPE), ("B", B_D), ("C", C_HD)):
        arrays["in_rope" + n] = rope_table(dim)
    for name, a in arrays.items():
        A[name[3:]] = nc.dram_tensor(name, a.shape, mybir.dt.from_np(a.dtype), kind="ExternalInput").ap()
    out = nc.dram_tensor("out_x", (1, LAT, D), F32, kind="ExternalOutput").ap()
    trunk(nc, A, out[0])
    r = run_bass_kernel_spmd(nc, [arrays], core_ids=[0])
    return r.results[0]["out_x"]
```
